# Optimizing a Trainium2 kernel written in Bass

```python
import jax, jax.numpy as jnp
from jax import lax
import numpy as np
import math
import jax
import jax.numpy as jnp

D_MODEL = 1024
BATCH = 1
SEQ = 256
DEPTH = 2

CHUNK = 64
WINDOW = 128
WIN_CHUNKS = WINDOW // CHUNK
BAND = (WIN_CHUNKS + 1) * CHUNK
HEAD_DIM = 64
ATTN_WIDTH = D_MODEL // 2
N_Q_HEADS = ATTN_WIDTH // HEAD_DIM
N_KV_HEADS = N_Q_HEADS // 4
KV_WIDTH = N_KV_HEADS * HEAD_DIM
LRU_WIDTH = D_MODEL
LRU_BLOCKS = 16
LRU_BLOCK = LRU_WIDTH // LRU_BLOCKS
CONV_WIDTH = 4
LRU_C = 8.0
N_MEM = 256
MEM_HEADS = 4
MEM_WIDTH = D_MODEL // 2
MEM_HEAD_DIM = MEM_WIDTH // MEM_HEADS
N_BRANCH = 3
D_FF = 11 * D_MODEL // 4
EPS = 1e-6
IN_WIDTH = ATTN_WIDTH + 2 * KV_WIDTH + 2 * LRU_WIDTH + MEM_WIDTH + N_BRANCH * D_MODEL


def rmsnorm(x, g):
    x32 = x.astype(jnp.float32)
    y = x32 * lax.rsqrt(jnp.mean(x32 * x32, axis=-1, keepdims=True) + EPS)
    return (y * g.astype(jnp.float32)).astype(x.dtype)

def swiglu(h, w_gate, w_up, w_down):
    return (jax.nn.silu(h @ w_gate) * (h @ w_up)) @ w_down

def alibi_slopes(n):
    return jnp.asarray(np.array([2.0 ** (-8.0 * (i + 1) / n) for i in range(n)], dtype=np.float32))

def window_attention(q, k, v, sinks):
    B, S = q.shape[0], q.shape[1]
    nc = S // CHUNK
    G = N_Q_HEADS // N_KV_HEADS
    pad = WIN_CHUNKS * CHUNK
    kp = jnp.pad(k, ((0, 0), (pad, 0), (0, 0), (0, 0))).reshape(B, nc + WIN_CHUNKS, CHUNK, N_KV_HEADS, HEAD_DIM)
    vp = jnp.pad(v, ((0, 0), (pad, 0), (0, 0), (0, 0))).reshape(B, nc + WIN_CHUNKS, CHUNK, N_KV_HEADS, HEAD_DIM)
    kb = jnp.concatenate([kp[:, j:j + nc] for j in range(WIN_CHUNKS + 1)], axis=2)
    vb = jnp.concatenate([vp[:, j:j + nc] for j in range(WIN_CHUNKS + 1)], axis=2)
    qb = q.reshape(B, nc, CHUNK, N_KV_HEADS, G, HEAD_DIM)
    s = jnp.einsum('bcqkgd,bcskd->bckgqs', qb, kb).astype(jnp.float32) * (HEAD_DIM ** -0.5)
    qi = jnp.arange(CHUNK) + pad
    kj = jnp.arange(BAND)
    dist = jnp.abs(qi[:, None] - kj[None, :]).astype(jnp.float32)
    slopes = alibi_slopes(N_Q_HEADS).reshape(N_KV_HEADS, G)
    s = s - slopes[:, :, None, None] * dist
    key_chunk = jnp.arange(nc)[:, None] - WIN_CHUNKS + kj[None, :] // CHUNK
    valid = key_chunk >= 0
    s = jnp.where(valid[None, :, None, None, None, :], s, -jnp.inf)
    sink = sinks.astype(jnp.float32).reshape(N_KV_HEADS, G)[None, None, :, :, None, None]
    m = jnp.maximum(jnp.max(s, axis=-1, keepdims=True), sink)
    p = jnp.exp(s - m)
    p = p / (jnp.sum(p, axis=-1, keepdims=True) + jnp.exp(sink - m))
    o = jnp.einsum('bckgqs,bcskd->bcqkgd', p.astype(v.dtype), vb)
    return o.reshape(B, S, ATTN_WIDTH)

def rglru_branch(xr, yr, conv_w, conv_b, wa, ba, wx, bx, lam):
    B, S = xr.shape[0], xr.shape[1]
    xc = lax.conv_general_dilated(xr, conv_w[:, None, :].astype(xr.dtype), window_strides=(1,),
                                  padding=[(CONV_WIDTH - 1, 0)],
                                  dimension_numbers=('NWC', 'WIO', 'NWC'),
                                  feature_group_count=LRU_WIDTH) + conv_b
    xb = xc.reshape(B, S, LRU_BLOCKS, LRU_BLOCK)
    r = jax.nn.sigmoid((jnp.einsum('bshi,hij->bshj', xb, wa).reshape(B, S, LRU_WIDTH) + ba).astype(jnp.float32))
    gi = jax.nn.sigmoid((jnp.einsum('bshi,hij->bshj', xb, wx).reshape(B, S, LRU_WIDTH) + bx).astype(jnp.float32))
    log_a = -LRU_C * r * jax.nn.softplus(-lam.astype(jnp.float32))
    a = jnp.exp(log_a)
    mult = jnp.sqrt(jnp.maximum(1.0 - jnp.exp(2.0 * log_a), 0.0))
    mult = jnp.where(jnp.arange(S)[None, :, None] == 0, 1.0, mult)
    b = mult * gi * xc.astype(jnp.float32)

    def combine(left, right):
        al, bl = left
        ar, br = right
        return al * ar, ar * bl + br

    _, h = lax.associative_scan(combine, (a, b), axis=1)
    return h.astype(xr.dtype) * jax.nn.gelu(yr)

def memory_attention(cq, mem_n, w_mem_kv):
    B, S = cq.shape[0], cq.shape[1]
    M = mem_n.shape[1]
    kv = mem_n @ w_mem_kv
    k = kv[..., :MEM_WIDTH].reshape(B, M, MEM_HEADS, MEM_HEAD_DIM)
    v = kv[..., MEM_WIDTH:].reshape(B, M, MEM_HEADS, MEM_HEAD_DIM)
    q = cq.reshape(B, S, MEM_HEADS, MEM_HEAD_DIM)
    s = jnp.einsum('bshd,bmhd->bhsm', q, k).astype(jnp.float32) * (MEM_HEAD_DIM ** -0.5)
    p = jax.nn.softmax(s, axis=-1).astype(v.dtype)
    return jnp.einsum('bhsm,bmhd->bshd', p, v).reshape(B, S, MEM_WIDTH)

def first_inputs(seed: int = 0) -> dict:
    key = jax.random.key(seed)
    ks = jax.random.split(key, 32)
    f32 = jnp.float32

    def nrm(k, shape, fan_in):
        return jax.random.normal(k, shape, f32) * (fan_in ** -0.5)

    def gain(k, shape):
        return 1.0 + 0.05 * jax.random.normal(k, shape, f32)

    u = jax.random.uniform(ks[20], (DEPTH, LRU_WIDTH), f32, 0.9, 0.999)
    a0 = u ** (1.0 / LRU_C)
    lam = jnp.log(a0) - jnp.log1p(-a0)
    return {
        'x': jax.random.normal(ks[0], (BATCH, SEQ, D_MODEL), f32),
        'mem': jax.random.normal(ks[1], (BATCH, N_MEM, D_MODEL), f32),
        'ffn1_norm': gain(ks[2], (DEPTH, D_MODEL)),
        'ffn1_w_gate': nrm(ks[3], (DEPTH, D_MODEL, D_FF), D_MODEL),
        'ffn1_w_up': nrm(ks[4], (DEPTH, D_MODEL, D_FF), D_MODEL),
        'ffn1_w_down': nrm(ks[5], (DEPTH, D_FF, D_MODEL), D_FF),
        'mix_norm': gain(ks[6], (DEPTH, D_MODEL)),
        'w_in': nrm(ks[7], (DEPTH, D_MODEL, IN_WIDTH), D_MODEL),
        'gate_bias': 0.1 * jax.random.normal(ks[8], (DEPTH, N_BRANCH * D_MODEL), f32),
        'attn_sinks': 0.5 * jax.random.normal(ks[9], (DEPTH, N_Q_HEADS), f32),
        'w_attn_out': nrm(ks[10], (DEPTH, ATTN_WIDTH, D_MODEL), ATTN_WIDTH),
        'conv_w': nrm(ks[11], (DEPTH, CONV_WIDTH, LRU_WIDTH), CONV_WIDTH),
        'conv_b': 0.02 * jax.random.normal(ks[12], (DEPTH, LRU_WIDTH), f32),
        'lru_wa': nrm(ks[13], (DEPTH, LRU_BLOCKS, LRU_BLOCK, LRU_BLOCK), LRU_BLOCK),
        'lru_ba': 0.1 * jax.random.normal(ks[14], (DEPTH, LRU_WIDTH), f32),
        'lru_wx': nrm(ks[15], (DEPTH, LRU_BLOCKS, LRU_BLOCK, LRU_BLOCK), LRU_BLOCK),
        'lru_bx': 0.1 * jax.random.normal(ks[16], (DEPTH, LRU_WIDTH), f32),
        'lru_lambda': lam,
        'w_lru_out': nrm(ks[17], (DEPTH, LRU_WIDTH, D_MODEL), LRU_WIDTH),
        'mem_norm': gain(ks[18], (DEPTH, D_MODEL)),
        'w_mem_kv': nrm(ks[19], (DEPTH, D_MODEL, 2 * MEM_WIDTH), D_MODEL),
        'w_mem_out': nrm(ks[21], (DEPTH, MEM_WIDTH, D_MODEL), MEM_WIDTH),
        'w_out': nrm(ks[22], (DEPTH, D_MODEL, D_MODEL), D_MODEL),
        'ffn2_norm': gain(ks[23], (DEPTH, D_MODEL)),
        'ffn2_w_gate': nrm(ks[24], (DEPTH, D_MODEL, D_FF), D_MODEL),
        'ffn2_w_up': nrm(ks[25], (DEPTH, D_MODEL, D_FF), D_MODEL),
        'ffn2_w_down': nrm(ks[26], (DEPTH, D_FF, D_MODEL), D_FF),
        'final_norm': gain(ks[27], (D_MODEL,)),
    }

def first_block(x, mem, ffn1_norm, ffn1_w_gate, ffn1_w_up, ffn1_w_down, mix_norm, w_in, gate_bias,
              attn_sinks, w_attn_out, conv_w, conv_b, lru_wa, lru_ba, lru_wx, lru_bx, lru_lambda,
              w_lru_out, mem_norm, w_mem_kv, w_mem_out, w_out, ffn2_norm, ffn2_w_gate, ffn2_w_up,
              ffn2_w_down, final_norm):
    B, S = x.shape[0], x.shape[1]
    o1 = ATTN_WIDTH
    o2 = o1 + KV_WIDTH
    o3 = o2 + KV_WIDTH
    o4 = o3 + LRU_WIDTH
    o5 = o4 + LRU_WIDTH
    o6 = o5 + MEM_WIDTH
    for l in range(DEPTH):
        x = x + 0.5 * swiglu(rmsnorm(x, ffn1_norm[l]), ffn1_w_gate[l], ffn1_w_up[l], ffn1_w_down[l])
        h = rmsnorm(x, mix_norm[l])
        proj = h @ w_in[l]
        q = proj[..., :o1].reshape(B, S, N_Q_HEADS, HEAD_DIM)
        k = proj[..., o1:o2].reshape(B, S, N_KV_HEADS, HEAD_DIM)
        v = proj[..., o2:o3].reshape(B, S, N_KV_HEADS, HEAD_DIM)
        xr = proj[..., o3:o4]
        yr = proj[..., o4:o5]
        cq = proj[..., o5:o6]
        g = jax.nn.sigmoid((proj[..., o6:] + gate_bias[l]).astype(jnp.float32)).astype(x.dtype)
        g = g.reshape(B, S, N_BRANCH, D_MODEL)
        br_attn = window_attention(q, k, v, attn_sinks[l]) @ w_attn_out[l]
        br_lru = rglru_branch(xr, yr, conv_w[l], conv_b[l], lru_wa[l], lru_ba[l], lru_wx[l], lru_bx[l],
                              lru_lambda[l]) @ w_lru_out[l]
        br_mem = memory_attention(cq, rmsnorm(mem, mem_norm[l]), w_mem_kv[l]) @ w_mem_out[l]
        merged = g[:, :, 0] * br_attn + g[:, :, 1] * br_lru + g[:, :, 2] * br_mem
        x = x + merged @ w_out[l]
        x = x + 0.5 * swiglu(rmsnorm(x, ffn2_norm[l]), ffn2_w_gate[l], ffn2_w_up[l], ffn2_w_down[l])
    return rmsnorm(x, final_norm)


DEPTH_2 = 1

ATT_PATTERNS = ((128, 1), (512, 4), (2048, 16))
N_ATT_GROUPS = 3
HEADS_PER_GROUP = 4
ATT_HEADS = N_ATT_GROUPS * HEADS_PER_GROUP
ATT_WIDTH = ATT_HEADS * HEAD_DIM
ATT_OUT_WIDTH = HEADS_PER_GROUP * HEAD_DIM
REL_BUCKETS = 32
REL_MAX_DIST = 2048
RWKV_HEADS = 8
RWKV_HEAD_DIM = 64
RWKV_WIDTH = RWKV_HEADS * RWKV_HEAD_DIM
DECAY_LORA = 64
ICLR_LORA = 64
GATE_LORA = 160
RWKV_SHIFT_WIDTH = 3 * RWKV_WIDTH + DECAY_LORA + ICLR_LORA + GATE_LORA
GN_EPS = 64e-5
N_BRANCHES = 2
IN_WIDTH_2 = 3 * ATT_WIDTH + RWKV_SHIFT_WIDTH + N_BRANCHES * D_MODEL
N_EXPERT_GROUPS = 4
EXPERTS_PER_GROUP = 8
N_EXPERTS = N_EXPERT_GROUPS * EXPERTS_PER_GROUP
TOP_K = 2
D_EXPERT = 512
ROW_BLOCK = 256
NORM_EPS = 1e-6
NEG_INF = -1e30


def rms_norm(x, gain, eps=NORM_EPS):
    xf = x.astype(jnp.float32)
    y = xf * lax.rsqrt(jnp.mean(xf * xf, axis=-1, keepdims=True) + eps)
    return (y * gain.astype(jnp.float32)).astype(x.dtype)

def t5_causal_bucket(dist):
    max_exact = REL_BUCKETS // 2
    d = jnp.maximum(dist.astype(jnp.float32), 1.0)
    large = max_exact + (jnp.log(d / max_exact) / math.log(REL_MAX_DIST / max_exact)
                         * (REL_BUCKETS - max_exact)).astype(jnp.int32)
    large = jnp.minimum(large, REL_BUCKETS - 1)
    return jnp.where(dist < max_exact, dist, large)

def dilated_window_attention(q, k, v, bias_table, window, dilation):
    B, S, H, E = q.shape
    L = S // dilation
    W = window // dilation
    n_blk = -(-L // W)
    Lp = n_blk * W

    def to_sub(t):
        return t.reshape(B, L, dilation, H, E).transpose(0, 2, 3, 1, 4)

    qb = jnp.pad(to_sub(q), ((0, 0),) * 3 + ((0, Lp - L), (0, 0))).reshape(B, dilation, H, n_blk, W, E)
    kv_pad = ((0, 0),) * 3 + ((W, Lp - L), (0, 0))

    def band(t):
        t = jnp.pad(to_sub(t), kv_pad)
        prev = t[:, :, :, :Lp].reshape(B, dilation, H, n_blk, W, E)
        cur = t[:, :, :, W:].reshape(B, dilation, H, n_blk, W, E)
        return jnp.concatenate([prev, cur], axis=4)

    kb, vb = band(k), band(v)
    qi = jnp.arange(W)[:, None]
    kj = jnp.arange(2 * W)[None, :]
    rel = qi + W - kj
    key_pos = (jnp.arange(n_blk) * W - W)[:, None, None] + kj[None]
    valid = (rel >= 0)[None] & (rel <= W)[None] & (key_pos >= 0)
    bias = bias_table[t5_causal_bucket(jnp.clip(rel, 0, W) * dilation)]
    bias = jnp.transpose(bias, (2, 0, 1)).astype(jnp.float32)[:, None]
    s = jnp.einsum('bdhnqe,bdhnke->bdhnqk', qb, kb).astype(jnp.float32) * (E ** -0.5) + bias
    s = jnp.where(valid, s, NEG_INF)
    lse = jax.nn.logsumexp(s, axis=-1)
    p = jnp.exp(s - lse[..., None])
    o = jnp.einsum('bdhnqk,bdhnke->bdhnqe', p.astype(v.dtype), vb)

    def from_sub(t):
        t = t.reshape((B, dilation, H, Lp) + t.shape[5:])[:, :, :, :L]
        t = jnp.moveaxis(t, 3, 1)
        return t.reshape((B, S, H) + t.shape[4:])

    return from_sub(o), from_sub(lse)

def wkv7_scan(r, decay, k, v, kk, a):
    B, S, H, N = r.shape

    def step(state, inp):
        r_t, w_t, k_t, v_t, kk_t, b_t = inp
        sa = jnp.einsum('bhvk,bhk->bhv', state, -kk_t)
        state = (state * w_t[:, :, None, :] + sa[..., None] * b_t[:, :, None, :]
                 + v_t[..., None] * k_t[:, :, None, :])
        return state, jnp.einsum('bhvk,bhk->bhv', state, r_t)

    xs = tuple(jnp.moveaxis(t, 1, 0) for t in (r, decay, k, v, kk, kk * a))
    _, out = lax.scan(step, jnp.zeros((B, H, N, N), jnp.float32), xs)
    return jnp.moveaxis(out, 0, 1)

def rwkv7_time_mix(p, shift_mu, w0, w_up, a0, a_up, g_up, k_k, k_a, r_k, ln_w, ln_b, w_rwkv_out):
    B, S, _ = p.shape
    H, N, C = RWKV_HEADS, RWKV_HEAD_DIM, RWKV_WIDTH
    pf = p.astype(jnp.float32)
    prev = jnp.pad(pf, ((0, 0), (1, 0), (0, 0)))[:, :-1]
    pm = pf + (prev - pf) * shift_mu
    r, k, v, xw, xa, xg = jnp.split(pm, [C, 2 * C, 3 * C, 3 * C + DECAY_LORA,
                                          3 * C + DECAY_LORA + ICLR_LORA], axis=-1)
    w_log = -jax.nn.softplus(-(w0 + jnp.tanh(xw) @ w_up)) - 0.5
    decay = jnp.exp(-jnp.exp(w_log))
    a = jax.nn.sigmoid(a0 + xa @ a_up)
    g = jax.nn.sigmoid(xg) @ g_up
    hd = lambda t: t.reshape(B, S, H, N)
    kk = hd(k * k_k)
    kk = kk / jnp.maximum(jnp.sqrt(jnp.sum(kk * kk, axis=-1, keepdims=True)), 1e-12)
    k = k * (1.0 + (a - 1.0) * k_a)
    o = wkv7_scan(hd(r), hd(decay), hd(k), hd(v), kk, hd(a))
    mu = jnp.mean(o, axis=-1, keepdims=True)
    var = jnp.mean(jnp.square(o - mu), axis=-1, keepdims=True)
    o = ((o - mu) * lax.rsqrt(var + GN_EPS)).reshape(B, S, C) * ln_w + ln_b
    bonus = jnp.sum(hd(r) * hd(k) * r_k, axis=-1, keepdims=True) * hd(v)
    o = (o + bonus.reshape(B, S, C)) * g
    return o.astype(p.dtype) @ w_rwkv_out

def hierarchical_moe(h, w_group_router, b_group_router, w_expert_router, b_expert_router,
                     w_expert_gate, w_expert_up, w_expert_down):
    B, S, D = h.shape
    T = B * S
    hf = h.reshape(T, D)
    grp_prob = jax.nn.softmax((hf @ w_group_router).astype(jnp.float32) + b_group_router, axis=-1)
    grp_p, grp_idx = lax.top_k(grp_prob, 1)
    exp_logits = ((hf @ w_expert_router).astype(jnp.float32) + b_expert_router).reshape(
        T, N_EXPERT_GROUPS, EXPERTS_PER_GROUP)
    sel_logits = jnp.take_along_axis(exp_logits, grp_idx[:, :, None], axis=1)[:, 0]
    top_p, top_i = lax.top_k(jax.nn.softmax(sel_logits, axis=-1), TOP_K)
    gates = grp_p * top_p / jnp.sum(top_p, axis=-1, keepdims=True)
    expert_id = grp_idx * EXPERTS_PER_GROUP + top_i

    A = T * TOP_K
    eid = expert_id.reshape(A).astype(jnp.int32)
    tok = jnp.arange(A, dtype=jnp.int32) // TOP_K
    gate = gates.reshape(A)
    order = jnp.argsort(eid)
    se = eid[order]
    counts = jnp.bincount(eid, length=N_EXPERTS)
    starts = jnp.cumsum(counts) - counts
    pcounts = (counts + ROW_BLOCK - 1) // ROW_BLOCK * ROW_BLOCK
    pends = jnp.cumsum(pcounts)
    pstarts = pends - pcounts
    dest = pstarts[se] + jnp.arange(A, dtype=jnp.int32) - starts[se]
    n_blocks = -(-A // ROW_BLOCK) + N_EXPERTS
    n_rows = n_blocks * ROW_BLOCK
    row_tok = jnp.full((n_rows,), T, jnp.int32).at[dest].set(tok[order])
    row_gate = jnp.zeros((n_rows,), jnp.float32).at[dest].set(gate[order])
    blk_expert = jnp.minimum(jnp.searchsorted(pends, jnp.arange(n_blocks) * ROW_BLOCK, side='right'),
                             N_EXPERTS - 1)
    h_pad = jnp.concatenate([hf, jnp.zeros((1, D), hf.dtype)], axis=0)
    xin = h_pad[row_tok].reshape(n_blocks, ROW_BLOCK, D)

    def expert_block(args):
        xb, e = args
        hid = jax.nn.silu(xb @ w_expert_gate[e]) * (xb @ w_expert_up[e])
        return hid @ w_expert_down[e]

    yb = lax.map(expert_block, (xin, blk_expert)).reshape(n_rows, D)
    y = jax.ops.segment_sum(yb.astype(jnp.float32) * row_gate[:, None], row_tok, num_segments=T + 1)[:T]
    return y.reshape(B, S, D).astype(h.dtype)

def hybrid_layer(x, norm1_gain, w_in, q_norm_gain, k_norm_gain, rel_bias_table, w_att_out,
                 shift_mu, w0, w_up, a0, a_up, g_up, k_k, k_a, r_k, ln_w, ln_b, w_rwkv_out,
                 w_out, norm2_gain, w_group_router, b_group_router, w_expert_router,
                 b_expert_router, w_expert_gate, w_expert_up, w_expert_down):
    B, S, D = x.shape
    h = rms_norm(x, norm1_gain)
    p = h @ w_in
    q, k, v, p_rwkv, p_gate = jnp.split(
        p, [ATT_WIDTH, 2 * ATT_WIDTH, 3 * ATT_WIDTH, 3 * ATT_WIDTH + RWKV_SHIFT_WIDTH], axis=-1)

    heads = lambda t: t.reshape(B, S, N_ATT_GROUPS, HEADS_PER_GROUP, HEAD_DIM)
    q = rms_norm(heads(q), q_norm_gain[:, None, :])
    k = rms_norm(heads(k), k_norm_gain[:, None, :])
    v = heads(v)
    outs, lses = [], []
    for g, (win, dil) in enumerate(ATT_PATTERNS):
        o_g, l_g = dilated_window_attention(
            q[:, :, g], k[:, :, g], v[:, :, g],
            rel_bias_table[:, g * HEADS_PER_GROUP:(g + 1) * HEADS_PER_GROUP], win, dil)
        outs.append(o_g)
        lses.append(l_g)
    wts = jax.nn.softmax(jnp.stack(lses, axis=0), axis=0)
    att = jnp.einsum('gbsh,gbshe->bshe', wts, jnp.stack(outs, axis=0).astype(jnp.float32))
    y_att = att.reshape(B, S, ATT_OUT_WIDTH).astype(x.dtype) @ w_att_out

    y_rwkv = rwkv7_time_mix(p_rwkv, shift_mu, w0, w_up, a0, a_up, g_up, k_k, k_a, r_k,
                            ln_w, ln_b, w_rwkv_out)

    gates = jax.nn.sigmoid(p_gate.astype(jnp.float32)).astype(x.dtype)
    mixed = gates[..., :D] * y_att + gates[..., D:] * y_rwkv
    x = x + mixed @ w_out

    x = x + hierarchical_moe(rms_norm(x, norm2_gain), w_group_router, b_group_router,
                             w_expert_router, b_expert_router, w_expert_gate, w_expert_up,
                             w_expert_down)
    return x

def second_inputs(seed: int = 0) -> dict:
    key = jax.random.key(seed)
    ks = jax.random.split(key, 28)
    f32 = jnp.float32
    L, D = DEPTH_2, D_MODEL
    nrm = lambda k, shape, scale: scale * jax.random.normal(k, shape, f32)
    return {
        'x': nrm(ks[0], (BATCH, SEQ, D), 1.0),
        'norm1_gain': 1.0 + nrm(ks[1], (L, D), 0.05),
        'w_in': nrm(ks[2], (L, D, IN_WIDTH_2), D ** -0.5),
        'q_norm_gain': 1.0 + nrm(ks[3], (L, N_ATT_GROUPS, HEAD_DIM), 0.05),
        'k_norm_gain': 1.0 + nrm(ks[4], (L, N_ATT_GROUPS, HEAD_DIM), 0.05),
        'rel_bias_table': nrm(ks[5], (REL_BUCKETS, ATT_HEADS), 0.5),
        'w_att_out': nrm(ks[6], (L, ATT_OUT_WIDTH, D), ATT_OUT_WIDTH ** -0.5),
        'rwkv_shift_mu': jax.random.uniform(ks[7], (L, RWKV_SHIFT_WIDTH), f32),
        'rwkv_w0': jax.random.uniform(ks[8], (L, RWKV_WIDTH), f32, -6.0, 1.0),
        'rwkv_w_up': nrm(ks[9], (L, DECAY_LORA, RWKV_WIDTH), 0.5 * DECAY_LORA ** -0.5),
        'rwkv_a0': nrm(ks[10], (L, RWKV_WIDTH), 0.1),
        'rwkv_a_up': nrm(ks[11], (L, ICLR_LORA, RWKV_WIDTH), ICLR_LORA ** -0.5),
        'rwkv_g_up': nrm(ks[12], (L, GATE_LORA, RWKV_WIDTH), GATE_LORA ** -0.5),
        'rwkv_k_k': 0.85 + nrm(ks[13], (L, RWKV_WIDTH), 0.05),
        'rwkv_k_a': 1.0 + nrm(ks[14], (L, RWKV_WIDTH), 0.05),
        'rwkv_r_k': nrm(ks[15], (L, RWKV_HEADS, RWKV_HEAD_DIM), 0.1),
        'rwkv_ln_w': 1.0 + nrm(ks[16], (L, RWKV_WIDTH), 0.05),
        'rwkv_ln_b': nrm(ks[17], (L, RWKV_WIDTH), 0.01),
        'w_rwkv_out': nrm(ks[18], (L, RWKV_WIDTH, D), RWKV_WIDTH ** -0.5),
        'w_out': nrm(ks[19], (L, D, D), D ** -0.5),
        'norm2_gain': 1.0 + nrm(ks[20], (L, D), 0.05),
        'w_group_router': nrm(ks[21], (L, D, N_EXPERT_GROUPS), D ** -0.5),
        'b_group_router': nrm(ks[22], (L, N_EXPERT_GROUPS), 0.01),
        'w_expert_router': nrm(ks[23], (L, D, N_EXPERTS), D ** -0.5),
        'b_expert_router': nrm(ks[24], (L, N_EXPERTS), 0.01),
        'w_expert_gate': nrm(ks[25], (L, N_EXPERTS, D, D_EXPERT), D ** -0.5),
        'w_expert_up': nrm(ks[26], (L, N_EXPERTS, D, D_EXPERT), D ** -0.5),
        'w_expert_down': nrm(ks[27], (L, N_EXPERTS, D_EXPERT, D), D_EXPERT ** -0.5),
    }

def second_block(x, norm1_gain, w_in, q_norm_gain, k_norm_gain, rel_bias_table, w_att_out,
              rwkv_shift_mu, rwkv_w0, rwkv_w_up, rwkv_a0, rwkv_a_up, rwkv_g_up, rwkv_k_k,
              rwkv_k_a, rwkv_r_k, rwkv_ln_w, rwkv_ln_b, w_rwkv_out, w_out, norm2_gain,
              w_group_router, b_group_router, w_expert_router, b_expert_router,
              w_expert_gate, w_expert_up, w_expert_down):
    for l in range(DEPTH_2):
        x = hybrid_layer(x, norm1_gain[l], w_in[l], q_norm_gain[l], k_norm_gain[l], rel_bias_table,
                         w_att_out[l], rwkv_shift_mu[l], rwkv_w0[l], rwkv_w_up[l], rwkv_a0[l],
                         rwkv_a_up[l], rwkv_g_up[l], rwkv_k_k[l], rwkv_k_a[l], rwkv_r_k[l],
                         rwkv_ln_w[l], rwkv_ln_b[l], w_rwkv_out[l], w_out[l], norm2_gain[l],
                         w_group_router[l], b_group_router[l], w_expert_router[l],
                         b_expert_router[l], w_expert_gate[l], w_expert_up[l], w_expert_down[l])
    return x


def setup_inputs(seed=0):
    out = dict(first_inputs(seed))
    for name, value in second_inputs(seed + 1).items():
        if name != "x":
            out[name + "_2"] = value
    return out


def reference(
    x, mem, ffn1_norm, ffn1_w_gate, ffn1_w_up, ffn1_w_down, mix_norm, w_in, gate_bias,
    attn_sinks, w_attn_out, conv_w, conv_b, lru_wa, lru_ba, lru_wx, lru_bx, lru_lambda,
    w_lru_out, mem_norm, w_mem_kv, w_mem_out, w_out, ffn2_norm, ffn2_w_gate, ffn2_w_up,
    ffn2_w_down, final_norm, norm1_gain_2, w_in_2, q_norm_gain_2, k_norm_gain_2,
    rel_bias_table_2, w_att_out_2, rwkv_shift_mu_2, rwkv_w0_2, rwkv_w_up_2, rwkv_a0_2,
    rwkv_a_up_2, rwkv_g_up_2, rwkv_k_k_2, rwkv_k_a_2, rwkv_r_k_2, rwkv_ln_w_2, rwkv_ln_b_2,
    w_rwkv_out_2, w_out_2, norm2_gain_2, w_group_router_2, b_group_router_2, w_expert_router_2,
    b_expert_router_2, w_expert_gate_2, w_expert_up_2, w_expert_down_2,
):
    x = first_block(
        x, mem, ffn1_norm, ffn1_w_gate, ffn1_w_up, ffn1_w_down, mix_norm, w_in, gate_bias,
        attn_sinks, w_attn_out, conv_w, conv_b, lru_wa, lru_ba, lru_wx, lru_bx, lru_lambda,
        w_lru_out, mem_norm, w_mem_kv, w_mem_out, w_out, ffn2_norm, ffn2_w_gate, ffn2_w_up,
        ffn2_w_down, final_norm,
    )
    return second_block(
        x, norm1_gain_2, w_in_2, q_norm_gain_2, k_norm_gain_2, rel_bias_table_2, w_att_out_2,
        rwkv_shift_mu_2, rwkv_w0_2, rwkv_w_up_2, rwkv_a0_2, rwkv_a_up_2, rwkv_g_up_2,
        rwkv_k_k_2, rwkv_k_a_2, rwkv_r_k_2, rwkv_ln_w_2, rwkv_ln_b_2, w_rwkv_out_2, w_out_2,
        norm2_gain_2, w_group_router_2, b_group_router_2, w_expert_router_2, b_expert_router_2,
        w_expert_gate_2, w_expert_up_2, w_expert_down_2,
    )


_drawn_inputs = setup_inputs


def setup_inputs(seed=0):
    import zlib

    import numpy as np

    out = dict(_drawn_inputs(seed))
    spreads = {}
    factors = {'attn_sinks': 3.327,
     'lru_ba': 4.538,
     'lru_bx': 3.173,
     'mem_norm': 2.995,
     'q_norm_gain_2': 8.0,
     'k_norm_gain_2': 8.0,
     'rwkv_w_up_2': 2.938,
     'rwkv_ln_b_2': 4.74,
     'b_group_router_2': 23.426,
     'rwkv_a0_2': 2.764,
     'b_expert_router_2': 3.284}
    for name, (base, spread) in spreads.items():
        noise = np.random.default_rng([zlib.crc32(name.encode()), seed]).standard_normal(out[name].shape)
        drawn = base * np.exp(spread * noise) if base else spread * noise
        out[name] = jnp.asarray(drawn.astype(out[name].dtype))
    for name, factor in factors.items():
        out[name] = (out[name] * factor).astype(out[name].dtype)
    return out
```

```python
from contextlib import ExitStack, contextmanager
from itertools import count

import concourse.bass as bass
from concourse import mybir
import numpy as np

F32 = mybir.dt.float32
ALU = mybir.AluOpType
ACT = mybir.ActivationFunctionType
AX = mybir.AxisListType

P = 128
SEQ = 256
TT = SEQ // P
D = 1024
KT = D // P
DEPTH = 2
EPS = 1e-6
NEG = -1e30

SLOT = 6144
NSLOT = 4
F_STEP = 256
D_FF = 2816
FF_STEPS = D_FF // F_STEP
GATE, UP, DOWN = 0, 2048, 4096

HEAD = 64
NQ = 8
NKV = 2
MEM_HEADS = 4
N_GATES = 3
CONV = 4
CHUNK = 64
PAR = {}
_at = 0
for _name, _n in (("ffn1", 8), ("mix", 8), ("mem", 8), ("ffn2", 8), ("gate_bias", 24), ("conv_w", 32),
                  ("conv_b", 8), ("ba", 8), ("bx", 8), ("lam", 8), ("sinks", 8)):
    PAR[_name] = slice(_at, _at + _n)
    _at += _n
N_PAR = _at

GROUPS = 3
GHEADS = 4
DIL = (1, 4, 16)
N_BUCKETS = 32
RW = 512
RT = RW // P
RHEADS = 8
GN_EPS = 64e-5
N_GRP, N_PER = 4, 8
N_EXP = N_GRP * N_PER
D_EXP = 512
EXP_STEPS = N_EXP * D_EXP // F_STEP
PAR2 = {}
_at = 0
for _name, _n in (("norm1", 8), ("norm2", 8), ("qgain", 6), ("kgain", 6), ("mu", 15), ("w0", 4), ("a0", 4),
                  ("k_k", 4), ("k_a", 4), ("r_k", 4), ("ln_w", 4), ("ln_b", 4)):
    PAR2[_name] = slice(_at, _at + _n)
    _at += _n
N_PAR2 = _at


class Tensors:
    pass


@contextmanager
def phase(nc, *names, keep=()):
    with ExitStack() as stack:
        sems = {n: stack.enter_context(nc.semaphore(n)) for n in names}
        with nc.Block() as block:
            yield block, sems
        for s in list(sems.values()) + list(keep):
            nc.gpsimd.sem_clear(s)
        nc.all_engine_barrier()


def on_chip(nc, c, stack, name, shape):
    return stack.enter_context(nc.sbuf_tensor(f"{name}_{next(c.ids)}", shape, F32))


class Chain:

    def __init__(self, eng, sem):
        self.eng, self.sem, self.counts = eng, sem, {}

    def __call__(self, ins, sem=None):
        sem = sem or self.sem
        n = self.counts[id(sem)] = self.counts.get(id(sem), 0) + 1
        ins.then_inc(sem, 1)
        self.eng.wait_ge(sem, n)


def steps(eng, n, head, body):
    for j in range(head):
        body(j, j % NSLOT, j // NSLOT)
    turns = (n - head) // NSLOT
    with eng.Fori(0, turns) as a:
        for u in range(head, head + NSLOT):
            body(a * NSLOT + u, u % NSLOT, a + u // NSLOT)
    for j in range(head + turns * NSLOT, n):
        body(j, j % NSLOT, j // NSLOT)


def prefetch(sp, c, stream, n=NSLOT):
    width = stream.shape[2]
    for s in range(n):
        sp.dma_start(c.ring[:, s, 0:width], stream[s]).then_inc(c.loaded[s], 16)


def norm_phase(nc, c, src, gain, dst, stream=None, n=NSLOT):
    with ExitStack() as st:
        sq = on_chip(nc, c, st, "norm_squares", [P, D])
        xn = on_chip(nc, c, st, "norm_scaled", [P, TT, D])
        s = on_chip(nc, c, st, "norm_stats", [P, 4, TT])
        block, m = st.enter_context(phase(nc, "squared", "mean_ready", "root_ready", "scaled", "turned", "vstep", "astep"))

        @block.sync
        def _(sp):
            if stream is not None:
                prefetch(sp, c, stream, n)

        @block.scalar
        def _(act):
            for t in range(TT):
                if t:
                    act.wait_ge(m["squared"], t)
                nc.scalar.activation(sq[:], src[:, t, :], ACT.Square, accum_out=s[:, 0, t:t + 1]).then_inc(m["squared"], 1)
            act.wait_ge(m["mean_ready"], 1)
            nc.scalar.activation(s[:, 2, :], s[:, 1, :], ACT.Sqrt).then_inc(m["root_ready"], 1)
            for k in (2, 3, 6, 7):
                act.wait_ge(m["turned"], k // 2 * 2 + 2)
                nc.scalar.activation(dst[:, k, :], c.ps[:, k // 2, (k % 2) * 256:(k % 2) * 256 + 256],
                                     ACT.Identity, scale=gain[:, k:k + 1])

        @block.vector
        def _(dve):
            do = Chain(dve, m["vstep"])
            dve.wait_ge(m["squared"], TT)
            do(nc.vector.tensor_scalar(s[:, 1, :], s[:, 0, :], 1.0 / D, EPS, ALU.mult, ALU.add), m["mean_ready"])
            dve.wait_ge(m["root_ready"], 1)
            inverse_root(nc, do, s[:, 2, :], s[:, 1, :], s[:, 2, :], s[:, 3, :])
            for t in range(TT):
                nc.vector.tensor_scalar(xn[:, t, :], src[:, t, :], s[:, 2, t:t + 1], None, ALU.mult).then_inc(m["scaled"], 1)
            for k in (0, 1, 4, 5):
                dve.wait_ge(m["turned"], k // 2 * 2 + 2)
                nc.vector.tensor_scalar(dst[:, k, :], c.ps[:, k // 2, (k % 2) * 256:(k % 2) * 256 + 256],
                                        gain[:, k:k + 1], None, ALU.mult)

        @block.tensor
        def _(pe):
            pe.wait_ge(m["scaled"], TT)
            for k in range(KT):
                for t in range(TT):
                    at = (k % 2) * 256 + t * P
                    last = nc.tensor.transpose(c.ps[:, k // 2, at:at + P], xn[:, t, k * P:(k + 1) * P], c.ident[:])
                last.then_inc(m["turned"], 1)


def inverse_root(nc, do, out, mean, root, tmp):
    do(nc.vector.reciprocal(out, root))
    do(nc.vector.tensor_tensor(tmp, out, out, ALU.mult))
    do(nc.vector.tensor_tensor(tmp, tmp, mean, ALU.mult))
    do(nc.vector.tensor_scalar(tmp, tmp, -0.5, 1.5, ALU.mult, ALU.add))
    do(nc.vector.tensor_tensor(out, out, tmp, ALU.mult))


def gate_up(nc, pe, c, m, j, s, q):
    pe.wait_ge(c.loaded[s], q * 16 + 16)
    for f in range(2):
        if not isinstance(j, int) or j >= 2:
            pe.wait_ge(m["hid_done"], j * 2 + (f - 3))
        bank = (s % 2) * 2 + f
        for part, at in ((0, GATE), (1, UP)):
            for k in range(KT):
                w = at + k * F_STEP + f * P
                last = nc.tensor.matmul(c.ps[:, bank, part * SEQ:(part + 1) * SEQ], c.ring[:, s, w:w + P],
                                        c.hT[:, k, :], start=(k == 0), stop=(k == KT - 1))
            if part:
                last.then_inc(m["up_ready"], 1)


def silu_gate(nc, act, c, m, gated, j, s):
    for f in range(2):
        act.wait_ge(m["up_ready"], j * 2 + (f + 1))
        nc.scalar.activation(gated[:, s % 2, f, :], c.ps[:, (s % 2) * 2 + f, 0:SEQ], ACT.Silu).then_inc(m["silu_done"], 1)


def hidden(nc, dve, c, m, hid, gated, j, s):
    if not isinstance(j, int) or j >= NSLOT:
        dve.wait_ge(m["down_used"], j - (NSLOT - 1))
    for f in range(2):
        dve.wait_ge(m["silu_done"], j * 2 + (f + 1))
        nc.vector.tensor_tensor(hid[:, s, f, :], gated[:, s % 2, f, :], c.ps[:, (s % 2) * 2 + f, SEQ:2 * SEQ],
                                ALU.mult).then_inc(m["hid_done"], 1)


def ffn_phase(nc, c, stream):
    N, HD = FF_STEPS, 2
    with ExitStack() as st:
        hid = on_chip(nc, c, st, "hidden", [P, NSLOT, 2, SEQ])
        gated = on_chip(nc, c, st, "silu_gate", [P, 2, 2, SEQ])
        block, m = st.enter_context(phase(nc, "up_ready", "silu_done", "hid_done", "down_used", "summed", keep=c.loaded))

        @block.sync
        def _(sp):
            for j in range(NSLOT, N):
                sp.wait_ge(m["down_used"], j - NSLOT + 1)
                sp.dma_start(c.ring[:, j % NSLOT, :], stream[j]).then_inc(c.loaded[j % NSLOT], 16)

        @block.tensor
        def _(pe):
            def down(j, s, first, final):
                pe.wait_ge(m["hid_done"], j * 2 + 2)
                for f in range(2):
                    for t in range(TT):
                        for n in range(2):
                            w = DOWN + f * D + n * 512
                            last = nc.tensor.matmul(c.ps[:, 4 + 2 * t + n, :], hid[:, s, f, t * P:(t + 1) * P],
                                                    c.ring[:, s, w:w + 512], start=(first and f == 0),
                                                    stop=(final and f == 1))
                last.then_inc(m["down_used"], 1)

            def body(j, s, q):
                gate_up(nc, pe, c, m, j, s, q)
                if not isinstance(j, int) or j > 0:
                    down(j - 1, (s - 1) % NSLOT, isinstance(j, int) and j == 1, False)

            steps(pe, N, HD, body)
            down(N - 1, (N - 1) % NSLOT, False, True)

        @block.scalar
        def _(act):
            steps(act, N, HD, lambda j, s, q: silu_gate(nc, act, c, m, gated, j, s))

        @block.vector
        def _(dve):
            steps(dve, N, NSLOT, lambda j, s, q: hidden(nc, dve, c, m, hid, gated, j, s))
            dve.wait_ge(m["down_used"], N)
            for t in range(TT):
                for n in range(2):
                    at = slice(n * 512, (n + 1) * 512)
                    nc.vector.scalar_tensor_tensor(c.x[:, t, at], c.ps[:, 4 + 2 * t + n, :], 0.5, c.x[:, t, at],
                                                   ALU.mult, ALU.add)


MIX_RING = 3
MIX_BANKS = 6
QS, CQS = HEAD ** -0.5, 128 ** -0.5


def mix_projection_phase(nc, c, par, w_in, w_kv, w_mem):
    N = 12
    VT = 16
    NT = 48
    with ExitStack() as st:
        block, m = st.enter_context(phase(nc, "tile_ready", "late_ready", "v_evacuated", "a_evacuated", keep=c.loaded))

        @block.sync
        def _(sp):
            with sp.Fori(0, 3) as a:
                for u in range(MIX_RING):
                    sp.wait_ge(m["tile_ready"], a * 12 + (4 * u + 4))
                    sp.dma_start(c.ring[:, u, 0:4096], w_in[a * MIX_RING + (3 + u)]).then_inc(c.loaded[u], 16)
            for u, src in enumerate((w_kv, w_mem[0], w_mem[1])):
                sp.wait_ge(m["tile_ready"], 36 + 4 * u + 4)
                sp.dma_start(c.ring[:, u, 0:src.shape[1]], src).then_inc(c.loaded[u], 16)

        @block.tensor
        def _(pe):
            def tile(s, u, bank):
                for k in range(KT):
                    w = k * 512 + u * P
                    last = nc.tensor.matmul(c.ps[:, bank, 0:SEQ], c.ring[:, s, w:w + P], c.hT[:, k, :],
                                            start=(k == 0), stop=(k == KT - 1))
                last.then_inc(m["tile_ready"], 1)

            for i in range(6):
                pe.wait_ge(c.loaded[i % 3], i // 3 * 16 + 16)
                for u in range(4):
                    n = i * 4 + u
                    if n >= VT + MIX_BANKS:
                        pe.wait_ge(m["a_evacuated"], n - MIX_BANKS - VT + 1)
                    elif n >= MIX_BANKS:
                        pe.wait_ge(m["v_evacuated"], n - MIX_BANKS + 1)
                    tile(i % 3, u, n % MIX_BANKS)
            with pe.Fori(0, 2) as a:
                for u in range(12):
                    if u % 4 == 0:
                        pe.wait_ge(c.loaded[u // 4], a * 16 + 48)
                    pe.wait_ge(m["a_evacuated"], a * 12 + (24 + u - MIX_BANKS - VT + 1))
                    tile(u // 4, u % 4, u % MIX_BANKS)
            pe.wait_ge(c.loaded[0], 80)
            for h in range(NKV):
                pe.wait_ge(m["a_evacuated"], 27 + h)
                for half in range(2):
                    for k in range(KT):
                        w = k * 256 + h * HEAD
                        last = nc.tensor.matmul(c.ps[half * HEAD:(half + 1) * HEAD, h, 0:SEQ], c.ring[:, 0, w:w + HEAD],
                                                c.hT[:, k, :], start=(k == 0), stop=(k == KT - 1))
                last.then_inc(m["late_ready"], 1)
            pe.wait_ge(m["a_evacuated"], 29)
            for t in range(TT):
                for k in range(KT):
                    w = k * 256 + P
                    last = nc.tensor.matmul(c.ps[:, 2, t * P:(t + 1) * P], c.hT[:, k, t * P:(t + 1) * P],
                                            c.ring[:, 0, w:w + P], start=(k == 0), stop=(k == KT - 1))
            last.then_inc(m["late_ready"], 1)
            pe.wait_ge(c.loaded[1], 80)
            for h in range(MEM_HEADS):
                if h < 3:
                    pe.wait_ge(m["a_evacuated"], 30 + h)
                else:
                    pe.wait_ge(m["v_evacuated"], VT + 1)
                for k in range(KT):
                    w = k * 512 + h * P
                    last = nc.tensor.matmul(c.ps[:, (3 + h) % MIX_BANKS, 0:SEQ], c.ring[:, 1, w:w + P], c.memT[:, k, :],
                                            start=(k == 0), stop=(k == KT - 1))
                last.then_inc(m["late_ready"], 1)
            pe.wait_ge(c.loaded[2], 80)
            for t in range(TT):
                pe.wait_ge(m["v_evacuated"], VT + 2 + t)
                for k in range(KT):
                    last = nc.tensor.matmul(c.ps[:, 1 + t, :], c.memT[:, k, t * P:(t + 1) * P],
                                            c.ring[:, 2, k * 512:(k + 1) * 512], start=(k == 0), stop=(k == KT - 1))
                last.then_inc(m["late_ready"], 1)

        @block.scalar
        def _(act):
            for k in range(KT):
                act.wait_ge(m["tile_ready"], VT + k + 1)
                nc.scalar.activation(c.yg[:, k, :], c.ps[:, (VT + k) % MIX_BANKS, 0:SEQ], ACT.Gelu_apprx_tanh).then_inc(m["a_evacuated"], 1)
            with act.Fori(0, 2) as a:
                for u in range(12):
                    act.wait_ge(m["tile_ready"], a * 12 + (24 + u + 1))
                    g = a * 12 + u
                    nc.scalar.activation(c.gT[:, bass.ds(g, 1), :], c.ps[:, u % MIX_BANKS:u % MIX_BANKS + 1, 0:SEQ], ACT.Sigmoid,
                                         bias=c.gate_bias[:, bass.ds(g, 1)]).then_inc(m["a_evacuated"], 1)

        @block.vector
        def _(dve):
            for n in range(VT):
                dve.wait_ge(m["tile_ready"], n + 1)
                src = c.ps[:, n % MIX_BANKS, 0:SEQ]
                if n < 4:
                    ins = nc.vector.tensor_scalar(c.qT[:, n, :], src, QS, None, ALU.mult)
                elif n < 8:
                    ins = nc.vector.tensor_scalar(c.cqT[:, n - 4, :], src, CQS, None, ALU.mult)
                else:
                    ins = nc.vector.tensor_copy(c.xr[:, n - 8, CONV - 1:], src)
                ins.then_inc(m["v_evacuated"], 1)
            outs = [c.kT[:, 0, :], c.kT[:, 1, :], c.v[:, :, :].rearrange("p t d -> p (t d)")]
            outs += [c.memK[:, h, :] for h in range(MEM_HEADS)] + [c.memV[:, t, :] for t in range(TT)]
            banks = [0, 1, 2, 3, 4, 5, 0, 1, 2]
            for n, (out, bank) in enumerate(zip(outs, banks)):
                dve.wait_ge(m["late_ready"], n + 1)
                nc.vector.tensor_copy(out, c.ps[:, bank, 0:out.shape[1]]).then_inc(m["v_evacuated"], 1)


def lru_phase(nc, c, par, stream):
    with ExitStack() as st:
        def sb(name, shape):
            return on_chip(nc, c, st, name, shape)
        xc, r = c.hT, c.memT
        gi, a2 = (sb(f"lru_{n}", [P, KT, SEQ]) for n in ("in_gate", "room"))
        rate = sb("lru_rate", [P, KT])
        block, m = st.enter_context(phase(nc, "conv_done", "gates_ready", "act_done", "decay_done", "room_done", "root_done", "rate_done", "vstep", "astep"))

        def cols(name):
            return par[:, PAR[name]]

        @block.sync
        def _(sp):
            prefetch(sp, c, stream)

        @block.scalar
        def _(act):
            do = Chain(act, m["astep"])
            do(nc.scalar.activation(rate[:], cols("lam"), ACT.Exp, scale=-1.0))
            do(nc.scalar.activation(rate[:], rate[:], ACT.Ln, bias=1.0), m["act_done"])
            for k in range(KT):
                act.wait_ge(m["gates_ready"], k + 1)
                nc.scalar.activation(r[:, k, :], c.ps[:, k, 0:SEQ], ACT.Sigmoid, bias=cols("ba")[:, k:k + 1]).then_inc(m["astep"], 1)
                nc.scalar.activation(gi[:, k, :], c.ps[:, k, SEQ:2 * SEQ], ACT.Sigmoid, bias=cols("bx")[:, k:k + 1]).then_inc(m["astep"], 1)
            act.wait_ge(m["astep"], 1 + 2 * KT)
            act.wait_ge(m["rate_done"], 1)
            for k in range(KT):
                nc.scalar.activation(r[:, k, :], r[:, k, :], ACT.Exp, scale=rate[:, k:k + 1]).then_inc(m["decay_done"], 1)
            act.wait_ge(m["room_done"], 1)
            nc.scalar.activation(a2[:], a2[:], ACT.Sqrt).then_inc(m["root_done"], 1)

        @block.vector
        def _(dve):
            do = Chain(dve, m["vstep"])
            dve.wait_ge(m["act_done"], 1)
            do(nc.vector.tensor_scalar(rate[:], rate[:], -8.0, None, ALU.mult), m["rate_done"])
            for i in range(CONV):
                for k in range(KT):
                    w = cols("conv_w")[:, k * CONV + i:k * CONV + i + 1]
                    x = c.xr[:, k, i:i + SEQ]
                    if i == 0:
                        ins = nc.vector.tensor_scalar(xc[:, k, :], x, w, cols("conv_b")[:, k:k + 1], ALU.mult, ALU.add)
                    else:
                        dve.wait_ge(m["vstep"], (i - 1) * KT + k + 1)
                        ins = nc.vector.scalar_tensor_tensor(xc[:, k, :], x, w, xc[:, k, :], ALU.mult, ALU.add)
                    ins.then_inc(m["vstep"] if i < CONV - 1 else m["conv_done"], 1)
            do.counts[id(m["vstep"])] = (CONV - 1) * KT
            dve.wait_ge(m["decay_done"], KT)
            do(nc.vector.tensor_tensor(a2[:], r[:], r[:], ALU.mult))
            do(nc.vector.tensor_scalar(a2[:], a2[:], -1.0, 1.0, ALU.mult, ALU.add))
            do(nc.vector.tensor_scalar(a2[:], a2[:], 0.0, None, ALU.max), m["room_done"])
            dve.wait_ge(m["conv_done"], KT)
            do(nc.vector.tensor_tensor(gi[:], gi[:], xc[:], ALU.mult))
            dve.wait_ge(m["root_done"], 1)
            do(nc.vector.memset(a2[:, :, 0:1], 1.0))
            do(nc.vector.tensor_tensor(gi[:], gi[:], a2[:], ALU.mult))
            for k in range(KT):
                nc.vector.tensor_tensor_scan(a2[:, k, :], r[:, k, :], gi[:, k, :], 0.0, ALU.mult, ALU.add).then_inc(m["vstep"], 1)
            dve.wait_ge(m["vstep"], do.counts[id(m["vstep"])] + KT)
            nc.vector.tensor_tensor(c.yg[:], a2[:], c.yg[:], ALU.mult)

        @block.tensor
        def _(pe):
            for k in range(KT):
                pe.wait_ge(m["conv_done"], k + 1)
                nc.tensor.matmul(c.ps[:, k, 0:SEQ], c.wa[:, k, :], xc[:, k, :], start=True, stop=True)
                nc.tensor.matmul(c.ps[:, k, SEQ:2 * SEQ], c.wx[:, k, :], xc[:, k, :], start=True, stop=True).then_inc(m["gates_ready"], 1)


class Unit:

    def __init__(self, scores, heads, length, pitch, outs, dst, from_ps, bias=None, slopes=None, distance=None, sink=None):
        self.scores, self.heads, self.length, self.pitch = scores, heads, length, pitch
        self.outs, self.dst, self.from_ps = outs, dst, from_ps
        self.bias, self.slopes, self.distance, self.sink = bias, slopes, distance, sink


def attention_phase(nc, c, units, name, S, pT):
    with ExitStack() as st:
        stats = on_chip(nc, c, st, f"{name}_stats", [P, 4, 8])
        block, m = st.enter_context(phase(nc, "scores_ready", "shifted", "exp_done", "sink_done", "probs_ready", "turned", "turned_copied", "out_ready", "out_copied", "vstep"))

        @block.tensor
        def _(pe):
            copies = 0
            for n, u in enumerate(units):
                if n:
                    pe.wait_ge(m["turned_copied"], n)
                    pe.wait_ge(m["out_copied"], n)
                for at, lhsT, rhs in u.scores:
                    last = nc.tensor.matmul(c.psflat[:, at:at + rhs.shape[1]], lhsT, rhs, start=True, stop=True)
                last.then_inc(m["scores_ready"], 1)
                pe.wait_ge(m["probs_ready"], n + 1)
                per = u.length // P
                for b in range(u.heads * per):
                    at = b // per * u.pitch + b % per * P
                    last = nc.tensor.transpose(c.psflat[:, 2048 + b * P:2048 + (b + 1) * P], S[:, at:at + P], c.ident[:])
                last.then_inc(m["turned"], 1)
                pe.wait_ge(m["turned_copied"], n + 1)
                for part, at, terms in u.outs:
                    for i, (val, b) in enumerate(terms):
                        last = nc.tensor.matmul(c.psflat[part, at:at + P], val, pT[:, b * P:(b + 1) * P],
                                                start=(i == 0), stop=(i == len(terms) - 1))
                last.then_inc(m["out_ready"], 1)

        @block.scalar
        def _(act):
            for n, u in enumerate(units):
                act.wait_ge(m["shifted"], n + 1)
                Sv = S[:, 0:u.heads * u.pitch].rearrange("p (h l) -> p h l", h=u.heads)[:, :, 0:u.length]
                nc.scalar.activation(Sv, Sv, ACT.Exp).then_inc(m["exp_done"], 1)
                if u.sink is not None:
                    nc.scalar.activation(stats[:, 1, 0:u.heads], stats[:, 1, 0:u.heads], ACT.Exp).then_inc(m["sink_done"], 1)

        @block.vector
        def _(dve):
            do = Chain(dve, m["vstep"])
            sinks = 0
            for n, u in enumerate(units):
                w, H, L = u.heads * u.length, u.heads, u.length
                Sv = S[:, 0:H * u.pitch].rearrange("p (h l) -> p h l", h=H)[:, :, 0:L]
                top, other, total = stats[:, 0, 0:H], stats[:, 1, 0:H], stats[:, 2, 0:H]
                dve.wait_ge(m["scores_ready"], n + 1)
                pv = c.psflat[:, 0:H * u.pitch].rearrange("p (h l) -> p h l", h=H)[:, :, 0:L]
                if u.slopes is not None:
                    for h in range(H):
                        do(nc.vector.scalar_tensor_tensor(Sv[:, h, :], u.distance, u.slopes[h], pv[:, h, :], ALU.mult, ALU.add))
                elif u.bias is not None:
                    do(nc.vector.tensor_tensor(Sv, pv, u.bias, ALU.add))
                else:
                    do(nc.vector.tensor_copy(Sv, pv))
                do(nc.vector.tensor_reduce(top, Sv, AX.X, ALU.max))
                if u.sink is not None:
                    do(nc.vector.tensor_tensor(top, top, u.sink, ALU.max))
                    do(nc.vector.tensor_tensor(other, u.sink, top, ALU.subtract))
                do(nc.vector.tensor_tensor(Sv, Sv, top.unsqueeze(2).to_broadcast([P, H, L]), ALU.subtract), m["shifted"])
                dve.wait_ge(m["exp_done"], n + 1)
                do(nc.vector.tensor_reduce(total, Sv, AX.X, ALU.add))
                if u.sink is not None:
                    sinks += 1
                    dve.wait_ge(m["sink_done"], sinks)
                    do(nc.vector.tensor_tensor(total, total, other, ALU.add))
                do(nc.vector.reciprocal(total, total))
                do(nc.vector.tensor_tensor(Sv, Sv, total.unsqueeze(2).to_broadcast([P, H, L]), ALU.mult), m["probs_ready"])
                dve.wait_ge(m["turned"], n + 1)
                do(nc.vector.tensor_copy(pT[:, 0:w], c.psflat[:, 2048:2048 + w]), m["turned_copied"])
                dve.wait_ge(m["out_ready"], n + 1)
                do(nc.vector.tensor_copy(u.dst, u.from_ps), m["out_copied"])


def window_units(c):
    units = []
    for t in range(TT):
        L = (t + 1) * P
        scores, outs = [], []
        for n, h in enumerate(ORDER):
            kv, half = h // (NQ // NKV), slice(h % 2 * HEAD, h % 2 * HEAD + HEAD)
            scores.append((n * L, c.qT[half, h // 2, t * P:(t + 1) * P], c.kT[half, kv, 0:L]))
            outs.append((half, h // 2 * P, [(c.v[:, j, kv * HEAD:(kv + 1) * HEAD], n * (t + 1) + j) for j in range(t + 1)]))
        distance = c.distance[:, 0:P] if t == 0 else c.distance[:, P:3 * P]
        units.append(Unit(scores=scores, heads=NQ, length=L, pitch=L, slopes=SLOPES, distance=distance, sink=c.par[:, PAR["sinks"]], outs=outs,
                                     dst=c.oT[:, :, t * P:(t + 1) * P],
                                     from_ps=c.psflat[:, 0:512].rearrange("p (a q) -> p a q", a=4)))
    return units


def memory_units(c):
    units = []
    for t in range(TT):
        scores, outs = [], []
        for h in range(MEM_HEADS):
            scores.append((h * SEQ, c.cqT[:, h, t * P:(t + 1) * P], c.memK[:, h, :]))
            outs.append((slice(0, P), h * P, [(c.memV[:, j, h * P:(h + 1) * P], h * TT + j) for j in range(TT)]))
        units.append(Unit(scores=scores, heads=MEM_HEADS, length=SEQ, pitch=SEQ, outs=outs,
                                     dst=c.omT[:, :, t * P:(t + 1) * P],
                                     from_ps=c.psflat[:, 0:512].rearrange("p (a q) -> p a q", a=4)))
    return units


def merge_phase(nc, c, branches, gates, name):
    NB = len(branches)
    WOUT = sum(b.shape[1] for b in branches) * F_STEP
    with ExitStack() as st:
        merged = on_chip(nc, c, st, f"{name}_merged", [P, KT, SEQ])
        term = on_chip(nc, c, st, f"{name}_term", [P, 2, SEQ])
        block, m = st.enter_context(phase(nc, "branches_ready", "merged_done", "out_ready", "vstep", keep=c.loaded))

        @block.tensor
        def _(pe):
            for n in range(KT):
                s, u = n // 2, n % 2
                if u == 0:
                    pe.wait_ge(c.loaded[s], 16)
                if n >= 2:
                    pe.wait_ge(m["merged_done"], n - 1)
                at = 0
                for b, src in enumerate(branches):
                    nk = src.shape[1]
                    for k in range(nk):
                        w = at + k * F_STEP + u * P
                        last = nc.tensor.matmul(c.ps[:, n % 2 * 4 + b, 0:SEQ], c.ring[:, s, w:w + P], src[:, k, :],
                                                start=(k == 0), stop=(k == nk - 1))
                    at += nk * F_STEP
                last.then_inc(m["branches_ready"], 1)
            pe.wait_ge(m["merged_done"], KT)
            for k in range(KT):
                for t in range(TT):
                    for h in range(2):
                        w = WOUT + (k % 2) * D + h * 512
                        last = nc.tensor.matmul(c.ps[:, 4 + 2 * t + h, :], merged[:, k, t * P:(t + 1) * P],
                                                c.ring[:, k // 2, w:w + 512], start=(k == 0), stop=(k == KT - 1))
            last.then_inc(m["out_ready"], 1)

        @block.vector
        def _(dve):
            do = Chain(dve, m["vstep"])
            for n in range(KT):
                dve.wait_ge(m["branches_ready"], n + 1)
                out = merged[:, n, :]
                do(nc.vector.tensor_tensor(out, c.ps[:, n % 2 * 4, 0:SEQ], gates[:, n, :], ALU.mult))
                for b in range(1, NB):
                    do(nc.vector.tensor_tensor(term[:, b % 2, :], c.ps[:, n % 2 * 4 + b, 0:SEQ], gates[:, b * KT + n, :], ALU.mult))
                    do(nc.vector.tensor_tensor(out, out, term[:, b % 2, :], ALU.add), m["merged_done"] if b == NB - 1 else None)
            dve.wait_ge(m["out_ready"], 1)
            for t in range(TT):
                for h in range(2):
                    at = slice(h * 512, (h + 1) * 512)
                    nc.vector.tensor_tensor(c.x[:, t, at], c.ps[:, 4 + 2 * t + h, :], c.x[:, t, at], ALU.add)


LATE = 15
NAT = 384
W2_WIDTHS = [4096] * 3 + [8 * 288] + [4096] * 4 + [8 * NAT] * 6


def scale_rows_phase(nc, c, gain_row):
    with ExitStack() as st:
        sq = on_chip(nc, c, st, "squares", [P, D])
        s = on_chip(nc, c, st, "stats", [P, 4, TT])
        row = on_chip(nc, c, st, "gain_row", [P, D])
        block, m = st.enter_context(phase(nc, "arrived", "squared", "mean_ready", "root_ready", "vstep"))

        @block.sync
        def _(sp):
            sp.dma_start(row[:], gain_row).then_inc(m["arrived"], 16)

        @block.scalar
        def _(act):
            for t in range(TT):
                if t:
                    act.wait_ge(m["squared"], t)
                nc.scalar.activation(sq[:], c.x[:, t, :], ACT.Square, accum_out=s[:, 0, t:t + 1]).then_inc(m["squared"], 1)
            act.wait_ge(m["mean_ready"], 1)
            nc.scalar.activation(s[:, 2, :], s[:, 1, :], ACT.Sqrt).then_inc(m["root_ready"], 1)

        @block.vector
        def _(dve):
            do = Chain(dve, m["vstep"])
            dve.wait_ge(m["squared"], TT)
            do(nc.vector.tensor_scalar(s[:, 1, :], s[:, 0, :], 1.0 / D, EPS, ALU.mult, ALU.add), m["mean_ready"])
            dve.wait_ge(m["root_ready"], 1)
            inverse_root(nc, do, s[:, 2, :], s[:, 1, :], s[:, 2, :], s[:, 3, :])
            dve.wait_ge(m["arrived"], 16)
            for t in range(TT):
                nc.vector.scalar_tensor_tensor(c.x[:, t, :], c.x[:, t, :], s[:, 2, t:t + 1], row[:], ALU.mult, ALU.mult)


def projection2_phase(nc, c, chunks):
    items = [4, 4, 4, 3, 4, 4, 4, 4] + [2] * 6
    VT = LATE
    with ExitStack() as st:
        block, m = st.enter_context(phase(nc, "item_ready", "v_evacuated", "a_evacuated", "padded", keep=c.loaded))

        @block.sync
        def _(sp):
            for i in range(MIX_RING, len(chunks)):
                sp.wait_ge(m["item_ready"], sum(items[:i - MIX_RING + 1]))
                sp.dma_start(c.ring[:, i % MIX_RING, 0:chunks[i].shape[1]], chunks[i]).then_inc(c.loaded[i % MIX_RING], 16)

        @block.tensor
        def _(pe):
            n = 0
            for i in range(8):
                pe.wait_ge(c.loaded[i % MIX_RING], i // MIX_RING * 16 + 16)
                width = W2_WIDTHS[i] // KT
                for u in range(items[i]):
                    if n >= VT + MIX_BANKS:
                        pe.wait_ge(m["a_evacuated"], n - MIX_BANKS - VT + 1)
                    elif n >= MIX_BANKS:
                        pe.wait_ge(m["v_evacuated"], n - MIX_BANKS + 1)
                    rows = min(P, width - u * P)
                    for k in range(KT):
                        w = k * width + u * P
                        last = nc.tensor.matmul(c.ps[0:rows, n % MIX_BANKS, 0:SEQ], c.ring[:, i % MIX_RING, w:w + rows],
                                                c.hT[:, k, :], start=(k == 0), stop=(k == KT - 1))
                    last.then_inc(m["item_ready"], 1)
                    n += 1
            with pe.Fori(0, 2) as a:
                for i in range(8, 11):
                    pe.wait_ge(c.loaded[i % MIX_RING], a * 16 + (i // MIX_RING * 16 + 16))
                    for t in range(TT):
                        e = n + (i - 8) * 2 + t
                        pe.wait_ge(m["a_evacuated"], a * 6 + (e - MIX_BANKS - VT + 1))
                        for k in range(KT):
                            last = nc.tensor.matmul(c.ps[:, e % MIX_BANKS, 0:NAT], c.hT[:, k, t * P:(t + 1) * P],
                                                    c.ring[:, i % MIX_RING, k * NAT:(k + 1) * NAT],
                                                    start=(k == 0), stop=(k == KT - 1))
                        last.then_inc(m["item_ready"], 1)

        @block.vector
        def _(dve):
            nc.vector.memset(c.rw[:], 0.0).then_inc(m["padded"], 1)
            dve.wait_ge(m["padded"], 1)
            for n in range(VT):
                dve.wait_ge(m["item_ready"], n + 1)
                rows = 32 if n == VT - 1 else P
                nc.vector.tensor_copy(c.rw[0:rows, n, 1:], c.ps[0:rows, n % MIX_BANKS, 0:SEQ]).then_inc(m["v_evacuated"], 1)

        @block.scalar
        def _(act):
            for g in range(16):
                n = VT + g
                act.wait_ge(m["item_ready"], n + 1)
                nc.scalar.activation(c.gT2[:, g, :], c.ps[:, n % MIX_BANKS, 0:SEQ], ACT.Sigmoid).then_inc(m["a_evacuated"], 1)
            with act.Fori(0, 2) as a:
                for e in range(6):
                    n = VT + 16 + e
                    act.wait_ge(m["item_ready"], a * 6 + (n + 1))
                    at = a * (3 * NAT) + (e // 2) * NAT
                    nc.scalar.activation(c.qkv[:, e % 2, bass.ds(at, NAT)], c.ps[:, n % MIX_BANKS, 0:NAT], ACT.Copy).then_inc(m["a_evacuated"], 1)


def qk_norm_phase(nc, c, a):
    NH = 24
    QK = 2 * GROUPS * GHEADS * HEAD
    with ExitStack() as st:
        sq = on_chip(nc, c, st, "squares", [P, QK])
        s = on_chip(nc, c, st, "stats", [P, 3, TT * NH])
        table = on_chip(nc, c, st, "bias_table", [N_BUCKETS + 1, 12])
        hot = on_chip(nc, c, st, "bucket_onehot", [N_BUCKETS + 1, GROUPS, 512])
        rows = on_chip(nc, c, st, "bias_rows", [GHEADS, GROUPS, 512])
        block, m = st.enter_context(phase(nc, "table_here", "ones_set", "rows_ready", "rows_copied", "rows_stored", "bias_here", "bias_ready", "bias_copied", "mean_ready", "root_ready",
                                          "scaled", "turned", "vstep"))

        @block.sync
        def _(sp):
            sp.wait_ge(m["ones_set"], 1)
            sp.dma_start(table[0:N_BUCKETS, :], a["bias_table"]).then_inc(m["table_here"], 16)
            sp.dma_start(hot[:], a["onehot"]).then_inc(m["table_here"], 16)
            sp.wait_ge(m["rows_copied"], 1)
            sp.dma_start(c.bias_rows.rearrange("(h g) i -> h g i", g=GROUPS), rows[:]).then_inc(m["rows_stored"], 16)
            sp.wait_ge(m["rows_stored"], 16)
            for t in range(TT):
                src = bass.AP(tensor=c.bias_rows.tensor, offset=c.bias_rows.offset + 255 - t * P - (P - 1),
                              ap=[[1, P], [512, 12], [1, (t + 1) * P]])
                dst = c.bias_reversed[:, t * 1536:t * 1536 + 12 * (t + 1) * P]
                sp.dma_start(dst.rearrange("p (h k) -> p h k", h=12), src).then_inc(m["bias_here"], 16)
            sp.wait_ge(m["bias_here"], 32)

        @block.tensor
        def _(pe):
            pe.wait_ge(m["table_here"], 32)
            for g in range(GROUPS):
                last = nc.tensor.matmul(c.ps[0:GHEADS, g, :], table[:, g * GHEADS:(g + 1) * GHEADS], hot[:, g, :], start=True, stop=True)
            last.then_inc(m["rows_ready"], 1)
            pe.wait_ge(m["rows_copied"], 1)
            pe.wait_ge(m["scaled"], TT)
            for i in range(12):
                for t in range(TT):
                    at = i * SEQ + t * P
                    last = nc.tensor.transpose(c.psflat[:, at:at + P], c.qkv[:, t, i * P:(i + 1) * P], c.ident[:])
            last.then_inc(m["turned"], 1)
            pe.wait_ge(m["bias_here"], 32)
            for i in range(9):
                if i >= 2:
                    pe.wait_ge(m["bias_copied"], i - 1)
                nc.tensor.matmul(c.ps[:, 6 + i % 2, :], c.exchange[:], c.bias_reversed[:, i * 512:(i + 1) * 512],
                                 start=True, stop=True).then_inc(m["bias_ready"], 1)

        @block.scalar
        def _(act):
            act.wait_ge(m["mean_ready"], 1)
            nc.scalar.activation(s[:, 1, :], s[:, 0, :], ACT.Sqrt).then_inc(m["root_ready"], 1)

        @block.vector
        def _(dve):
            do = Chain(dve, m["vstep"])
            do(nc.vector.memset(table[:], 1.0), m["ones_set"])
            for t in range(TT):
                qk = c.qkv[:, t, 0:QK]
                do(nc.vector.tensor_tensor(sq[:], qk, qk, ALU.mult))
                do(nc.vector.tensor_reduce(s[:, 0, t * NH:(t + 1) * NH], sq[:].rearrange("p (h e) -> p h e", e=HEAD), AX.X, ALU.add))
            do(nc.vector.tensor_scalar(s[:, 0, :], s[:, 0, :], 1.0 / HEAD, EPS, ALU.mult, ALU.add), m["mean_ready"])
            dve.wait_ge(m["rows_ready"], 1)
            do(nc.vector.tensor_copy(rows[:], c.ps[0:GHEADS, 0:GROUPS, :]), m["rows_copied"])
            dve.wait_ge(m["root_ready"], 1)
            inverse_root(nc, do, s[:, 1, :], s[:, 0, :], s[:, 1, :], s[:, 2, :])
            for t in range(TT):
                qk = c.qkv[:, t, 0:QK].rearrange("p (h e) -> p h e", e=HEAD)
                by = s[:, 1, t * NH:(t + 1) * NH].unsqueeze(2).to_broadcast([P, NH, HEAD])
                do(nc.vector.tensor_tensor(qk, qk, by, ALU.mult), m["scaled"])
            dve.wait_ge(m["turned"], 1)
            for i in range(12):
                src = c.psflat[:, i * SEQ:(i + 1) * SEQ]
                if i < 6:
                    nc.vector.tensor_scalar(c.qT2[:, i, :], src, c.par2[:, PAR2["qgain"]][:, i:i + 1], HEAD ** -0.5, ALU.mult, ALU.mult)
                else:
                    nc.vector.tensor_scalar(c.kT2[:, i - 6, :], src, c.par2[:, PAR2["kgain"]][:, i - 6:i - 5], None, ALU.mult)
            for i in range(9):
                dve.wait_ge(m["bias_ready"], i + 1)
                nc.vector.tensor_copy(c.bias_all[:, i * 512:(i + 1) * 512], c.ps[:, 6 + i % 2, :]).then_inc(m["bias_copied"], 1)


def dilated_units(c):
    units = []
    for t, heads in ((0, (0, 1, 2, 3)), (1, (0, 1)), (1, (2, 3))):
        K = (t + 1) * P
        L = GROUPS * K
        pitch = 512 if t == 0 else 1024
        scores, outs = [], []
        for n, h in enumerate(heads):
            half = slice(h % 2 * HEAD, h % 2 * HEAD + HEAD)
            terms = []
            for g in range(GROUPS):
                i = g * GHEADS + h
                scores.append((n * pitch + g * K, c.qT2[half, i // 2, t * P:(t + 1) * P], c.kT2[half, i // 2, 0:K]))
                terms += [(c.qkv[:, j, 1536 + i * HEAD:1536 + (i + 1) * HEAD], n * L // P + g * (t + 1) + j) for j in range(t + 1)]
            outs.append((half, n // 2 * P, terms))
        nt = len(heads) // 2
        bias = c.bias0[:, :, :] if t == 0 else c.bias1[:, heads[0]:heads[0] + 2, :]
        units.append(Unit(scores=scores, heads=len(heads), length=L, pitch=pitch, bias=bias, outs=outs,
                                     dst=c.oT2[:, heads[0] // 2:heads[0] // 2 + nt, t * P:(t + 1) * P],
                                     from_ps=c.psflat[:, 0:nt * P].rearrange("p (a q) -> p a q", a=nt)))
    return units


def rwkv_prepare_phase(nc, c, r, a):
    W = RT * SEQ
    with ExitStack() as st:
        block, m = st.enter_context(phase(nc, "weights_here", "mixed", "squashed", "loras_ready", "rates_done", "decay_done", "squares_done", "norms_ready",
                                          "floor_done", "root_done", "bonus_in", "bonus_ready", "natural_ready", "natural_in", "vstep", "astep"))
        p2 = c.par2

        def col(name, i):
            return p2[:, PAR2[name]][:, i:i + 1]

        def flat(t):
            return t.rearrange("p a s -> p (a s)")

        @block.sync
        def _(sp):
            sp.dma_start(r.lora[:], a["lora"]).then_inc(m["weights_here"], 16)
            sp.dma_start(r.gup[:], a["gup"]).then_inc(m["weights_here"], 16)
            sp.wait_ge(m["weights_here"], 32)

        @block.vector
        def _(dve):
            do = Chain(dve, m["vstep"])
            do(nc.vector.tensor_tensor(r.pm[:], c.rw[:, :, 0:SEQ], c.rw[:, :, 1:], ALU.subtract))
            for i in (12, 13, 14) + tuple(range(12)):
                ins = nc.vector.scalar_tensor_tensor(r.pm[:, i, :], r.pm[:, i, :], col("mu", i), c.rw[:, i, 1:], ALU.mult, ALU.add)
                do(ins, m["mixed"] if i >= 12 else None)
            rr, k, v = r.pm[:, 0:4, :], r.pm[:, 4:8, :], r.pm[:, 8:12, :]
            for i in range(RT):
                do(nc.vector.tensor_scalar(r.kk[:, i, :], k[:, i, :], col("k_k", i), None, ALU.mult))
            do(nc.vector.tensor_tensor(r.tmp[:], r.kk[:], r.kk[:], ALU.mult), m["squares_done"])
            dve.wait_ge(m["rates_done"], 1)
            for i in range(RT):
                do(nc.vector.tensor_scalar(r.k2[:, i, :], r.rate[:, i, :], -1.0, col("k_a", i), ALU.add, ALU.mult))
                do(nc.vector.scalar_tensor_tensor(r.k2[:, i, :], r.k2[:, i, :], 1.0, k[:, i, :], ALU.add, ALU.mult))
            do(nc.vector.tensor_copy(r.gate[:], c.psflat[:, 2048:2048 + W].rearrange("p (a s) -> p a s", a=RT)))
            dve.wait_ge(m["norms_ready"], 1)
            do(nc.vector.tensor_scalar(flat(r.tmp[:]), c.psflat[:, 3072:3072 + W], 1e-24, None, ALU.max), m["floor_done"])
            for i in range(RT):
                do(nc.vector.scalar_tensor_tensor(r.bonus[:, i, :], rr[:, i, :], col("r_k", i), r.k2[:, i, :], ALU.mult, ALU.mult),
                   m["bonus_in"] if i == RT - 1 else None)
            dve.wait_ge(m["root_done"], 1)
            do(nc.vector.reciprocal(r.tmp[:], r.tmp[:]))
            do(nc.vector.tensor_tensor(r.kk[:], r.kk[:], r.tmp[:], ALU.mult))
            dve.wait_ge(m["bonus_ready"], 1)
            do(nc.vector.tensor_tensor(flat(r.bonus[:]), c.psflat[:, 0:W], flat(v), ALU.mult))
            dve.wait_ge(m["decay_done"], 1)
            do(nc.vector.memset(r.tmp[:], 0.0))
            cum = r.cum[:].rearrange("p (a n) s -> p a n s", a=RT)
            do(nc.vector.memset(r.cum[:, :, 0:1], 1.0))
            for i in range(RT):
                for n in range(4):
                    do(nc.vector.tensor_tensor_scan(cum[:, i, n, 1:], r.decay[:, i, n * CHUNK:(n + 1) * CHUNK], r.tmp[:, 0, 0:CHUNK],
                                                    1.0, ALU.mult, ALU.add))
            before, upto = r.cum[:, :, 0:CHUNK], r.cum[:, :, 1:CHUNK + 1]

            def chunks(t):
                return t.rearrange("p a (n s) -> p (a n) s", s=CHUNK)

            do(nc.vector.tensor_copy(chunks(r.decay[:]), upto))
            do(nc.vector.reciprocal(r.tmp[:], r.decay[:]))
            do(nc.vector.scalar_tensor_tensor(chunks(r.aT[:]), chunks(r.kk[:]), -1.0, before, ALU.mult, ALU.mult))
            do(nc.vector.tensor_tensor(r.rT[:], rr, r.decay[:], ALU.mult))
            do(nc.vector.tensor_tensor(r.kk[:], r.kk[:], r.rate[:], ALU.mult))
            do(nc.vector.tensor_tensor(r.bT[:], r.kk[:], r.tmp[:], ALU.mult))
            do(nc.vector.tensor_tensor(r.kT[:], r.k2[:], r.tmp[:], ALU.mult), m["natural_in"])
            dve.wait_ge(m["natural_ready"], 1)
            for t in range(TT):
                at = c.psflat[:, t * 2048:(t + 1) * 2048].rearrange("p (x h e) -> p x h e", x=4, h=RHEADS)
                do(nc.vector.tensor_copy(r.Z[:, t, :, HEAD:], at[:, 0]))
                do(nc.vector.tensor_copy(r.nat[:, t, :, :], c.psflat[:, t * 2048 + 512:(t + 1) * 2048].rearrange("p (x e) -> p x e", x=3)))

        @block.scalar
        def _(act):
            act.wait_ge(m["mixed"], 3)
            do = Chain(act, m["astep"])
            do(nc.scalar.activation(r.pm[0:HEAD, 12, :], r.pm[0:HEAD, 12, :], ACT.Tanh))
            do(nc.scalar.activation(r.pm[:, 13:15, :], r.pm[:, 13:15, :], ACT.Sigmoid), m["squashed"])
            act.wait_ge(m["loras_ready"], 1)
            for i in range(RT):
                do(nc.scalar.activation(r.decay[:, i, :], c.psflat[:, i * SEQ:(i + 1) * SEQ], ACT.Sigmoid, bias=col("w0", i)))
            for i in range(RT):
                do(nc.scalar.activation(r.rate[:, i, :], c.psflat[:, 1024 + i * SEQ:1024 + (i + 1) * SEQ], ACT.Sigmoid, bias=col("a0", i)),
                   m["rates_done"] if i == RT - 1 else None)
            do(nc.scalar.activation(r.decay[:], r.decay[:], ACT.Exp, scale=-float(np.exp(-0.5))), m["decay_done"])
            act.wait_ge(m["floor_done"], 1)
            do(nc.scalar.activation(r.tmp[:], r.tmp[:], ACT.Sqrt), m["root_done"])

        @block.tensor
        def _(pe):
            pe.wait_ge(m["weights_here"], 32)
            pe.wait_ge(m["squashed"], 1)
            for i in range(RT):
                w = slice(i * P, (i + 1) * P)
                nc.tensor.matmul(c.psflat[:, i * SEQ:(i + 1) * SEQ], r.lora[0:HEAD, w], r.pm[0:HEAD, 12, :], start=True, stop=True)
                nc.tensor.matmul(c.psflat[:, 1024 + i * SEQ:1024 + (i + 1) * SEQ], r.lora[HEAD:P, w], r.pm[HEAD:P, 12, :], start=True, stop=True)
            for i in range(RT):
                for x in range(2):
                    last = nc.tensor.matmul(c.psflat[:, 2048 + i * SEQ:2048 + (i + 1) * SEQ], r.gup[:, x, i * P:(i + 1) * P], r.pm[:, 13 + x, :],
                                            start=(x == 0), stop=(x == 1))
            last.then_inc(m["loras_ready"], 1)
            pe.wait_ge(m["squares_done"], 1)
            for i in range(RT):
                last = nc.tensor.matmul(c.psflat[:, 3072 + i * SEQ:3072 + (i + 1) * SEQ], c.head_ones[:], r.tmp[:, i, :], start=True, stop=True)
            last.then_inc(m["norms_ready"], 1)
            pe.wait_ge(m["bonus_in"], 1)
            pe.wait_ge(m["decay_done"], 1)
            for i in range(RT):
                last = nc.tensor.matmul(c.psflat[:, i * SEQ:(i + 1) * SEQ], c.head_ones[:], r.bonus[:, i, :], start=True, stop=True)
            last.then_inc(m["bonus_ready"], 1)
            pe.wait_ge(m["natural_in"], 1)
            for t in range(TT):
                for x, src in enumerate((r.aT, r.bT, r.kT, r.pm[:, 8:12, :])):
                    for i in range(RT):
                        at = t * 2048 + x * 512 + i * P
                        last = nc.tensor.transpose(c.psflat[:, at:at + P], src[:, i, t * P:(t + 1) * P], c.ident[:])
            last.then_inc(m["natural_ready"], 1)


STRICT16, OFF_LOWER, LOWER16, STRICT64, UPTO64, = range(5)
WKV_GROUPS = [(t, half) for t in range(TT) for half in range(2)]


def wkv_phase(nc, c, r):
    J = 4

    def head(j, half):
        return 2 * j + half

    def chan(x):
        return lambda t, half, j: x[half * HEAD:(half + 1) * HEAD, j, t * P:(t + 1) * P]

    def mat(x):
        return lambda t, half, j: x[:, t * 2 + half, j, :]

    aT, bT, kT, rT = (chan(x) for x in (r.aT, r.bT, r.kT, r.rT))
    M = {n: mat(r.mats[n]) for n in r.mats}
    vn = lambda t, half, j: r.nat[:, t, 2, head(j, half) * HEAD:(head(j, half) + 1) * HEAD]
    z = lambda t, half, j: r.Z[:, t, head(j, half), :]
    MASK, COPY, ADD = "mask", "copy", "add"
    plan = [
        (bT, aT, [("p1t", MASK, STRICT16)]),
        (aT, bT, [("p1", MASK, LOWER16), ("lo", MASK, OFF_LOWER)]),
        (kT, aT, [("mt", MASK, STRICT64)]),
        (bT, rT, [("qb", MASK, UPTO64)]),
        (kT, rT, [("qk", MASK, UPTO64)]),
        (M["p1t"], M["p1"], [("p2", COPY, None)]),
        (M["p1"], M["p1t"], [("p2t", COPY, None)]),
        (M["p2"], M["d"], [("d", ADD, None)]),
        (M["p2t"], M["p2"], [("p1", COPY, None)]),
        (M["p2"], M["p2t"], [("p1t", COPY, None)]),
        (M["p1"], M["d"], [("d", ADD, None)]),
        (M["p1t"], M["p1"], [("p2", COPY, None)]),
        (M["p2"], M["d"], [("d", ADD, None)]),
        (M["d"], M["lo"], [("p1", COPY, None)]),
        (M["lo"], M["d"], [("p1t", COPY, None)]),
        (M["p1"], M["p1t"], [("p2t", COPY, None)]),
        (M["mt"], vn, [("Z", "left", None)]),
        (M["d"], z, [("Z", "z", None)]),
        (M["p2t"], z, [("Z", "zadd", None)]),
        (M["p1t"], z, [("Z", "zadd", None)]),
    ]
    with ExitStack() as st:
        block, m = st.enter_context(phase(nc, "product_ready", "product_used", "rest_ready", "rest_used", "state_ready", "state_used", "vstep"))

        def bank(n, g):
            return n % 2 * 4 + g

        @block.tensor
        def _(pe):
            for n, (left, right, _) in enumerate(plan):
                for g, (t, half) in enumerate(WKV_GROUPS):
                    if n:
                        pe.wait_ge(m["product_used"], (n - 1) * 4 + g + 1)
                    for j in range(J):
                        rhs = right(t, half, j)
                        last = nc.tensor.matmul(c.ps[:, bank(n, g), j * P:j * P + rhs.shape[1]], left(t, half, j), rhs, start=True, stop=True)
                    last.then_inc(m["product_ready"], 1)
            pe.wait_ge(m["product_used"], len(plan) * 4)
            for g, (t, half) in enumerate(WKV_GROUPS):
                part = slice(half * HEAD, (half + 1) * HEAD)
                for j in range(J):
                    h = head(j, half)
                    last = nc.tensor.matmul(c.ps[part, g, j * P:(j + 1) * P], r.Z[:, t, h, HEAD:], M["qb"](t, half, j), start=True, stop=True)
                last.then_inc(m["rest_ready"], 1)
            for g, (t, half) in enumerate(WKV_GROUPS):
                part = slice(half * HEAD, (half + 1) * HEAD)
                for j in range(J):
                    h = head(j, half)
                    nc.tensor.matmul(c.ps[part, 4 + g, j * P:(j + 1) * P], r.Z[:, t, h, 0:HEAD], M["qb"](t, half, j), start=True, stop=False)
                    last = nc.tensor.matmul(c.ps[part, 4 + g, j * P:(j + 1) * P], vn(t, half, j), M["qk"](t, half, j), start=False, stop=True)
                last.then_inc(m["rest_ready"], 1)
            for n in range(4):
                t, rows = n // 2, slice(n % 2 * HEAD, n % 2 * HEAD + HEAD)
                pe.wait_ge(m["rest_used"], n + 5)
                for half in range(2):
                    part = slice(half * HEAD, (half + 1) * HEAD)
                    for j in range(J):
                        h = head(j, half)
                        hs = slice(h * HEAD, (h + 1) * HEAD)
                        Bn, Kn, Vn = (r.nat[rows, t, x, hs] for x in range(3))
                        nc.tensor.matmul(c.ps[part, n, j * HEAD:(j + 1) * HEAD], r.Z[rows, t, h, HEAD:], Bn, start=True, stop=True)
                        nc.tensor.matmul(c.ps[part, n, 256 + j * HEAD:256 + (j + 1) * HEAD], Bn, r.Z[rows, t, h, 0:HEAD], start=True, stop=False)
                        last = nc.tensor.matmul(c.ps[part, n, 256 + j * HEAD:256 + (j + 1) * HEAD], Kn, Vn, start=False, stop=True)
                last.then_inc(m["rest_ready"], 1)
            pe.wait_ge(m["rest_used"], 12)
            for n in range(1, 4):
                pe.wait_ge(m["state_used"], n)
                for half in range(2):
                    part = slice(half * HEAD, (half + 1) * HEAD)
                    for j in range(J):
                        at = slice(j * HEAD, (j + 1) * HEAD)
                        last = nc.tensor.matmul(c.ps[part, half, at], r.state[part, j, :], r.rT[part, j, n * CHUNK:(n + 1) * CHUNK], start=True, stop=True)
                        if n < 3:
                            last = nc.tensor.matmul(c.ps[part, 2 + half, at], r.step[part, n, j, :], r.state[part, j, :], start=True, stop=True)
                last.then_inc(m["state_ready"], 1)

        @block.vector
        def _(dve):
            do = Chain(dve, m["vstep"])
            for n, (_, _, results) in enumerate(plan):
                for g, (t, half) in enumerate(WKV_GROUPS):
                    dve.wait_ge(m["product_ready"], n * 4 + g + 1)
                    ps = c.ps[:, bank(n, g), :].rearrange("p (j s) -> p j s", j=J)
                    for i, (name, how, arg) in enumerate(results):
                        done = m["product_used"] if i == len(results) - 1 else None
                        Zg = r.Z[:, t, :, :].rearrange("p (j x) e -> p x j e", x=2)[:, half]
                        if how in ("left", "z", "zadd"):
                            if how == "left":
                                do(nc.vector.tensor_copy(Zg[:, :, 0:HEAD], ps[:, :, 0:HEAD]), done)
                            elif how == "z":
                                do(nc.vector.tensor_copy(Zg, ps), done)
                            else:
                                do(nc.vector.tensor_tensor(Zg, ps, Zg, ALU.add), done)
                            continue
                        out = r.mats[name][:, g, :, :]
                        if how == MASK:
                            do(nc.vector.tensor_tensor(out, ps, c.masks[:, arg, :].unsqueeze(1).to_broadcast([P, J, P]), ALU.mult),
                               done if name != "p1t" else None)
                            if name == "p1t":
                                do(nc.vector.tensor_tensor(r.mats["d"][:, g, :, :], out, c.ident[:].unsqueeze(1).to_broadcast([P, J, P]), ALU.add), done)
                        elif how == COPY:
                            do(nc.vector.tensor_copy(out, ps), done)
                        else:
                            do(nc.vector.tensor_tensor(out, ps, out, ALU.add), done)
            for g, (t, half) in enumerate(WKV_GROUPS):
                part = slice(half * HEAD, (half + 1) * HEAD)
                dve.wait_ge(m["rest_ready"], g + 1)
                ps = c.ps[part, g, :].rearrange("p (j s) -> p j s", j=J)
                G = r.rT[part, :, t * P:(t + 1) * P]
                do(nc.vector.tensor_tensor(G, ps, G, ALU.add), m["rest_used"])
            for g, (t, half) in enumerate(WKV_GROUPS):
                part = slice(half * HEAD, (half + 1) * HEAD)
                dve.wait_ge(m["rest_ready"], 4 + g + 1)
                ps = c.ps[part, 4 + g, :].rearrange("p (j s) -> p j s", j=J)
                do(nc.vector.tensor_copy(r.out[part, :, t * P:(t + 1) * P], ps), m["rest_used"])
            for n in range(4):
                dve.wait_ge(m["rest_ready"], 8 + n + 1)
                ps = c.ps[:, n, 0:256].rearrange("p (j s) -> p j s", j=J)
                do(nc.vector.tensor_tensor(r.step[:, n, :, :], ps, c.ident2[:].unsqueeze(1).to_broadcast([P, J, HEAD]), ALU.add))
                ps = c.ps[:, n, 256:512].rearrange("p (j s) -> p j s", j=J)
                end = r.decay[:, :, (n + 1) * CHUNK - 1:(n + 1) * CHUNK].to_broadcast([P, J, HEAD])
                do(nc.vector.tensor_tensor(r.fresh[:, n, :, :], ps, end, ALU.mult), m["rest_used"])
            do(nc.vector.tensor_copy(r.state[:], r.fresh[:, 0, :, :]), m["state_used"])
            for n in range(1, 4):
                dve.wait_ge(m["state_ready"], n)
                for half in range(2):
                    part = slice(half * HEAD, (half + 1) * HEAD)
                    ps = c.ps[part, half, 0:256].rearrange("p (j s) -> p j s", j=J)
                    O = r.out[part, :, n * CHUNK:(n + 1) * CHUNK]
                    do(nc.vector.tensor_tensor(O, ps, O, ALU.add))
                    if n < 3:
                        ps = c.ps[part, 2 + half, 0:256].rearrange("p (j s) -> p j s", j=J)
                        end = r.decay[part, :, (n + 1) * CHUNK - 1:(n + 1) * CHUNK].to_broadcast([HEAD, J, HEAD])
                        do(nc.vector.tensor_tensor(r.state[part, :, :], ps, end, ALU.mult))
                        do(nc.vector.tensor_tensor(r.state[part, :, :], r.state[part, :, :], r.fresh[part, n, :, :], ALU.add),
                           m["state_used"] if half else None)


def rwkv_output_phase(nc, c, r, stream):
    W = RT * SEQ
    with ExitStack() as st:
        block, m = st.enter_context(phase(nc, "sums_ready", "squares_done", "var_ready", "mean_ready", "root_ready", "vstep"))

        def flat(t):
            return t.rearrange("p a s -> p (a s)")

        @block.sync
        def _(sp):
            prefetch(sp, c, stream)

        @block.tensor
        def _(pe):
            for src, at, before, ready in ((r.out, 0, None, m["sums_ready"]), (r.centred, 1024, m["squares_done"], m["var_ready"])):
                if before is not None:
                    pe.wait_ge(before, 1)
                for i in range(RT):
                    last = nc.tensor.matmul(c.psflat[:, at + i * SEQ:at + (i + 1) * SEQ], c.head_ones[:], src[:, i, :], start=True, stop=True)
                last.then_inc(ready, 1)

        @block.scalar
        def _(act):
            act.wait_ge(m["mean_ready"], 1)
            nc.scalar.activation(r.root[:], r.centred[:], ACT.Sqrt).then_inc(m["root_ready"], 1)

        @block.vector
        def _(dve):
            do = Chain(dve, m["vstep"])
            dve.wait_ge(m["sums_ready"], 1)
            do(nc.vector.scalar_tensor_tensor(flat(r.out[:]), c.psflat[:, 0:W], -1.0 / HEAD, flat(r.out[:]), ALU.mult, ALU.add))
            do(nc.vector.tensor_tensor(r.centred[:], r.out[:], r.out[:], ALU.mult), m["squares_done"])
            dve.wait_ge(m["var_ready"], 1)
            do(nc.vector.tensor_scalar(flat(r.centred[:]), c.psflat[:, 1024:1024 + W], 1.0 / HEAD, GN_EPS, ALU.mult, ALU.add), m["mean_ready"])
            dve.wait_ge(m["root_ready"], 1)
            inverse_root(nc, do, r.root[:], r.centred[:], r.root[:], r.scratch[:])
            do(nc.vector.tensor_tensor(r.out[:], r.out[:], r.root[:], ALU.mult))
            for i in range(RT):
                lw, lb = (c.par2[:, PAR2[x]][:, i:i + 1] for x in ("ln_w", "ln_b"))
                do(nc.vector.tensor_scalar(r.out[:, i, :], r.out[:, i, :], lw, lb, ALU.mult, ALU.add))
            do(nc.vector.tensor_tensor(r.out[:], r.out[:], r.bonus[:], ALU.add))
            do(nc.vector.tensor_tensor(r.out[:], r.out[:], r.gate[:], ALU.mult))


def routing_phase(nc, c, a):
    BIG = 64.0
    with ExitStack() as st:
        w = on_chip(nc, c, st, "router", [P, KT, N_GRP + N_EXP])
        bias = on_chip(nc, c, st, "router_bias", [P, N_GRP + N_EXP])
        order = on_chip(nc, c, st, "ordinals", [P, N_PER])
        lg = on_chip(nc, c, st, "logits", [P, TT, N_GRP + N_EXP])
        g4 = on_chip(nc, c, st, "group_work", [P, 3, TT, N_GRP])
        e8 = on_chip(nc, c, st, "expert_work", [P, 6, TT, N_PER])
        wide = on_chip(nc, c, st, "wide_work", [P, TT, N_GRP, N_PER])
        one = on_chip(nc, c, st, "token_work", [P, 8, TT])
        block, m = st.enter_context(phase(nc, "arrived", "logits_ready", "shifted", "exp_done", "vstep"))

        @block.sync
        def _(sp):
            sp.dma_start(w[:], a["router"]).then_inc(m["arrived"], 16)
            sp.dma_start(bias[:], a["router_bias"]).then_inc(m["arrived"], 16)
            sp.dma_start(order[:], a["ordinals"]).then_inc(m["arrived"], 16)

        @block.tensor
        def _(pe):
            pe.wait_ge(m["arrived"], 48)
            for t in range(TT):
                for k in range(KT):
                    last = nc.tensor.matmul(c.ps[:, t, 0:N_GRP + N_EXP], c.hT[:, k, t * P:(t + 1) * P], w[:, k, :], start=(k == 0), stop=(k == KT - 1))
            last.then_inc(m["logits_ready"], 1)

        @block.scalar
        def _(act):
            act.wait_ge(m["shifted"], 1)
            nc.scalar.activation(g4[:, 1], g4[:, 1], ACT.Exp).then_inc(m["exp_done"], 1)
            act.wait_ge(m["shifted"], 2)
            nc.scalar.activation(e8[:, 1], e8[:, 1], ACT.Exp).then_inc(m["exp_done"], 1)

        @block.vector
        def _(dve):
            do = Chain(dve, m["vstep"])
            tt, V = nc.vector.tensor_tensor, nc.vector

            def spread(x, n):
                return x.unsqueeze(2).to_broadcast([P, TT, n])

            def first_top(out, x, top, n, work, least):
                do(V.tensor_reduce(top, x, AX.X, ALU.max))
                do(tt(work, x, spread(top, n), ALU.is_equal))
                do(V.scalar_tensor_tensor(work, work, -BIG, order[:, 0:n].unsqueeze(1).to_broadcast([P, TT, n]), ALU.mult, ALU.add))
                do(V.tensor_reduce(least, work, AX.X, ALU.min))
                do(tt(out, work, spread(least, n), ALU.is_equal))

            dve.wait_ge(m["logits_ready"], 1)
            do(tt(lg[:], c.ps[:, 0:TT, 0:N_GRP + N_EXP], bias[:].unsqueeze(1).to_broadcast([P, TT, N_GRP + N_EXP]), ALU.add))
            grp = lg[:, :, 0:N_GRP]
            first_top(g4[:, 0], grp, one[:, 0], N_GRP, g4[:, 2], one[:, 1])
            do(tt(g4[:, 1], grp, spread(one[:, 0], N_GRP), ALU.subtract), m["shifted"])
            ex = lg[:, :, N_GRP:].rearrange("p t (g e) -> p t g e", g=N_GRP)
            do(tt(wide[:], ex, g4[:, 0].unsqueeze(3).to_broadcast([P, TT, N_GRP, N_PER]), ALU.mult))
            do(V.tensor_reduce(e8[:, 0], wide[:].rearrange("p t g e -> p t e g"), AX.X, ALU.add))
            do(V.tensor_reduce(one[:, 2], e8[:, 0], AX.X, ALU.max))
            do(tt(e8[:, 1], e8[:, 0], spread(one[:, 2], N_PER), ALU.subtract), m["shifted"])
            dve.wait_ge(m["exp_done"], 1)
            do(V.tensor_reduce(one[:, 3], g4[:, 1], AX.X, ALU.add))
            do(V.reciprocal(one[:, 3], one[:, 3]))
            dve.wait_ge(m["exp_done"], 2)
            do(V.tensor_reduce(one[:, 4], e8[:, 1], AX.X, ALU.add))
            do(V.reciprocal(one[:, 4], one[:, 4]))
            do(tt(e8[:, 1], e8[:, 1], spread(one[:, 4], N_PER), ALU.mult))
            first_top(e8[:, 2], e8[:, 1], one[:, 5], N_PER, e8[:, 5], one[:, 1])
            do(V.scalar_tensor_tensor(e8[:, 4], e8[:, 2], -BIG, e8[:, 1], ALU.mult, ALU.add))
            first_top(e8[:, 3], e8[:, 4], one[:, 6], N_PER, e8[:, 5], one[:, 1])
            do(tt(one[:, 7], one[:, 5], one[:, 6], ALU.add))
            do(V.reciprocal(one[:, 7], one[:, 7]))
            do(tt(one[:, 7], one[:, 7], one[:, 3], ALU.mult))
            do(tt(e8[:, 2], e8[:, 2], e8[:, 3], ALU.add))
            do(tt(e8[:, 2], e8[:, 2], e8[:, 1], ALU.mult))
            do(tt(e8[:, 2], e8[:, 2], spread(one[:, 7], N_PER), ALU.mult))
            for t in range(TT):
                do(tt(c.gates[:, t, :].rearrange("p (g e) -> p g e", g=N_GRP), g4[:, 0, t].unsqueeze(2).to_broadcast([P, N_GRP, N_PER]),
                      e8[:, 2, t].unsqueeze(1).to_broadcast([P, N_GRP, N_PER]), ALU.mult))


def experts_phase(nc, c, stream):
    N = EXP_STEPS
    with ExitStack() as st:
        hid = on_chip(nc, c, st, "hidden", [P, NSLOT, 2, SEQ])
        gated = on_chip(nc, c, st, "silu_gate", [P, 2, 2, SEQ])
        block, m = st.enter_context(phase(nc, "up_ready", "silu_done", "hid_done", "down_used", "summed", keep=c.loaded))

        @block.sync
        def _(sp):
            def body(j, s, q):
                if not isinstance(j, int) or j >= NSLOT:
                    sp.wait_ge(m["down_used"], j - (NSLOT - 1))
                    sp.dma_start(c.ring[:, s, :], stream[j]).then_inc(c.loaded[s], 16)

            steps(sp, N, NSLOT, body)

        @block.tensor
        def _(pe):
            def down(j, s, q):
                pe.wait_ge(m["hid_done"], j * 2 + 2)
                expert = q * 2 + s // 2
                if s % 2 == 0 and not (isinstance(expert, int) and expert == 0):
                    pe.wait_ge(m["summed"], expert)
                for f in range(2):
                    for t in range(TT):
                        for n in range(2):
                            w = DOWN + f * D + n * 512
                            last = nc.tensor.matmul(c.ps[:, 4 + 2 * t + n, :], hid[:, s, f, t * P:(t + 1) * P],
                                                    c.ring[:, s, w:w + 512], start=(s % 2 == 0 and f == 0), stop=(s % 2 == 1 and f == 1))
                last.then_inc(m["down_used"], 1)

            def body(j, s, q):
                gate_up(nc, pe, c, m, j, s, q)
                if not isinstance(j, int) or j > 0:
                    down(j - 1, (s - 1) % NSLOT, q if s else q - 1)

            steps(pe, N, 2, body)
            down(N - 1, (N - 1) % NSLOT, (N - 1) // NSLOT)

        @block.scalar
        def _(act):
            steps(act, N, 2, lambda j, s, q: silu_gate(nc, act, c, m, gated, j, s))

        @block.vector
        def _(dve):
            def add(j, s, q):
                dve.wait_ge(m["down_used"], j + 1)
                expert = q * 2 + s // 2
                for t in range(TT):
                    for n in range(2):
                        at = slice(n * 512, (n + 1) * 512)
                        g = c.gates[:, t, bass.ds(expert, 1)]
                        last = nc.vector.scalar_tensor_tensor(c.x[:, t, at], c.ps[:, 4 + 2 * t + n, :], g, c.x[:, t, at], ALU.mult, ALU.add)
                last.then_inc(m["summed"], 1)

            def body(j, s, q):
                hidden(nc, dve, c, m, hid, gated, j, s)
                if s % 2 == 0 and not (isinstance(j, int) and j == 0):
                    if not isinstance(j, int) or j >= 4:
                        dve.wait_ge(m["summed"], q * 2 + (s // 2 - 1))
                    add(j - 1, (s - 1) % NSLOT, q if s else q - 1)

            steps(dve, N, NSLOT, body)
            dve.wait_ge(m["summed"], N_EXP - 1)
            add(N - 1, (N - 1) % NSLOT, (N - 1) // NSLOT)


def second_block(nc, c, a):
    with ExitStack() as st:
        def sb(stack, name, shape):
            return on_chip(nc, c, stack, name, shape)
        c.par2, c.head_ones, c.masks, c.ident2 = (sb(st, "params2", [P, N_PAR2]), sb(st, "head_ones", [P, P]), sb(st, "masks", [P, 5, P]),
                                                  sb(st, "half_identity", [P, HEAD]))
        c.exchange = sb(st, "exchange", [P, P])
        c.gates = sb(st, "expert_gates", [P, TT, N_EXP])
        load_phase(nc, c, (c.par2[:], a["par2"]), (c.head_ones[:], a["head_ones"]), (c.masks[:], a["masks"]), (c.ident2[:], a["ident2"]), (c.exchange[:], a["exchange"]))
        scale_rows_phase(nc, c, a["final_gain"])
        chunks = [a["rkv"][n] for n in range(3)] + [a["lora_in"]] + [a["gates2"][n] for n in range(4)] + [a["qkv"][n] for n in range(6)]
        norm_phase(nc, c, c.x, c.par2[:, PAR2["norm1"]], c.hT, a["rkv"], MIX_RING)
        with ExitStack() as mid:
            c.gT2, c.rw, c.oT2 = sb(mid, "branch_gates", [P, 16, SEQ]), sb(mid, "rwkv_in", [P, LATE, SEQ + 1]), sb(mid, "att_out", [P, 2, SEQ])
            with ExitStack() as inner:
                c.qkv, c.qT2, c.kT2 = sb(inner, "qkv", [P, TT, 2304]), sb(inner, "qT", [P, 6, SEQ]), sb(inner, "kT", [P, 6, SEQ])
                projection2_phase(nc, c, chunks)
                flat = c.ring[:, :, :].rearrange("p s n -> p (s n)")
                c.bias0 = flat[:, 0:1536].rearrange("p (h l) -> p h l", h=4)
                c.bias1 = flat[:, 1536:1536 + 3072].rearrange("p (h l) -> p h l", h=4)
                c.bias_all, c.bias_reversed = flat[:, 0:4608], flat[:, 4608:9216]
                c.bias_rows = nc.dram_tensor("bias_rows", (12, 512), F32).ap()
                qk_norm_phase(nc, c, a)
                attention_phase(nc, c, dilated_units(c), "dilated", *[t[:, :, :].rearrange("p k s -> p (k s)") for t in (c.hT, c.memT)])
            r = Tensors()
            r.at = 0
            flat = c.ring[:, :, :].rearrange("p s n -> p (s n)")

            def carve(*shape):
                n = int(np.prod(shape))
                assert r.at + n <= NSLOT * SLOT
                v = flat[:, r.at:r.at + n]
                r.at += n
                names = "abcd"[:len(shape)]
                spec = f"p ({' '.join(names)}) -> p {' '.join(names)}"
                return v.rearrange(spec, **dict(zip(names[1:], shape[1:])))

            r.pm, r.lora, r.gup = carve(LATE, SEQ), carve(1, RW)[:, 0], carve(2, RW)
            r.kk, r.k2, r.rate, r.tmp = (carve(RT, SEQ) for _ in range(4))
            r.cum = carve(RT * 4, CHUNK + 1)
            r.decay, r.bonus, r.gate, r.out = (sb(mid, n, [P, RT, SEQ]) for n in ("decay", "bonus", "rwkv_gate", "rwkv_out"))
            with ExitStack() as inner:
                r.kT, r.rT = (sb(inner, n, [P, RT, SEQ]) for n in ("kT", "rT"))
                r.nat = sb(inner, "natural", [P, TT, 3, RW])
                r.aT, r.bT = c.hT[:, 0:RT, :], c.hT[:, RT:KT, :]
                r.Z = c.memT[:, :, :].rearrange("p k s -> p (k s)").rearrange("p (t h e) -> p t h e", t=TT, h=RHEADS)
                rwkv_prepare_phase(nc, c, r, a)
                r.at = 0
                r.mats = {n: carve(4, 4, P) for n in ("p1", "p1t", "p2", "p2t", "lo", "mt", "qb", "qk", "d")}
                r.step, r.fresh, r.state = carve(4, 4, HEAD), carve(4, 4, HEAD), carve(4, HEAD)
                wkv_phase(nc, c, r)
            r.centred, r.root, r.scratch = (sb(mid, n, [P, RT, SEQ]) for n in ("centred", "root", "newton"))
            rwkv_output_phase(nc, c, r, a["merge2"])
            merge_phase(nc, c, [c.oT2, r.out], c.gT2, "second")
        norm_phase(nc, c, c.x, c.par2[:, PAR2["norm2"]], c.hT, a["experts"])
        routing_phase(nc, c, a)
        experts_phase(nc, c, a["experts"])


ORDER = [0, 2, 4, 6, 1, 3, 5, 7]
SLOPES = [2.0 ** (-8.0 * (h + 1) / NQ) for h in ORDER]


def load_phase(nc, c, *pairs):
    block_sems = ("arrived",)
    with phase(nc, *block_sems) as (block, m):
        @block.sync
        def _(sp):
            for dst, src in pairs:
                sp.dma_start(dst, src).then_inc(m["arrived"], 16)
            sp.wait_ge(m["arrived"], 16 * len(pairs))


def layer(nc, c, a, l):
    par = c.par
    load_phase(nc, c, (par[:], a["par"][l]),
               (c.wa[0:HEAD, :, 0:HEAD], a["wa"][l][0:HEAD]), (c.wa[HEAD:P, :, HEAD:P], a["wa"][l][HEAD:P]),
               (c.wx[0:HEAD, :, 0:HEAD], a["wx"][l][0:HEAD]), (c.wx[HEAD:P, :, HEAD:P], a["wx"][l][HEAD:P]))
    norm_phase(nc, c, c.x, par[:, PAR["ffn1"]], c.hT, a["ffn1"][l])
    ffn_phase(nc, c, a["ffn1"][l])
    with ExitStack() as st:
        memx = on_chip(nc, c, st, "memory", [P, TT, D])
        load_phase(nc, c, (memx[:], a["mem"].rearrange("(t p) d -> p t d", p=P)))
        norm_phase(nc, c, memx, par[:, PAR["mem"]], c.memT)
    norm_phase(nc, c, c.x, par[:, PAR["mix"]], c.hT, a["w_in"][l], MIX_RING)
    with ExitStack() as st:
        def sb(name, shape):
            return on_chip(nc, c, st, name, shape)
        c.gT, c.yg, c.xr = sb("gates", [P, N_GATES * KT, SEQ]), sb("gelu_y", [P, KT, SEQ]), sb("conv_in", [P, KT, SEQ + CONV - 1])
        c.oT, c.omT = sb("window_out", [P, 4, SEQ]), sb("memory_out", [P, 4, SEQ])
        c.gate_bias = par[:, PAR["gate_bias"]]
        with phase(nc, "padded") as (block, m):
            @block.vector
            def _(dve):
                nc.vector.memset(c.xr[:, :, 0:CONV - 1], 0.0)
        with ExitStack() as inner:
            def sb2(name, shape):
                return on_chip(nc, c, inner, name, shape)
            c.qT, c.cqT, c.kT, c.v = sb2("q", [P, 4, SEQ]), sb2("mem_q", [P, 4, SEQ]), sb2("k", [P, NKV, SEQ]), sb2("v", [P, TT, P])
            c.memK, c.memV = sb2("mem_k", [P, MEM_HEADS, SEQ]), sb2("mem_v", [P, TT, 512])
            mix_projection_phase(nc, c, par, a["w_in"][l], a["w_kv"][l], a["w_mem"][l])
            flat = [t[:, :, :].rearrange("p k s -> p (k s)") for t in (c.hT, c.memT)]
            attention_phase(nc, c, window_units(c), "window", *flat)
            attention_phase(nc, c, memory_units(c), "memory", *flat)
        lru_phase(nc, c, par, a["merge"][l])
        merge_phase(nc, c, [c.oT, c.omT, c.yg], c.gT, "mix")
    norm_phase(nc, c, c.x, par[:, PAR["ffn2"]], c.hT, a["ffn2"][l])
    ffn_phase(nc, c, a["ffn2"][l])


def program(nc, a, out, stop=None):
    c = Tensors()
    c.ids = count()
    with ExitStack() as st:
        def sb(name, shape):
            return on_chip(nc, c, st, name, shape)
        c.ps = st.enter_context(nc.psum_tensor("psum", [P, 8, 512], F32))
        c.psflat = c.ps[:, :, :].rearrange("p b n -> p (b n)")
        c.ring = sb("weight_ring", [P, NSLOT, SLOT])
        c.loaded = [st.enter_context(nc.semaphore(f"weights_loaded_{i}")) for i in range(NSLOT)]
        c.x, c.hT, c.memT = sb("residual", [P, TT, D]), sb("normed", [P, KT, SEQ]), sb("memory_normed", [P, KT, SEQ])
        c.ident = sb("identity", [P, P])
        with ExitStack() as first:
            def sb1(name, shape):
                return on_chip(nc, c, first, name, shape)
            c.par, c.distance = sb1("params", [P, N_PAR]), sb1("distances", [P, 3 * P])
            c.wa, c.wx = sb1("gate_a_blocks", [P, KT, P]), sb1("gate_x_blocks", [P, KT, P])
            with phase(nc, "arrived") as (block, m):
                @block.sync
                def _(sp):
                    pairs = ((c.x[:], a["x"].rearrange("(t p) d -> p t d", p=P)), (c.ident[:], a["ident"]),
                             (c.distance[:], a["distance"]))
                    for dst, src in pairs:
                        sp.dma_start(dst, src).then_inc(m["arrived"], 16)
                    sp.wait_ge(m["arrived"], 16 * len(pairs))

                @block.vector
                def _(dve):
                    nc.vector.memset(c.wa[:], 0.0)
                    nc.vector.memset(c.wx[:], 0.0)
            with nc.Fori(0, DEPTH) as l:
                layer(nc, c, a, l)
        if stop == 1:
            store_phase(nc, c, out)
            return
        second_block(nc, c, a)
        store_phase(nc, c, out)


def store_phase(nc, c, out):
    with phase(nc, "stored") as (block, m):
        @block.sync
        def _(sp):
            sp.dma_start(out.rearrange("(t p) d -> p t d", p=P), c.x[:]).then_inc(m["stored"], 16)
            sp.wait_ge(m["stored"], 16)


def layout(i):
    f = np.float32
    def rows(w, n):
        L, K, N = w.shape
        return w.reshape(L, K // P, P, N // n, n).transpose(0, 3, 2, 1, 4).reshape(L, N // n, P, K // P * n)

    def down(w, n=2):
        L, K, N = w.shape
        return w.reshape(L, K // (n * P), n, P, N).transpose(0, 1, 3, 2, 4).reshape(L, K // (n * P), P, n * N)

    def cols(v):
        return v.reshape(v.shape[0], -1, P).transpose(0, 2, 1)

    a = {}
    a["x"], a["mem"] = i["x"][0], i["mem"][0]
    a["ident"] = np.eye(P, dtype=f)
    q, k = np.arange(SEQ)[:, None], np.arange(SEQ)[None, :]
    seen = (k // CHUNK <= q // CHUNK) & (k // CHUNK >= q // CHUNK - 2)
    dist = np.where(seen, -np.abs(q - k), NEG).astype(f)
    a["distance"] = np.concatenate([dist[:P, :P], dist[P:, :]], 1)
    for n in (1, 2):
        a[f"ffn{n}"] = np.concatenate([rows(i[f"ffn{n}_w_gate"], F_STEP), rows(i[f"ffn{n}_w_up"], F_STEP), down(i[f"ffn{n}_w_down"])], 3)
    w = i["w_in"]
    o = np.cumsum([0, 512, 128, 128, 1024, 1024, 512, 3072])
    part = [w[:, :, o[n]:o[n + 1]] for n in range(7)]
    def order(g):
        return [g[..., n * D:(n + 1) * D] for n in (0, 2, 1)]

    a["w_in"] = rows(np.concatenate([part[0], part[5], part[3], part[4], *order(part[6])], 2), 512)
    a["w_kv"] = rows(np.concatenate([part[1], part[2]], 2), 256)[:, 0]
    a["w_mem"] = rows(i["w_mem_kv"], 512)
    a["merge"] = np.concatenate([rows(i["w_attn_out"], F_STEP), rows(i["w_mem_out"], F_STEP), rows(i["w_lru_out"], F_STEP),
                                 down(i["w_out"])], 3)
    L = DEPTH
    gb = np.concatenate(order(i["gate_bias"]), 1)
    small = [cols(i["ffn1_norm"]), cols(i["mix_norm"]), cols(i["mem_norm"]), cols(i["ffn2_norm"]), cols(gb),
             i["conv_w"].reshape(L, CONV, KT, P).transpose(0, 3, 2, 1).reshape(L, P, CONV * KT),
             cols(i["conv_b"]), cols(i["lru_ba"]), cols(i["lru_bx"]), cols(i["lru_lambda"]),
             np.repeat(i["attn_sinks"][:, None, ORDER], P, 1)]
    a["par"] = np.concatenate(small, 2)
    for n in ("wa", "wx"):
        a[n] = i[f"lru_{n}"].reshape(L, KT, 2, HEAD, HEAD).transpose(0, 2, 3, 1, 4).reshape(L, P, KT, HEAD)
    w = i["w_in_2"][0]
    n1, n2 = 2304, 2304 + 3 * RW
    qkv, rkv, lora, gates = w[:, :n1], w[:, n1:n2], w[:, n2:n2 + 288], w[:, n2 + 288:]
    a["qkv"], a["rkv"], a["gates2"] = rows(qkv[None], NAT)[0], rows(rkv[None], 512)[0], rows(gates[None], 512)[0]
    a["lora_in"] = rows(lora[None], 288)[0, 0]
    mu = np.concatenate([i["rwkv_shift_mu_2"], np.zeros((1, LATE * P - 1824), f)], 1)

    def heads_gain(g):
        return np.concatenate([g[0, n // 2][[*range(HEAD), *range(HEAD)], None] for n in range(6)], 1)

    a["par2"] = np.concatenate([cols(i["norm1_gain_2"])[0], cols(i["norm2_gain_2"])[0], heads_gain(i["q_norm_gain_2"]), heads_gain(i["k_norm_gain_2"]),
                                cols(mu)[0]] + [cols(i[f"rwkv_{n}_2"].reshape(1, RW))[0] for n in ("w0", "a0", "k_k", "k_a", "r_k", "ln_w", "ln_b")], 1)
    a["final_gain"] = np.repeat(i["final_norm"][None], P, 0)
    a["lora"] = np.concatenate([i["rwkv_w_up_2"][0], i["rwkv_a_up_2"][0]], 0)
    gup = np.concatenate([i["rwkv_g_up_2"][0], np.zeros((2 * P - 160, RW), f)], 0)
    a["gup"] = gup.reshape(2, P, RW).transpose(1, 0, 2)
    same = (np.arange(P)[:, None] // HEAD == np.arange(P)[None, :] // HEAD)
    a["head_ones"] = same.astype(f)
    a["exchange"] = np.eye(P, dtype=f)[::-1]
    a["ident2"] = np.tile(np.eye(HEAD, dtype=f), (2, 1))
    s, t = np.arange(P)[:, None], np.arange(P)[None, :]
    same16 = s // 16 == t // 16
    a["masks"] = np.stack([same16 & (s < t), same & ~same16 & (s > t), same16 & (s > t), same & (s < t), same & (s <= t)], 1).astype(f)
    d = 255 - np.arange(512)
    df = np.maximum(d, 1).astype(f)
    large = 16 + (np.log(df / f(16)) / f(np.log(2048 / 16)) * f(16)).astype(np.int32)
    bucket = np.where(d < 16, d, np.minimum(large, N_BUCKETS - 1))
    hot = np.zeros((N_BUCKETS + 1, GROUPS, 512), f)
    for g, dil in enumerate(DIL):
        seen = (d >= 0) & (d % dil == 0) & (d <= P * dil)
        hot[:N_BUCKETS, g] = seen & (bucket[None] == np.arange(N_BUCKETS)[:, None])
        hot[N_BUCKETS, g] = np.where(seen, 0, NEG)
    a["onehot"], a["bias_table"] = hot, i["rel_bias_table_2"]
    a["merge2"] = np.concatenate([rows(i["w_att_out_2"], F_STEP), rows(i["w_rwkv_out_2"], F_STEP), down(i["w_out_2"])], 3)[0]
    a["router"] = np.concatenate([i["w_group_router_2"][0], i["w_expert_router_2"][0]], 1).reshape(KT, P, -1).transpose(1, 0, 2)
    a["router_bias"] = np.repeat(np.concatenate([i["b_group_router_2"], i["b_expert_router_2"]], 1), P, 0)
    a["ordinals"] = np.repeat(np.arange(N_PER, dtype=f)[None], P, 0)
    a["experts"] = np.concatenate([rows(i["w_expert_gate_2"][0], F_STEP), rows(i["w_expert_up_2"][0], F_STEP), down(i["w_expert_down_2"][0])],
                                  3).reshape(EXP_STEPS, P, SLOT)
    return {n: np.ascontiguousarray(v) for n, v in a.items()}


def kernel(**inputs):
    import concourse.bacc as _bacc
    from concourse.bass_utils import run_bass_kernel_spmd as _run

    nc = _bacc.Bacc("TRN2", target_bir_lowering=False, num_devices=1)
    arrays, args = {}, {}
    for name, a in layout({n: np.asarray(v) for n, v in inputs.items()}).items():
        arrays[f"in_{name}_dram"] = a
        args[name] = nc.dram_tensor(f"in_{name}_dram", a.shape, mybir.dt.from_np(a.dtype), kind="ExternalInput").ap()
    out = nc.dram_tensor("out_0_dram", (SEQ, D), F32, kind="ExternalOutput").ap()
    program(nc, args, out)
    r = _run(nc, [arrays], core_ids=[0])
    return r.results[0]["out_0_dram"].reshape(1, SEQ, D)
```

```python
from contextlib import ExitStack, contextmanager
from itertools import count

import concourse.bass as bass
from concourse import mybir
import numpy as np

F32 = mybir.dt.float32
ALU = mybir.AluOpType
ACT = mybir.ActivationFunctionType
AX = mybir.AxisListType

P = 128
SEQ = 256
TT = SEQ // P
D = 1024
KT = D // P
DEPTH = 2
EPS = 1e-6
NEG = -1e30

SLOT = 6144
NSLOT = 4
F_STEP = 256
D_FF = 2816
FF_STEPS = D_FF // F_STEP
GATE, UP, DOWN = 0, 2048, 4096

HEAD = 64
NQ = 8
NKV = 2
MEM_HEADS = 4
N_GATES = 3
CONV = 4
CHUNK = 64
PAR = {}
_at = 0
for _name, _n in (("ffn1", 8), ("mix", 8), ("mem", 8), ("ffn2", 8), ("gate_bias", 24), ("conv_w", 32),
                  ("conv_b", 8), ("ba", 8), ("bx", 8), ("lam", 8), ("sinks", 8)):
    PAR[_name] = slice(_at, _at + _n)
    _at += _n
N_PAR = _at

GROUPS = 3
GHEADS = 4
DIL = (1, 4, 16)
N_BUCKETS = 32
RW = 512
RT = RW // P
RHEADS = 8
GN_EPS = 64e-5
N_GRP, N_PER = 4, 8
N_EXP = N_GRP * N_PER
D_EXP = 512
EXP_STEPS = N_EXP * D_EXP // F_STEP
PAR2 = {}
_at = 0
for _name, _n in (("norm1", 8), ("norm2", 8), ("qgain", 6), ("kgain", 6), ("mu", 15), ("w0", 4), ("a0", 4),
                  ("k_k", 4), ("k_a", 4), ("r_k", 4), ("ln_w", 4), ("ln_b", 4)):
    PAR2[_name] = slice(_at, _at + _n)
    _at += _n
N_PAR2 = _at


class Tensors:
    pass


@contextmanager
def phase(nc, *names, keep=()):
    with ExitStack() as stack:
        sems = {n: stack.enter_context(nc.semaphore(n)) for n in names}
        with nc.Block() as block:
            yield block, sems
        for s in list(sems.values()) + list(keep):
            nc.gpsimd.sem_clear(s)
        nc.all_engine_barrier()


def on_chip(nc, c, stack, name, shape):
    return stack.enter_context(nc.sbuf_tensor(f"{name}_{next(c.ids)}", shape, F32))


class Chain:

    def __init__(self, eng, sem):
        self.eng, self.sem, self.counts = eng, sem, {}

    def __call__(self, ins, sem=None):
        sem = sem or self.sem
        n = self.counts[id(sem)] = self.counts.get(id(sem), 0) + 1
        ins.then_inc(sem, 1)
        self.eng.wait_ge(sem, n)


def steps(eng, n, head, body):
    for j in range(head):
        body(j, j % NSLOT, j // NSLOT)
    turns = (n - head) // NSLOT
    with eng.Fori(0, turns) as a:
        for u in range(head, head + NSLOT):
            body(a * NSLOT + u, u % NSLOT, a + u // NSLOT)
    for j in range(head + turns * NSLOT, n):
        body(j, j % NSLOT, j // NSLOT)


def prefetch(sp, c, stream, n=NSLOT):
    width = stream.shape[2]
    for s in range(n):
        sp.dma_start(c.ring[:, s, 0:width], stream[s]).then_inc(c.loaded[s], 16)


def norm_phase(nc, c, src, gain, dst, stream=None, n=NSLOT, scaled=None, load=prefetch):
    with ExitStack() as st:
        sq = on_chip(nc, c, st, "norm_squares", [P, D])
        xn = scaled or on_chip(nc, c, st, "norm_scaled", [P, TT, D])
        s = on_chip(nc, c, st, "norm_stats", [P, 4, TT])
        block, m = st.enter_context(phase(nc, "squared", "mean_ready", "root_ready", "scaled", "turned", "vstep", "astep"))

        @block.sync
        def _(sp):
            if stream is not None:
                load(sp, c, stream, n)

        @block.scalar
        def _(act):
            for t in range(TT):
                if t:
                    act.wait_ge(m["squared"], t)
                nc.scalar.activation(sq[:], src[:, t, :], ACT.Square, accum_out=s[:, 0, t:t + 1]).then_inc(m["squared"], 1)
            act.wait_ge(m["mean_ready"], 1)
            nc.scalar.activation(s[:, 2, :], s[:, 1, :], ACT.Sqrt).then_inc(m["root_ready"], 1)
            for k in (2, 3, 6, 7):
                act.wait_ge(m["turned"], k // 2 * 2 + 2)
                nc.scalar.activation(dst[:, k, :], c.ps[:, k // 2, (k % 2) * 256:(k % 2) * 256 + 256],
                                     ACT.Identity, scale=gain[:, k:k + 1])

        @block.vector
        def _(dve):
            do = Chain(dve, m["vstep"])
            dve.wait_ge(m["squared"], TT)
            do(nc.vector.tensor_scalar(s[:, 1, :], s[:, 0, :], 1.0 / D, EPS, ALU.mult, ALU.add), m["mean_ready"])
            dve.wait_ge(m["root_ready"], 1)
            inverse_root(nc, do, s[:, 2, :], s[:, 1, :], s[:, 2, :], s[:, 3, :])
            for t in range(TT):
                nc.vector.tensor_scalar(xn[:, t, :], src[:, t, :], s[:, 2, t:t + 1], None, ALU.mult).then_inc(m["scaled"], 1)
            for k in (0, 1, 4, 5):
                dve.wait_ge(m["turned"], k // 2 * 2 + 2)
                nc.vector.tensor_scalar(dst[:, k, :], c.ps[:, k // 2, (k % 2) * 256:(k % 2) * 256 + 256],
                                        gain[:, k:k + 1], None, ALU.mult)

        @block.tensor
        def _(pe):
            pe.wait_ge(m["scaled"], TT)
            for k in range(KT):
                for t in range(TT):
                    at = (k % 2) * 256 + t * P
                    last = nc.tensor.transpose(c.ps[:, k // 2, at:at + P], xn[:, t, k * P:(k + 1) * P], c.ident[:])
                last.then_inc(m["turned"], 1)


def inverse_root(nc, do, out, mean, root, tmp):
    do(nc.vector.reciprocal(out, root))
    do(nc.vector.tensor_tensor(tmp, out, out, ALU.mult))
    do(nc.vector.tensor_tensor(tmp, tmp, mean, ALU.mult))
    do(nc.vector.tensor_scalar(tmp, tmp, -0.5, 1.5, ALU.mult, ALU.add))
    do(nc.vector.tensor_tensor(out, out, tmp, ALU.mult))


def gate_up(nc, pe, c, m, j, s, q):
    pe.wait_ge(c.loaded[s], q * 16 + 16)
    for f in range(2):
        if not isinstance(j, int) or j >= 2:
            pe.wait_ge(m["hid_done"], j * 2 + (f - 3))
        bank = (s % 2) * 2 + f
        for part, at in ((0, GATE), (1, UP)):
            for k in range(KT):
                w = at + k * F_STEP + f * P
                last = nc.tensor.matmul(c.ps[:, bank, part * SEQ:(part + 1) * SEQ], c.ring[:, s, w:w + P],
                                        c.hT[:, k, :], start=(k == 0), stop=(k == KT - 1))
            if part:
                last.then_inc(m["up_ready"], 1)


def silu_gate(nc, act, c, m, gated, j, s):
    for f in range(2):
        act.wait_ge(m["up_ready"], j * 2 + (f + 1))
        nc.scalar.activation(gated[:, s % 2, f, :], c.ps[:, (s % 2) * 2 + f, 0:SEQ], ACT.Silu).then_inc(m["silu_done"], 1)


def hidden(nc, dve, c, m, hid, gated, j, s):
    if not isinstance(j, int) or j >= NSLOT:
        dve.wait_ge(m["down_used"], j - (NSLOT - 1))
    for f in range(2):
        dve.wait_ge(m["silu_done"], j * 2 + (f + 1))
        nc.vector.tensor_tensor(hid[:, s, f, :], gated[:, s % 2, f, :], c.ps[:, (s % 2) * 2 + f, SEQ:2 * SEQ],
                                ALU.mult).then_inc(m["hid_done"], 1)


F32R = mybir.dt.float32r
NPART = 4
PART = 2048


def split_bufs(nc, c, stack, name, shape):
    return [stack.enter_context(nc.sbuf_tensor(f"{name}_{part}_{next(c.ids)}", shape, F32R)) for part in ("high", "low")]


def terms(a, b):
    return (a[0], b[0]), (a[0], b[1]), (a[1], b[0])


def take_high(nc, split, at, src):
    return nc.scalar.activation(split[0][at], src, ACT.Copy)


def take_low(nc, split, at, src):
    return nc.vector.tensor_tensor(split[1][at], src, split[0][at].bitcast(F32), ALU.subtract)


def ffn_phase(nc, c, stream):
    N = FF_STEPS
    with ExitStack() as st:
        w = split_bufs(nc, c, st, "weights", [P, NPART, PART])
        hs = split_bufs(nc, c, st, "inputs", [P, KT, SEQ])
        hids = split_bufs(nc, c, st, "hidden", [P, 2, 2, SEQ])
        hid = on_chip(nc, c, st, "hidden_whole", [P, 2, SEQ])
        gated = on_chip(nc, c, st, "silu_gate", [P, 2, SEQ])
        block, m = st.enter_context(phase(nc, "in_high", "in_split", "high_done", "split_done", "part_used", "silu_done", "hid_done",
                                          "hid_high", "hid_split", keep=c.loaded))
        whole = (slice(None), slice(None), slice(None))

        def buf(number):
            return (slice(None), number % NPART, slice(None))

        def later(j, least):
            return not isinstance(j, int) or j >= least

        @block.sync
        def _(sp):
            for j in range(NSLOT, N):
                sp.wait_ge(m["split_done"], 3 * j - 7)
                sp.dma_start(c.ring[:, j % NSLOT, :], stream[j]).then_inc(c.loaded[j % NSLOT], 16)

        @block.tensor
        def _(pe):
            def gate_up(j, s):
                if later(j, 2):
                    pe.wait_ge(m["hid_done"], j - 1)
                for part in range(2):
                    number = 3 * s - 1 + part if s or later(j, 1) else part
                    pe.wait_ge(m["split_done"], j * 3 + part if later(j, 1) else part + 1)
                    ws = [x[buf(number)] for x in w]
                    for f in range(2):
                        for k in range(KT):
                            at = slice(k * F_STEP + f * P, k * F_STEP + (f + 1) * P)
                            for n, (a, b) in enumerate(terms([x[:, at] for x in ws], [x[:, k, :] for x in hs])):
                                last = nc.tensor.matmul(c.ps[:, s % 2 * 2 + f, part * SEQ:(part + 1) * SEQ], a, b,
                                                        start=(k == 0 and n == 0), stop=(k == KT - 1 and n == 2))
                    last.then_inc(m["part_used"], 1)

            def down(j, s, number, count, first=False, final=False):
                pe.wait_ge(m["hid_split"], j + 1)
                pe.wait_ge(m["split_done"], count)
                ws = [x[buf(number)] for x in w]
                for f in range(2):
                    for t in range(TT):
                        for h in range(2):
                            at = slice(f * D + h * 512, f * D + (h + 1) * 512)
                            pairs = terms([x[:, s % 2, f, t * P:(t + 1) * P] for x in hids], [x[:, at] for x in ws])
                            for n, (a, b) in enumerate(pairs):
                                last = nc.tensor.matmul(c.ps[:, 4 + 2 * t + h, :], a, b, start=(first and f == 0 and n == 0),
                                                        stop=(final and f == 1 and n == 2))
                last.then_inc(m["part_used"], 1)

            def body(j, s, q):
                gate_up(j, s)
                if later(j, 1):
                    down(j - 1, s - 1, 3 * s + 1, j * 3 + 2, first=isinstance(j, int) and j == 1)

            pe.wait_ge(m["in_split"], 1)
            steps(pe, N, 2, body)
            down(N - 1, N - 1, 3 * N - 1, 3 * N, final=True)

        @block.scalar
        def _(act):
            def high(number, slot, q, part, used):
                if q is not None:
                    act.wait_ge(c.loaded[slot], q * 16 + 16)
                if used is not None:
                    act.wait_ge(m["part_used"], used)
                take_high(nc, w, buf(number), c.ring[:, slot, part * PART:(part + 1) * PART]).then_inc(m["high_done"], 1)

            def silu(j, s):
                act.wait_ge(m["part_used"], j * 3 + 1 if later(j, 1) else 2)
                nc.scalar.activation(gated[:], c.ps[:, s % 2 * 2:s % 2 * 2 + 2, 0:SEQ], ACT.Silu).then_inc(m["silu_done"], 1)

            def hid_high(j, s):
                act.wait_ge(m["hid_done"], j + 1)
                take_high(nc, hids, (slice(None), s % 2, slice(None), slice(None)), hid[:]).then_inc(m["hid_high"], 1)

            def body(j, s, q):
                if not later(j, 1):
                    high(0, 0, 0, 0, None)
                    high(1, 0, None, 1, None)
                    return
                high(3 * s - 1, s, q, 0, j * 3 - 4 if later(j, 2) else None)
                high(3 * s, s, None, 1, j * 3 - 3 if later(j, 2) else None)
                silu(j - 1, s - 1)
                high(3 * s + 1, (s - 1) % NSLOT, None, 2, None)
                hid_high(j - 1, s - 1)

            take_high(nc, hs, whole, c.hT[:]).then_inc(m["in_high"], 1)
            steps(act, N, 2, body)
            silu(N - 1, N - 1)
            high(3 * N - 1, (N - 1) % NSLOT, None, 2, None)
            hid_high(N - 1, N - 1)

        @block.vector
        def _(dve):
            def low(number, slot, part, count):
                dve.wait_ge(m["high_done"], count)
                take_low(nc, w, buf(number), c.ring[:, slot, part * PART:(part + 1) * PART]).then_inc(m["split_done"], 1)

            def hidden_values(j, s):
                if later(j, 1):
                    dve.wait_ge(m["hid_split"], j)
                dve.wait_ge(m["silu_done"], j + 1)
                nc.vector.tensor_tensor(hid[:], gated[:], c.ps[:, s % 2 * 2:s % 2 * 2 + 2, SEQ:2 * SEQ], ALU.mult).then_inc(m["hid_done"], 1)

            def hid_low(j, s):
                dve.wait_ge(m["hid_high"], j + 1)
                take_low(nc, hids, (slice(None), s % 2, slice(None), slice(None)), hid[:]).then_inc(m["hid_split"], 1)

            def body(j, s, q):
                if not later(j, 1):
                    low(0, 0, 0, 1)
                    low(1, 0, 1, 2)
                    return
                low(3 * s - 1, s, 0, j * 3)
                low(3 * s, s, 1, j * 3 + 1)
                hidden_values(j - 1, s - 1)
                low(3 * s + 1, (s - 1) % NSLOT, 2, j * 3 + 2)
                hid_low(j - 1, s - 1)

            dve.wait_ge(m["in_high"], 1)
            take_low(nc, hs, whole, c.hT[:]).then_inc(m["in_split"], 1)
            steps(dve, N, 2, body)
            hidden_values(N - 1, N - 1)
            low(3 * N - 1, (N - 1) % NSLOT, 2, 3 * N)
            hid_low(N - 1, N - 1)
            dve.wait_ge(m["part_used"], 3 * N)
            for t in range(TT):
                for n in range(2):
                    at = slice(n * 512, (n + 1) * 512)
                    nc.vector.scalar_tensor_tensor(c.x[:, t, at], c.ps[:, 4 + 2 * t + n, :], 0.5, c.x[:, t, at],
                                                   ALU.mult, ALU.add)


MIX_RING = 3
MIX_BANKS = 6
QS, CQS = HEAD ** -0.5, 128 ** -0.5


def mix_projection_phase(nc, c, par, w_in, w_kv, w_mem):
    N = 12
    VT = 16
    NT = 48
    with ExitStack() as st:
        block, m = st.enter_context(phase(nc, "tile_ready", "late_ready", "v_evacuated", "a_evacuated", keep=c.loaded))

        @block.sync
        def _(sp):
            with sp.Fori(0, 3) as a:
                for u in range(MIX_RING):
                    sp.wait_ge(m["tile_ready"], a * 12 + (4 * u + 4))
                    sp.dma_start(c.ring[:, u, 0:4096], w_in[a * MIX_RING + (3 + u)]).then_inc(c.loaded[u], 16)
            for u, src in enumerate((w_kv, w_mem[0], w_mem[1])):
                sp.wait_ge(m["tile_ready"], 36 + 4 * u + 4)
                sp.dma_start(c.ring[:, u, 0:src.shape[1]], src).then_inc(c.loaded[u], 16)

        @block.tensor
        def _(pe):
            def tile(s, u, bank):
                for k in range(KT):
                    w = k * 512 + u * P
                    last = nc.tensor.matmul(c.ps[:, bank, 0:SEQ], c.ring[:, s, w:w + P], c.hT[:, k, :],
                                            start=(k == 0), stop=(k == KT - 1))
                last.then_inc(m["tile_ready"], 1)

            for i in range(6):
                pe.wait_ge(c.loaded[i % 3], i // 3 * 16 + 16)
                for u in range(4):
                    n = i * 4 + u
                    if n >= VT + MIX_BANKS:
                        pe.wait_ge(m["a_evacuated"], n - MIX_BANKS - VT + 1)
                    elif n >= MIX_BANKS:
                        pe.wait_ge(m["v_evacuated"], n - MIX_BANKS + 1)
                    tile(i % 3, u, n % MIX_BANKS)
            with pe.Fori(0, 2) as a:
                for u in range(12):
                    if u % 4 == 0:
                        pe.wait_ge(c.loaded[u // 4], a * 16 + 48)
                    pe.wait_ge(m["a_evacuated"], a * 12 + (24 + u - MIX_BANKS - VT + 1))
                    tile(u // 4, u % 4, u % MIX_BANKS)
            pe.wait_ge(c.loaded[0], 80)
            for h in range(NKV):
                pe.wait_ge(m["a_evacuated"], 27 + h)
                for half in range(2):
                    for k in range(KT):
                        w = k * 256 + h * HEAD
                        last = nc.tensor.matmul(c.ps[half * HEAD:(half + 1) * HEAD, h, 0:SEQ], c.ring[:, 0, w:w + HEAD],
                                                c.hT[:, k, :], start=(k == 0), stop=(k == KT - 1))
                last.then_inc(m["late_ready"], 1)
            pe.wait_ge(m["a_evacuated"], 29)
            for t in range(TT):
                for k in range(KT):
                    w = k * 256 + P
                    last = nc.tensor.matmul(c.ps[:, 2, t * P:(t + 1) * P], c.hT[:, k, t * P:(t + 1) * P],
                                            c.ring[:, 0, w:w + P], start=(k == 0), stop=(k == KT - 1))
            last.then_inc(m["late_ready"], 1)
            pe.wait_ge(c.loaded[1], 80)
            for h in range(MEM_HEADS):
                if h < 3:
                    pe.wait_ge(m["a_evacuated"], 30 + h)
                else:
                    pe.wait_ge(m["v_evacuated"], VT + 1)
                for k in range(KT):
                    w = k * 512 + h * P
                    last = nc.tensor.matmul(c.ps[:, (3 + h) % MIX_BANKS, 0:SEQ], c.ring[:, 1, w:w + P], c.memT[:, k, :],
                                            start=(k == 0), stop=(k == KT - 1))
                last.then_inc(m["late_ready"], 1)
            pe.wait_ge(c.loaded[2], 80)
            for t in range(TT):
                pe.wait_ge(m["v_evacuated"], VT + 2 + t)
                for k in range(KT):
                    last = nc.tensor.matmul(c.ps[:, 1 + t, :], c.memT[:, k, t * P:(t + 1) * P],
                                            c.ring[:, 2, k * 512:(k + 1) * 512], start=(k == 0), stop=(k == KT - 1))
                last.then_inc(m["late_ready"], 1)

        @block.scalar
        def _(act):
            for k in range(KT):
                act.wait_ge(m["tile_ready"], VT + k + 1)
                nc.scalar.activation(c.yg[:, k, :], c.ps[:, (VT + k) % MIX_BANKS, 0:SEQ], ACT.Gelu_apprx_tanh).then_inc(m["a_evacuated"], 1)
            with act.Fori(0, 2) as a:
                for u in range(12):
                    act.wait_ge(m["tile_ready"], a * 12 + (24 + u + 1))
                    g = a * 12 + u
                    nc.scalar.activation(c.gT[:, bass.ds(g, 1), :], c.ps[:, u % MIX_BANKS:u % MIX_BANKS + 1, 0:SEQ], ACT.Sigmoid,
                                         bias=c.gate_bias[:, bass.ds(g, 1)]).then_inc(m["a_evacuated"], 1)

        @block.vector
        def _(dve):
            for n in range(VT):
                dve.wait_ge(m["tile_ready"], n + 1)
                src = c.ps[:, n % MIX_BANKS, 0:SEQ]
                if n < 4:
                    ins = nc.vector.tensor_scalar(c.qT[:, n, :], src, QS, None, ALU.mult)
                elif n < 8:
                    ins = nc.vector.tensor_scalar(c.cqT[:, n - 4, :], src, CQS, None, ALU.mult)
                else:
                    ins = nc.vector.tensor_copy(c.xr[:, n - 8, CONV - 1:], src)
                ins.then_inc(m["v_evacuated"], 1)
            outs = [c.kT[:, 0, :], c.kT[:, 1, :], c.v[:, :, :].rearrange("p t d -> p (t d)")]
            outs += [c.memK[:, h, :] for h in range(MEM_HEADS)] + [c.memV[:, t, :] for t in range(TT)]
            banks = [0, 1, 2, 3, 4, 5, 0, 1, 2]
            for n, (out, bank) in enumerate(zip(outs, banks)):
                dve.wait_ge(m["late_ready"], n + 1)
                nc.vector.tensor_copy(out, c.ps[:, bank, 0:out.shape[1]]).then_inc(m["v_evacuated"], 1)


def lru_phase(nc, c, par, stream):
    with ExitStack() as st:
        def sb(name, shape):
            return on_chip(nc, c, st, name, shape)
        xc, r = c.hT, c.memT
        gi, a2 = (sb(f"lru_{n}", [P, KT, SEQ]) for n in ("in_gate", "room"))
        rate = sb("lru_rate", [P, KT])
        block, m = st.enter_context(phase(nc, "conv_done", "gates_ready", "act_done", "decay_done", "room_done", "root_done", "rate_done", "vstep", "astep"))

        def cols(name):
            return par[:, PAR[name]]

        @block.sync
        def _(sp):
            prefetch(sp, c, stream)

        @block.scalar
        def _(act):
            do = Chain(act, m["astep"])
            do(nc.scalar.activation(rate[:], cols("lam"), ACT.Exp, scale=-1.0))
            do(nc.scalar.activation(rate[:], rate[:], ACT.Ln, bias=1.0), m["act_done"])
            for k in range(KT):
                act.wait_ge(m["gates_ready"], k + 1)
                nc.scalar.activation(r[:, k, :], c.ps[:, k, 0:SEQ], ACT.Sigmoid, bias=cols("ba")[:, k:k + 1]).then_inc(m["astep"], 1)
                nc.scalar.activation(gi[:, k, :], c.ps[:, k, SEQ:2 * SEQ], ACT.Sigmoid, bias=cols("bx")[:, k:k + 1]).then_inc(m["astep"], 1)
            act.wait_ge(m["astep"], 1 + 2 * KT)
            act.wait_ge(m["rate_done"], 1)
            for k in range(KT):
                nc.scalar.activation(r[:, k, :], r[:, k, :], ACT.Exp, scale=rate[:, k:k + 1]).then_inc(m["decay_done"], 1)
            act.wait_ge(m["room_done"], 1)
            nc.scalar.activation(a2[:], a2[:], ACT.Sqrt).then_inc(m["root_done"], 1)

        @block.vector
        def _(dve):
            do = Chain(dve, m["vstep"])
            dve.wait_ge(m["act_done"], 1)
            do(nc.vector.tensor_scalar(rate[:], rate[:], -8.0, None, ALU.mult), m["rate_done"])
            for i in range(CONV):
                for k in range(KT):
                    w = cols("conv_w")[:, k * CONV + i:k * CONV + i + 1]
                    x = c.xr[:, k, i:i + SEQ]
                    if i == 0:
                        ins = nc.vector.tensor_scalar(xc[:, k, :], x, w, cols("conv_b")[:, k:k + 1], ALU.mult, ALU.add)
                    else:
                        dve.wait_ge(m["vstep"], (i - 1) * KT + k + 1)
                        ins = nc.vector.scalar_tensor_tensor(xc[:, k, :], x, w, xc[:, k, :], ALU.mult, ALU.add)
                    ins.then_inc(m["vstep"] if i < CONV - 1 else m["conv_done"], 1)
            do.counts[id(m["vstep"])] = (CONV - 1) * KT
            dve.wait_ge(m["decay_done"], KT)
            do(nc.vector.tensor_tensor(a2[:], r[:], r[:], ALU.mult))
            do(nc.vector.tensor_scalar(a2[:], a2[:], -1.0, 1.0, ALU.mult, ALU.add))
            do(nc.vector.tensor_scalar(a2[:], a2[:], 0.0, None, ALU.max), m["room_done"])
            dve.wait_ge(m["conv_done"], KT)
            do(nc.vector.tensor_tensor(gi[:], gi[:], xc[:], ALU.mult))
            dve.wait_ge(m["root_done"], 1)
            do(nc.vector.memset(a2[:, :, 0:1], 1.0))
            do(nc.vector.tensor_tensor(gi[:], gi[:], a2[:], ALU.mult))
            for k in range(KT):
                nc.vector.tensor_tensor_scan(a2[:, k, :], r[:, k, :], gi[:, k, :], 0.0, ALU.mult, ALU.add).then_inc(m["vstep"], 1)
            dve.wait_ge(m["vstep"], do.counts[id(m["vstep"])] + KT)
            nc.vector.tensor_tensor(c.yg[:], a2[:], c.yg[:], ALU.mult)

        @block.tensor
        def _(pe):
            for k in range(KT):
                pe.wait_ge(m["conv_done"], k + 1)
                nc.tensor.matmul(c.ps[:, k, 0:SEQ], c.wa[:, k, :], xc[:, k, :], start=True, stop=True)
                nc.tensor.matmul(c.ps[:, k, SEQ:2 * SEQ], c.wx[:, k, :], xc[:, k, :], start=True, stop=True).then_inc(m["gates_ready"], 1)


class Unit:

    def __init__(self, scores, heads, length, pitch, outs, dst, from_ps, bias=None, slopes=None, distance=None, sink=None):
        self.scores, self.heads, self.length, self.pitch = scores, heads, length, pitch
        self.outs, self.dst, self.from_ps = outs, dst, from_ps
        self.bias, self.slopes, self.distance, self.sink = bias, slopes, distance, sink


def attention_phase(nc, c, units, name, S, pT):
    with ExitStack() as st:
        stats = on_chip(nc, c, st, f"{name}_stats", [P, 4, 8])
        block, m = st.enter_context(phase(nc, "scores_ready", "shifted", "exp_done", "sink_done", "probs_ready", "turned", "turned_copied", "out_ready", "out_copied", "vstep"))

        @block.tensor
        def _(pe):
            copies = 0
            for n, u in enumerate(units):
                if n:
                    pe.wait_ge(m["turned_copied"], n)
                    pe.wait_ge(m["out_copied"], n)
                for at, lhsT, rhs in u.scores:
                    last = nc.tensor.matmul(c.psflat[:, at:at + rhs.shape[1]], lhsT, rhs, start=True, stop=True)
                last.then_inc(m["scores_ready"], 1)
                pe.wait_ge(m["probs_ready"], n + 1)
                per = u.length // P
                for b in range(u.heads * per):
                    at = b // per * u.pitch + b % per * P
                    last = nc.tensor.transpose(c.psflat[:, 2048 + b * P:2048 + (b + 1) * P], S[:, at:at + P], c.ident[:])
                last.then_inc(m["turned"], 1)
                pe.wait_ge(m["turned_copied"], n + 1)
                for part, at, terms in u.outs:
                    for i, (val, b) in enumerate(terms):
                        last = nc.tensor.matmul(c.psflat[part, at:at + P], val, pT[:, b * P:(b + 1) * P],
                                                start=(i == 0), stop=(i == len(terms) - 1))
                last.then_inc(m["out_ready"], 1)

        @block.scalar
        def _(act):
            for n, u in enumerate(units):
                act.wait_ge(m["shifted"], n + 1)
                Sv = S[:, 0:u.heads * u.pitch].rearrange("p (h l) -> p h l", h=u.heads)[:, :, 0:u.length]
                nc.scalar.activation(Sv, Sv, ACT.Exp).then_inc(m["exp_done"], 1)
                if u.sink is not None:
                    nc.scalar.activation(stats[:, 1, 0:u.heads], stats[:, 1, 0:u.heads], ACT.Exp).then_inc(m["sink_done"], 1)

        @block.vector
        def _(dve):
            do = Chain(dve, m["vstep"])
            sinks = 0
            for n, u in enumerate(units):
                w, H, L = u.heads * u.length, u.heads, u.length
                Sv = S[:, 0:H * u.pitch].rearrange("p (h l) -> p h l", h=H)[:, :, 0:L]
                top, other, total = stats[:, 0, 0:H], stats[:, 1, 0:H], stats[:, 2, 0:H]
                dve.wait_ge(m["scores_ready"], n + 1)
                pv = c.psflat[:, 0:H * u.pitch].rearrange("p (h l) -> p h l", h=H)[:, :, 0:L]
                if u.slopes is not None:
                    for h in range(H):
                        do(nc.vector.scalar_tensor_tensor(Sv[:, h, :], u.distance, u.slopes[h], pv[:, h, :], ALU.mult, ALU.add))
                elif u.bias is not None:
                    do(nc.vector.tensor_tensor(Sv, pv, u.bias, ALU.add))
                else:
                    do(nc.vector.tensor_copy(Sv, pv))
                do(nc.vector.tensor_reduce(top, Sv, AX.X, ALU.max))
                if u.sink is not None:
                    do(nc.vector.tensor_tensor(top, top, u.sink, ALU.max))
                    do(nc.vector.tensor_tensor(other, u.sink, top, ALU.subtract))
                do(nc.vector.tensor_tensor(Sv, Sv, top.unsqueeze(2).to_broadcast([P, H, L]), ALU.subtract), m["shifted"])
                dve.wait_ge(m["exp_done"], n + 1)
                do(nc.vector.tensor_reduce(total, Sv, AX.X, ALU.add))
                if u.sink is not None:
                    sinks += 1
                    dve.wait_ge(m["sink_done"], sinks)
                    do(nc.vector.tensor_tensor(total, total, other, ALU.add))
                do(nc.vector.reciprocal(total, total))
                do(nc.vector.tensor_tensor(Sv, Sv, total.unsqueeze(2).to_broadcast([P, H, L]), ALU.mult), m["probs_ready"])
                dve.wait_ge(m["turned"], n + 1)
                do(nc.vector.tensor_copy(pT[:, 0:w], c.psflat[:, 2048:2048 + w]), m["turned_copied"])
                dve.wait_ge(m["out_ready"], n + 1)
                do(nc.vector.tensor_copy(u.dst, u.from_ps), m["out_copied"])


def window_units(c):
    units = []
    for t in range(TT):
        L = (t + 1) * P
        scores, outs = [], []
        for n, h in enumerate(ORDER):
            kv, half = h // (NQ // NKV), slice(h % 2 * HEAD, h % 2 * HEAD + HEAD)
            scores.append((n * L, c.qT[half, h // 2, t * P:(t + 1) * P], c.kT[half, kv, 0:L]))
            outs.append((half, h // 2 * P, [(c.v[:, j, kv * HEAD:(kv + 1) * HEAD], n * (t + 1) + j) for j in range(t + 1)]))
        distance = c.distance[:, 0:P] if t == 0 else c.distance[:, P:3 * P]
        units.append(Unit(scores=scores, heads=NQ, length=L, pitch=L, slopes=SLOPES, distance=distance, sink=c.par[:, PAR["sinks"]], outs=outs,
                                     dst=c.oT[:, :, t * P:(t + 1) * P],
                                     from_ps=c.psflat[:, 0:512].rearrange("p (a q) -> p a q", a=4)))
    return units


def memory_units(c):
    units = []
    for t in range(TT):
        scores, outs = [], []
        for h in range(MEM_HEADS):
            scores.append((h * SEQ, c.cqT[:, h, t * P:(t + 1) * P], c.memK[:, h, :]))
            outs.append((slice(0, P), h * P, [(c.memV[:, j, h * P:(h + 1) * P], h * TT + j) for j in range(TT)]))
        units.append(Unit(scores=scores, heads=MEM_HEADS, length=SEQ, pitch=SEQ, outs=outs,
                                     dst=c.omT[:, :, t * P:(t + 1) * P],
                                     from_ps=c.psflat[:, 0:512].rearrange("p (a q) -> p a q", a=4)))
    return units


def merge_phase(nc, c, branches, gates, name):
    NB = len(branches)
    WOUT = sum(b.shape[1] for b in branches) * F_STEP
    with ExitStack() as st:
        merged = on_chip(nc, c, st, f"{name}_merged", [P, KT, SEQ])
        term = on_chip(nc, c, st, f"{name}_term", [P, 2, SEQ])
        block, m = st.enter_context(phase(nc, "branches_ready", "merged_done", "out_ready", "vstep", keep=c.loaded))

        @block.tensor
        def _(pe):
            for n in range(KT):
                s, u = n // 2, n % 2
                if u == 0:
                    pe.wait_ge(c.loaded[s], 16)
                if n >= 2:
                    pe.wait_ge(m["merged_done"], n - 1)
                at = 0
                for b, src in enumerate(branches):
                    nk = src.shape[1]
                    for k in range(nk):
                        w = at + k * F_STEP + u * P
                        last = nc.tensor.matmul(c.ps[:, n % 2 * 4 + b, 0:SEQ], c.ring[:, s, w:w + P], src[:, k, :],
                                                start=(k == 0), stop=(k == nk - 1))
                    at += nk * F_STEP
                last.then_inc(m["branches_ready"], 1)
            pe.wait_ge(m["merged_done"], KT)
            for k in range(KT):
                for t in range(TT):
                    for h in range(2):
                        w = WOUT + (k % 2) * D + h * 512
                        last = nc.tensor.matmul(c.ps[:, 4 + 2 * t + h, :], merged[:, k, t * P:(t + 1) * P],
                                                c.ring[:, k // 2, w:w + 512], start=(k == 0), stop=(k == KT - 1))
            last.then_inc(m["out_ready"], 1)

        @block.vector
        def _(dve):
            do = Chain(dve, m["vstep"])
            for n in range(KT):
                dve.wait_ge(m["branches_ready"], n + 1)
                out = merged[:, n, :]
                do(nc.vector.tensor_tensor(out, c.ps[:, n % 2 * 4, 0:SEQ], gates[:, n, :], ALU.mult))
                for b in range(1, NB):
                    do(nc.vector.tensor_tensor(term[:, b % 2, :], c.ps[:, n % 2 * 4 + b, 0:SEQ], gates[:, b * KT + n, :], ALU.mult))
                    do(nc.vector.tensor_tensor(out, out, term[:, b % 2, :], ALU.add), m["merged_done"] if b == NB - 1 else None)
            dve.wait_ge(m["out_ready"], 1)
            for t in range(TT):
                for h in range(2):
                    at = slice(h * 512, (h + 1) * 512)
                    nc.vector.tensor_tensor(c.x[:, t, at], c.ps[:, 4 + 2 * t + h, :], c.x[:, t, at], ALU.add)


LATE = 15
NAT = 384
W2_WIDTHS = [4096] * 3 + [8 * 288] + [4096] * 4 + [8 * NAT] * 6


def scale_rows_phase(nc, c, gain_row):
    with ExitStack() as st:
        sq = on_chip(nc, c, st, "squares", [P, D])
        s = on_chip(nc, c, st, "stats", [P, 4, TT])
        row = on_chip(nc, c, st, "gain_row", [P, D])
        block, m = st.enter_context(phase(nc, "arrived", "squared", "mean_ready", "root_ready", "vstep"))

        @block.sync
        def _(sp):
            sp.dma_start(row[:], gain_row).then_inc(m["arrived"], 16)

        @block.scalar
        def _(act):
            for t in range(TT):
                if t:
                    act.wait_ge(m["squared"], t)
                nc.scalar.activation(sq[:], c.x[:, t, :], ACT.Square, accum_out=s[:, 0, t:t + 1]).then_inc(m["squared"], 1)
            act.wait_ge(m["mean_ready"], 1)
            nc.scalar.activation(s[:, 2, :], s[:, 1, :], ACT.Sqrt).then_inc(m["root_ready"], 1)

        @block.vector
        def _(dve):
            do = Chain(dve, m["vstep"])
            dve.wait_ge(m["squared"], TT)
            do(nc.vector.tensor_scalar(s[:, 1, :], s[:, 0, :], 1.0 / D, EPS, ALU.mult, ALU.add), m["mean_ready"])
            dve.wait_ge(m["root_ready"], 1)
            inverse_root(nc, do, s[:, 2, :], s[:, 1, :], s[:, 2, :], s[:, 3, :])
            dve.wait_ge(m["arrived"], 16)
            for t in range(TT):
                nc.vector.scalar_tensor_tensor(c.x[:, t, :], c.x[:, t, :], s[:, 2, t:t + 1], row[:], ALU.mult, ALU.mult)


def projection2_phase(nc, c, chunks):
    items = [4, 4, 4, 3, 4, 4, 4, 4] + [2] * 6
    VT = LATE
    with ExitStack() as st:
        block, m = st.enter_context(phase(nc, "item_ready", "v_evacuated", "a_evacuated", "padded", keep=c.loaded))

        @block.sync
        def _(sp):
            for i in range(MIX_RING, len(chunks)):
                sp.wait_ge(m["item_ready"], sum(items[:i - MIX_RING + 1]))
                sp.dma_start(c.ring[:, i % MIX_RING, 0:chunks[i].shape[1]], chunks[i]).then_inc(c.loaded[i % MIX_RING], 16)

        @block.tensor
        def _(pe):
            n = 0
            for i in range(8):
                pe.wait_ge(c.loaded[i % MIX_RING], i // MIX_RING * 16 + 16)
                width = W2_WIDTHS[i] // KT
                for u in range(items[i]):
                    if n >= VT + MIX_BANKS:
                        pe.wait_ge(m["a_evacuated"], n - MIX_BANKS - VT + 1)
                    elif n >= MIX_BANKS:
                        pe.wait_ge(m["v_evacuated"], n - MIX_BANKS + 1)
                    rows = min(P, width - u * P)
                    for k in range(KT):
                        w = k * width + u * P
                        last = nc.tensor.matmul(c.ps[0:rows, n % MIX_BANKS, 0:SEQ], c.ring[:, i % MIX_RING, w:w + rows],
                                                c.hT[:, k, :], start=(k == 0), stop=(k == KT - 1))
                    last.then_inc(m["item_ready"], 1)
                    n += 1
            with pe.Fori(0, 2) as a:
                for i in range(8, 11):
                    pe.wait_ge(c.loaded[i % MIX_RING], a * 16 + (i // MIX_RING * 16 + 16))
                    for t in range(TT):
                        e = n + (i - 8) * 2 + t
                        pe.wait_ge(m["a_evacuated"], a * 6 + (e - MIX_BANKS - VT + 1))
                        for k in range(KT):
                            last = nc.tensor.matmul(c.ps[:, e % MIX_BANKS, 0:NAT], c.hT[:, k, t * P:(t + 1) * P],
                                                    c.ring[:, i % MIX_RING, k * NAT:(k + 1) * NAT],
                                                    start=(k == 0), stop=(k == KT - 1))
                        last.then_inc(m["item_ready"], 1)

        @block.vector
        def _(dve):
            nc.vector.memset(c.rw[:], 0.0).then_inc(m["padded"], 1)
            dve.wait_ge(m["padded"], 1)
            for n in range(VT):
                dve.wait_ge(m["item_ready"], n + 1)
                rows = 32 if n == VT - 1 else P
                nc.vector.tensor_copy(c.rw[0:rows, n, 1:], c.ps[0:rows, n % MIX_BANKS, 0:SEQ]).then_inc(m["v_evacuated"], 1)

        @block.scalar
        def _(act):
            for g in range(16):
                n = VT + g
                act.wait_ge(m["item_ready"], n + 1)
                nc.scalar.activation(c.gT2[:, g, :], c.ps[:, n % MIX_BANKS, 0:SEQ], ACT.Sigmoid).then_inc(m["a_evacuated"], 1)
            with act.Fori(0, 2) as a:
                for e in range(6):
                    n = VT + 16 + e
                    act.wait_ge(m["item_ready"], a * 6 + (n + 1))
                    at = a * (3 * NAT) + (e // 2) * NAT
                    nc.scalar.activation(c.qkv[:, e % 2, bass.ds(at, NAT)], c.ps[:, n % MIX_BANKS, 0:NAT], ACT.Copy).then_inc(m["a_evacuated"], 1)


def qk_norm_phase(nc, c, a):
    NH = 24
    QK = 2 * GROUPS * GHEADS * HEAD
    with ExitStack() as st:
        sq = on_chip(nc, c, st, "squares", [P, QK])
        s = on_chip(nc, c, st, "stats", [P, 3, TT * NH])
        table = on_chip(nc, c, st, "bias_table", [N_BUCKETS + 1, 12])
        hot = on_chip(nc, c, st, "bucket_onehot", [N_BUCKETS + 1, GROUPS, 512])
        rows = on_chip(nc, c, st, "bias_rows", [GHEADS, GROUPS, 512])
        block, m = st.enter_context(phase(nc, "table_here", "ones_set", "rows_ready", "rows_copied", "rows_stored", "bias_here", "bias_ready", "bias_copied", "mean_ready", "root_ready",
                                          "scaled", "turned", "vstep"))

        @block.sync
        def _(sp):
            sp.wait_ge(m["ones_set"], 1)
            sp.dma_start(table[0:N_BUCKETS, :], a["bias_table"]).then_inc(m["table_here"], 16)
            sp.dma_start(hot[:], a["onehot"]).then_inc(m["table_here"], 16)
            sp.wait_ge(m["rows_copied"], 1)
            sp.dma_start(c.bias_rows.rearrange("(h g) i -> h g i", g=GROUPS), rows[:]).then_inc(m["rows_stored"], 16)
            sp.wait_ge(m["rows_stored"], 16)
            for t in range(TT):
                src = bass.AP(tensor=c.bias_rows.tensor, offset=c.bias_rows.offset + 255 - t * P - (P - 1),
                              ap=[[1, P], [512, 12], [1, (t + 1) * P]])
                dst = c.bias_reversed[:, t * 1536:t * 1536 + 12 * (t + 1) * P]
                sp.dma_start(dst.rearrange("p (h k) -> p h k", h=12), src).then_inc(m["bias_here"], 16)
            sp.wait_ge(m["bias_here"], 32)

        @block.tensor
        def _(pe):
            pe.wait_ge(m["table_here"], 32)
            for g in range(GROUPS):
                last = nc.tensor.matmul(c.ps[0:GHEADS, g, :], table[:, g * GHEADS:(g + 1) * GHEADS], hot[:, g, :], start=True, stop=True)
            last.then_inc(m["rows_ready"], 1)
            pe.wait_ge(m["rows_copied"], 1)
            pe.wait_ge(m["scaled"], TT)
            for i in range(12):
                for t in range(TT):
                    at = i * SEQ + t * P
                    last = nc.tensor.transpose(c.psflat[:, at:at + P], c.qkv[:, t, i * P:(i + 1) * P], c.ident[:])
            last.then_inc(m["turned"], 1)
            pe.wait_ge(m["bias_here"], 32)
            for i in range(9):
                if i >= 2:
                    pe.wait_ge(m["bias_copied"], i - 1)
                nc.tensor.matmul(c.ps[:, 6 + i % 2, :], c.exchange[:], c.bias_reversed[:, i * 512:(i + 1) * 512],
                                 start=True, stop=True).then_inc(m["bias_ready"], 1)

        @block.scalar
        def _(act):
            act.wait_ge(m["mean_ready"], 1)
            nc.scalar.activation(s[:, 1, :], s[:, 0, :], ACT.Sqrt).then_inc(m["root_ready"], 1)

        @block.vector
        def _(dve):
            do = Chain(dve, m["vstep"])
            do(nc.vector.memset(table[:], 1.0), m["ones_set"])
            for t in range(TT):
                qk = c.qkv[:, t, 0:QK]
                do(nc.vector.tensor_tensor(sq[:], qk, qk, ALU.mult))
                do(nc.vector.tensor_reduce(s[:, 0, t * NH:(t + 1) * NH], sq[:].rearrange("p (h e) -> p h e", e=HEAD), AX.X, ALU.add))
            do(nc.vector.tensor_scalar(s[:, 0, :], s[:, 0, :], 1.0 / HEAD, EPS, ALU.mult, ALU.add), m["mean_ready"])
            dve.wait_ge(m["rows_ready"], 1)
            do(nc.vector.tensor_copy(rows[:], c.ps[0:GHEADS, 0:GROUPS, :]), m["rows_copied"])
            dve.wait_ge(m["root_ready"], 1)
            inverse_root(nc, do, s[:, 1, :], s[:, 0, :], s[:, 1, :], s[:, 2, :])
            for t in range(TT):
                qk = c.qkv[:, t, 0:QK].rearrange("p (h e) -> p h e", e=HEAD)
                by = s[:, 1, t * NH:(t + 1) * NH].unsqueeze(2).to_broadcast([P, NH, HEAD])
                do(nc.vector.tensor_tensor(qk, qk, by, ALU.mult), m["scaled"])
            dve.wait_ge(m["turned"], 1)
            for i in range(12):
                src = c.psflat[:, i * SEQ:(i + 1) * SEQ]
                if i < 6:
                    nc.vector.tensor_scalar(c.qT2[:, i, :], src, c.par2[:, PAR2["qgain"]][:, i:i + 1], HEAD ** -0.5, ALU.mult, ALU.mult)
                else:
                    nc.vector.tensor_scalar(c.kT2[:, i - 6, :], src, c.par2[:, PAR2["kgain"]][:, i - 6:i - 5], None, ALU.mult)
            for i in range(9):
                dve.wait_ge(m["bias_ready"], i + 1)
                nc.vector.tensor_copy(c.bias_all[:, i * 512:(i + 1) * 512], c.ps[:, 6 + i % 2, :]).then_inc(m["bias_copied"], 1)


def dilated_units(c):
    units = []
    for t, heads in ((0, (0, 1, 2, 3)), (1, (0, 1)), (1, (2, 3))):
        K = (t + 1) * P
        L = GROUPS * K
        pitch = 512 if t == 0 else 1024
        scores, outs = [], []
        for n, h in enumerate(heads):
            half = slice(h % 2 * HEAD, h % 2 * HEAD + HEAD)
            terms = []
            for g in range(GROUPS):
                i = g * GHEADS + h
                scores.append((n * pitch + g * K, c.qT2[half, i // 2, t * P:(t + 1) * P], c.kT2[half, i // 2, 0:K]))
                terms += [(c.qkv[:, j, 1536 + i * HEAD:1536 + (i + 1) * HEAD], n * L // P + g * (t + 1) + j) for j in range(t + 1)]
            outs.append((half, n // 2 * P, terms))
        nt = len(heads) // 2
        bias = c.bias0[:, :, :] if t == 0 else c.bias1[:, heads[0]:heads[0] + 2, :]
        units.append(Unit(scores=scores, heads=len(heads), length=L, pitch=pitch, bias=bias, outs=outs,
                                     dst=c.oT2[:, heads[0] // 2:heads[0] // 2 + nt, t * P:(t + 1) * P],
                                     from_ps=c.psflat[:, 0:nt * P].rearrange("p (a q) -> p a q", a=nt)))
    return units


def rwkv_prepare_phase(nc, c, r, a):
    W = RT * SEQ
    with ExitStack() as st:
        block, m = st.enter_context(phase(nc, "weights_here", "mixed", "squashed", "loras_ready", "rates_done", "decay_done", "squares_done", "norms_ready",
                                          "floor_done", "root_done", "bonus_in", "bonus_ready", "natural_ready", "natural_in", "vstep", "astep"))
        p2 = c.par2

        def col(name, i):
            return p2[:, PAR2[name]][:, i:i + 1]

        def flat(t):
            return t.rearrange("p a s -> p (a s)")

        @block.sync
        def _(sp):
            sp.dma_start(r.lora[:], a["lora"]).then_inc(m["weights_here"], 16)
            sp.dma_start(r.gup[:], a["gup"]).then_inc(m["weights_here"], 16)
            sp.wait_ge(m["weights_here"], 32)

        @block.vector
        def _(dve):
            do = Chain(dve, m["vstep"])
            do(nc.vector.tensor_tensor(r.pm[:], c.rw[:, :, 0:SEQ], c.rw[:, :, 1:], ALU.subtract))
            for i in (12, 13, 14) + tuple(range(12)):
                ins = nc.vector.scalar_tensor_tensor(r.pm[:, i, :], r.pm[:, i, :], col("mu", i), c.rw[:, i, 1:], ALU.mult, ALU.add)
                do(ins, m["mixed"] if i >= 12 else None)
            rr, k, v = r.pm[:, 0:4, :], r.pm[:, 4:8, :], r.pm[:, 8:12, :]
            for i in range(RT):
                do(nc.vector.tensor_scalar(r.kk[:, i, :], k[:, i, :], col("k_k", i), None, ALU.mult))
            do(nc.vector.tensor_tensor(r.tmp[:], r.kk[:], r.kk[:], ALU.mult), m["squares_done"])
            dve.wait_ge(m["rates_done"], 1)
            for i in range(RT):
                do(nc.vector.tensor_scalar(r.k2[:, i, :], r.rate[:, i, :], -1.0, col("k_a", i), ALU.add, ALU.mult))
                do(nc.vector.scalar_tensor_tensor(r.k2[:, i, :], r.k2[:, i, :], 1.0, k[:, i, :], ALU.add, ALU.mult))
            do(nc.vector.tensor_copy(r.gate[:], c.psflat[:, 2048:2048 + W].rearrange("p (a s) -> p a s", a=RT)))
            dve.wait_ge(m["norms_ready"], 1)
            do(nc.vector.tensor_scalar(flat(r.tmp[:]), c.psflat[:, 3072:3072 + W], 1e-24, None, ALU.max), m["floor_done"])
            for i in range(RT):
                do(nc.vector.scalar_tensor_tensor(r.bonus[:, i, :], rr[:, i, :], col("r_k", i), r.k2[:, i, :], ALU.mult, ALU.mult),
                   m["bonus_in"] if i == RT - 1 else None)
            dve.wait_ge(m["root_done"], 1)
            do(nc.vector.reciprocal(r.tmp[:], r.tmp[:]))
            do(nc.vector.tensor_tensor(r.kk[:], r.kk[:], r.tmp[:], ALU.mult))
            dve.wait_ge(m["bonus_ready"], 1)
            do(nc.vector.tensor_tensor(flat(r.bonus[:]), c.psflat[:, 0:W], flat(v), ALU.mult))
            dve.wait_ge(m["decay_done"], 1)
            do(nc.vector.memset(r.tmp[:], 0.0))
            cum = r.cum[:].rearrange("p (a n) s -> p a n s", a=RT)
            do(nc.vector.memset(r.cum[:, :, 0:1], 1.0))
            for i in range(RT):
                for n in range(4):
                    do(nc.vector.tensor_tensor_scan(cum[:, i, n, 1:], r.decay[:, i, n * CHUNK:(n + 1) * CHUNK], r.tmp[:, 0, 0:CHUNK],
                                                    1.0, ALU.mult, ALU.add))
            before, upto = r.cum[:, :, 0:CHUNK], r.cum[:, :, 1:CHUNK + 1]

            def chunks(t):
                return t.rearrange("p a (n s) -> p (a n) s", s=CHUNK)

            do(nc.vector.tensor_copy(chunks(r.decay[:]), upto))
            do(nc.vector.reciprocal(r.tmp[:], r.decay[:]))
            do(nc.vector.scalar_tensor_tensor(chunks(r.aT[:]), chunks(r.kk[:]), -1.0, before, ALU.mult, ALU.mult))
            do(nc.vector.tensor_tensor(r.rT[:], rr, r.decay[:], ALU.mult))
            do(nc.vector.tensor_tensor(r.kk[:], r.kk[:], r.rate[:], ALU.mult))
            do(nc.vector.tensor_tensor(r.bT[:], r.kk[:], r.tmp[:], ALU.mult))
            do(nc.vector.tensor_tensor(r.kT[:], r.k2[:], r.tmp[:], ALU.mult), m["natural_in"])
            dve.wait_ge(m["natural_ready"], 1)
            for t in range(TT):
                at = c.psflat[:, t * 2048:(t + 1) * 2048].rearrange("p (x h e) -> p x h e", x=4, h=RHEADS)
                do(nc.vector.tensor_copy(r.Z[:, t, :, HEAD:], at[:, 0]))
                do(nc.vector.tensor_copy(r.nat[:, t, :, :], c.psflat[:, t * 2048 + 512:(t + 1) * 2048].rearrange("p (x e) -> p x e", x=3)))

        @block.scalar
        def _(act):
            act.wait_ge(m["mixed"], 3)
            do = Chain(act, m["astep"])
            do(nc.scalar.activation(r.pm[0:HEAD, 12, :], r.pm[0:HEAD, 12, :], ACT.Tanh))
            do(nc.scalar.activation(r.pm[:, 13:15, :], r.pm[:, 13:15, :], ACT.Sigmoid), m["squashed"])
            act.wait_ge(m["loras_ready"], 1)
            for i in range(RT):
                do(nc.scalar.activation(r.decay[:, i, :], c.psflat[:, i * SEQ:(i + 1) * SEQ], ACT.Sigmoid, bias=col("w0", i)))
            for i in range(RT):
                do(nc.scalar.activation(r.rate[:, i, :], c.psflat[:, 1024 + i * SEQ:1024 + (i + 1) * SEQ], ACT.Sigmoid, bias=col("a0", i)),
                   m["rates_done"] if i == RT - 1 else None)
            do(nc.scalar.activation(r.decay[:], r.decay[:], ACT.Exp, scale=-float(np.exp(-0.5))), m["decay_done"])
            act.wait_ge(m["floor_done"], 1)
            do(nc.scalar.activation(r.tmp[:], r.tmp[:], ACT.Sqrt), m["root_done"])

        @block.tensor
        def _(pe):
            pe.wait_ge(m["weights_here"], 32)
            pe.wait_ge(m["squashed"], 1)
            for i in range(RT):
                w = slice(i * P, (i + 1) * P)
                nc.tensor.matmul(c.psflat[:, i * SEQ:(i + 1) * SEQ], r.lora[0:HEAD, w], r.pm[0:HEAD, 12, :], start=True, stop=True)
                nc.tensor.matmul(c.psflat[:, 1024 + i * SEQ:1024 + (i + 1) * SEQ], r.lora[HEAD:P, w], r.pm[HEAD:P, 12, :], start=True, stop=True)
            for i in range(RT):
                for x in range(2):
                    last = nc.tensor.matmul(c.psflat[:, 2048 + i * SEQ:2048 + (i + 1) * SEQ], r.gup[:, x, i * P:(i + 1) * P], r.pm[:, 13 + x, :],
                                            start=(x == 0), stop=(x == 1))
            last.then_inc(m["loras_ready"], 1)
            pe.wait_ge(m["squares_done"], 1)
            for i in range(RT):
                last = nc.tensor.matmul(c.psflat[:, 3072 + i * SEQ:3072 + (i + 1) * SEQ], c.head_ones[:], r.tmp[:, i, :], start=True, stop=True)
            last.then_inc(m["norms_ready"], 1)
            pe.wait_ge(m["bonus_in"], 1)
            pe.wait_ge(m["decay_done"], 1)
            for i in range(RT):
                last = nc.tensor.matmul(c.psflat[:, i * SEQ:(i + 1) * SEQ], c.head_ones[:], r.bonus[:, i, :], start=True, stop=True)
            last.then_inc(m["bonus_ready"], 1)
            pe.wait_ge(m["natural_in"], 1)
            for t in range(TT):
                for x, src in enumerate((r.aT, r.bT, r.kT, r.pm[:, 8:12, :])):
                    for i in range(RT):
                        at = t * 2048 + x * 512 + i * P
                        last = nc.tensor.transpose(c.psflat[:, at:at + P], src[:, i, t * P:(t + 1) * P], c.ident[:])
            last.then_inc(m["natural_ready"], 1)


STRICT16, OFF_LOWER, LOWER16, STRICT64, UPTO64, = range(5)
WKV_GROUPS = [(t, half) for t in range(TT) for half in range(2)]


def wkv_phase(nc, c, r):
    J = 4

    def head(j, half):
        return 2 * j + half

    def chan(x):
        return lambda t, half, j: x[half * HEAD:(half + 1) * HEAD, j, t * P:(t + 1) * P]

    def mat(x):
        return lambda t, half, j: x[:, t * 2 + half, j, :]

    aT, bT, kT, rT = (chan(x) for x in (r.aT, r.bT, r.kT, r.rT))
    M = {n: mat(r.mats[n]) for n in r.mats}
    vn = lambda t, half, j: r.nat[:, t, 2, head(j, half) * HEAD:(head(j, half) + 1) * HEAD]
    z = lambda t, half, j: r.Z[:, t, head(j, half), :]
    MASK, COPY, ADD = "mask", "copy", "add"
    plan = [
        (bT, aT, [("p1t", MASK, STRICT16)]),
        (aT, bT, [("p1", MASK, LOWER16), ("lo", MASK, OFF_LOWER)]),
        (kT, aT, [("mt", MASK, STRICT64)]),
        (bT, rT, [("qb", MASK, UPTO64)]),
        (kT, rT, [("qk", MASK, UPTO64)]),
        (M["p1t"], M["p1"], [("p2", COPY, None)]),
        (M["p1"], M["p1t"], [("p2t", COPY, None)]),
        (M["p2"], M["d"], [("d", ADD, None)]),
        (M["p2t"], M["p2"], [("p1", COPY, None)]),
        (M["p2"], M["p2t"], [("p1t", COPY, None)]),
        (M["p1"], M["d"], [("d", ADD, None)]),
        (M["p1t"], M["p1"], [("p2", COPY, None)]),
        (M["p2"], M["d"], [("d", ADD, None)]),
        (M["d"], M["lo"], [("p1", COPY, None)]),
        (M["lo"], M["d"], [("p1t", COPY, None)]),
        (M["p1"], M["p1t"], [("p2t", COPY, None)]),
        (M["mt"], vn, [("Z", "left", None)]),
        (M["d"], z, [("Z", "z", None)]),
        (M["p2t"], z, [("Z", "zadd", None)]),
        (M["p1t"], z, [("Z", "zadd", None)]),
    ]
    with ExitStack() as st:
        block, m = st.enter_context(phase(nc, "product_ready", "product_used", "rest_ready", "rest_used", "state_ready", "state_used", "vstep"))

        def bank(n, g):
            return n % 2 * 4 + g

        @block.tensor
        def _(pe):
            for n, (left, right, _) in enumerate(plan):
                for g, (t, half) in enumerate(WKV_GROUPS):
                    if n:
                        pe.wait_ge(m["product_used"], (n - 1) * 4 + g + 1)
                    for j in range(J):
                        rhs = right(t, half, j)
                        last = nc.tensor.matmul(c.ps[:, bank(n, g), j * P:j * P + rhs.shape[1]], left(t, half, j), rhs, start=True, stop=True)
                    last.then_inc(m["product_ready"], 1)
            pe.wait_ge(m["product_used"], len(plan) * 4)
            for g, (t, half) in enumerate(WKV_GROUPS):
                part = slice(half * HEAD, (half + 1) * HEAD)
                for j in range(J):
                    h = head(j, half)
                    last = nc.tensor.matmul(c.ps[part, g, j * P:(j + 1) * P], r.Z[:, t, h, HEAD:], M["qb"](t, half, j), start=True, stop=True)
                last.then_inc(m["rest_ready"], 1)
            for g, (t, half) in enumerate(WKV_GROUPS):
                part = slice(half * HEAD, (half + 1) * HEAD)
                for j in range(J):
                    h = head(j, half)
                    nc.tensor.matmul(c.ps[part, 4 + g, j * P:(j + 1) * P], r.Z[:, t, h, 0:HEAD], M["qb"](t, half, j), start=True, stop=False)
                    last = nc.tensor.matmul(c.ps[part, 4 + g, j * P:(j + 1) * P], vn(t, half, j), M["qk"](t, half, j), start=False, stop=True)
                last.then_inc(m["rest_ready"], 1)
            for n in range(4):
                t, rows = n // 2, slice(n % 2 * HEAD, n % 2 * HEAD + HEAD)
                pe.wait_ge(m["rest_used"], n + 5)
                for half in range(2):
                    part = slice(half * HEAD, (half + 1) * HEAD)
                    for j in range(J):
                        h = head(j, half)
                        hs = slice(h * HEAD, (h + 1) * HEAD)
                        Bn, Kn, Vn = (r.nat[rows, t, x, hs] for x in range(3))
                        nc.tensor.matmul(c.ps[part, n, j * HEAD:(j + 1) * HEAD], r.Z[rows, t, h, HEAD:], Bn, start=True, stop=True)
                        nc.tensor.matmul(c.ps[part, n, 256 + j * HEAD:256 + (j + 1) * HEAD], Bn, r.Z[rows, t, h, 0:HEAD], start=True, stop=False)
                        last = nc.tensor.matmul(c.ps[part, n, 256 + j * HEAD:256 + (j + 1) * HEAD], Kn, Vn, start=False, stop=True)
                last.then_inc(m["rest_ready"], 1)
            pe.wait_ge(m["rest_used"], 12)
            for n in range(1, 4):
                pe.wait_ge(m["state_used"], n)
                for half in range(2):
                    part = slice(half * HEAD, (half + 1) * HEAD)
                    for j in range(J):
                        at = slice(j * HEAD, (j + 1) * HEAD)
                        last = nc.tensor.matmul(c.ps[part, half, at], r.state[part, j, :], r.rT[part, j, n * CHUNK:(n + 1) * CHUNK], start=True, stop=True)
                        if n < 3:
                            last = nc.tensor.matmul(c.ps[part, 2 + half, at], r.step[part, n, j, :], r.state[part, j, :], start=True, stop=True)
                last.then_inc(m["state_ready"], 1)

        @block.vector
        def _(dve):
            do = Chain(dve, m["vstep"])
            for n, (_, _, results) in enumerate(plan):
                for g, (t, half) in enumerate(WKV_GROUPS):
                    dve.wait_ge(m["product_ready"], n * 4 + g + 1)
                    ps = c.ps[:, bank(n, g), :].rearrange("p (j s) -> p j s", j=J)
                    for i, (name, how, arg) in enumerate(results):
                        done = m["product_used"] if i == len(results) - 1 else None
                        Zg = r.Z[:, t, :, :].rearrange("p (j x) e -> p x j e", x=2)[:, half]
                        if how in ("left", "z", "zadd"):
                            if how == "left":
                                do(nc.vector.tensor_copy(Zg[:, :, 0:HEAD], ps[:, :, 0:HEAD]), done)
                            elif how == "z":
                                do(nc.vector.tensor_copy(Zg, ps), done)
                            else:
                                do(nc.vector.tensor_tensor(Zg, ps, Zg, ALU.add), done)
                            continue
                        out = r.mats[name][:, g, :, :]
                        if how == MASK:
                            do(nc.vector.tensor_tensor(out, ps, c.masks[:, arg, :].unsqueeze(1).to_broadcast([P, J, P]), ALU.mult),
                               done if name != "p1t" else None)
                            if name == "p1t":
                                do(nc.vector.tensor_tensor(r.mats["d"][:, g, :, :], out, c.ident[:].unsqueeze(1).to_broadcast([P, J, P]), ALU.add), done)
                        elif how == COPY:
                            do(nc.vector.tensor_copy(out, ps), done)
                        else:
                            do(nc.vector.tensor_tensor(out, ps, out, ALU.add), done)
            for g, (t, half) in enumerate(WKV_GROUPS):
                part = slice(half * HEAD, (half + 1) * HEAD)
                dve.wait_ge(m["rest_ready"], g + 1)
                ps = c.ps[part, g, :].rearrange("p (j s) -> p j s", j=J)
                G = r.rT[part, :, t * P:(t + 1) * P]
                do(nc.vector.tensor_tensor(G, ps, G, ALU.add), m["rest_used"])
            for g, (t, half) in enumerate(WKV_GROUPS):
                part = slice(half * HEAD, (half + 1) * HEAD)
                dve.wait_ge(m["rest_ready"], 4 + g + 1)
                ps = c.ps[part, 4 + g, :].rearrange("p (j s) -> p j s", j=J)
                do(nc.vector.tensor_copy(r.out[part, :, t * P:(t + 1) * P], ps), m["rest_used"])
            for n in range(4):
                dve.wait_ge(m["rest_ready"], 8 + n + 1)
                ps = c.ps[:, n, 0:256].rearrange("p (j s) -> p j s", j=J)
                do(nc.vector.tensor_tensor(r.step[:, n, :, :], ps, c.ident2[:].unsqueeze(1).to_broadcast([P, J, HEAD]), ALU.add))
                ps = c.ps[:, n, 256:512].rearrange("p (j s) -> p j s", j=J)
                end = r.decay[:, :, (n + 1) * CHUNK - 1:(n + 1) * CHUNK].to_broadcast([P, J, HEAD])
                do(nc.vector.tensor_tensor(r.fresh[:, n, :, :], ps, end, ALU.mult), m["rest_used"])
            do(nc.vector.tensor_copy(r.state[:], r.fresh[:, 0, :, :]), m["state_used"])
            for n in range(1, 4):
                dve.wait_ge(m["state_ready"], n)
                for half in range(2):
                    part = slice(half * HEAD, (half + 1) * HEAD)
                    ps = c.ps[part, half, 0:256].rearrange("p (j s) -> p j s", j=J)
                    O = r.out[part, :, n * CHUNK:(n + 1) * CHUNK]
                    do(nc.vector.tensor_tensor(O, ps, O, ALU.add))
                    if n < 3:
                        ps = c.ps[part, 2 + half, 0:256].rearrange("p (j s) -> p j s", j=J)
                        end = r.decay[part, :, (n + 1) * CHUNK - 1:(n + 1) * CHUNK].to_broadcast([HEAD, J, HEAD])
                        do(nc.vector.tensor_tensor(r.state[part, :, :], ps, end, ALU.mult))
                        do(nc.vector.tensor_tensor(r.state[part, :, :], r.state[part, :, :], r.fresh[part, n, :, :], ALU.add),
                           m["state_used"] if half else None)


def rwkv_output_phase(nc, c, r, stream):
    W = RT * SEQ
    with ExitStack() as st:
        block, m = st.enter_context(phase(nc, "sums_ready", "squares_done", "var_ready", "mean_ready", "root_ready", "vstep"))

        def flat(t):
            return t.rearrange("p a s -> p (a s)")

        @block.sync
        def _(sp):
            prefetch(sp, c, stream)

        @block.tensor
        def _(pe):
            for src, at, before, ready in ((r.out, 0, None, m["sums_ready"]), (r.centred, 1024, m["squares_done"], m["var_ready"])):
                if before is not None:
                    pe.wait_ge(before, 1)
                for i in range(RT):
                    last = nc.tensor.matmul(c.psflat[:, at + i * SEQ:at + (i + 1) * SEQ], c.head_ones[:], src[:, i, :], start=True, stop=True)
                last.then_inc(ready, 1)

        @block.scalar
        def _(act):
            act.wait_ge(m["mean_ready"], 1)
            nc.scalar.activation(r.root[:], r.centred[:], ACT.Sqrt).then_inc(m["root_ready"], 1)

        @block.vector
        def _(dve):
            do = Chain(dve, m["vstep"])
            dve.wait_ge(m["sums_ready"], 1)
            do(nc.vector.scalar_tensor_tensor(flat(r.out[:]), c.psflat[:, 0:W], -1.0 / HEAD, flat(r.out[:]), ALU.mult, ALU.add))
            do(nc.vector.tensor_tensor(r.centred[:], r.out[:], r.out[:], ALU.mult), m["squares_done"])
            dve.wait_ge(m["var_ready"], 1)
            do(nc.vector.tensor_scalar(flat(r.centred[:]), c.psflat[:, 1024:1024 + W], 1.0 / HEAD, GN_EPS, ALU.mult, ALU.add), m["mean_ready"])
            dve.wait_ge(m["root_ready"], 1)
            inverse_root(nc, do, r.root[:], r.centred[:], r.root[:], r.scratch[:])
            do(nc.vector.tensor_tensor(r.out[:], r.out[:], r.root[:], ALU.mult))
            for i in range(RT):
                lw, lb = (c.par2[:, PAR2[x]][:, i:i + 1] for x in ("ln_w", "ln_b"))
                do(nc.vector.tensor_scalar(r.out[:, i, :], r.out[:, i, :], lw, lb, ALU.mult, ALU.add))
            do(nc.vector.tensor_tensor(r.out[:], r.out[:], r.bonus[:], ALU.add))
            do(nc.vector.tensor_tensor(r.out[:], r.out[:], r.gate[:], ALU.mult))


SLOTS = 64
PAIRS = N_EXP // 2
PAIR = 2 * SLOTS


def prefetch_experts(sp, c, stream, n):
    for s in range(NSLOT):
        sp.dma_start(c.ring[:, s, 0:DOWN], stream[s][:, 0:DOWN]).then_inc(c.loaded[s], 16)
    for s in range(NSLOT):
        sp.dma_start(c.ring[:, s, DOWN:], stream[s][:, DOWN:]).then_inc(c.down_loaded[s], 16)


def dispatch_phase(nc, c, a):
    with ExitStack() as st:
        before, ones, slots = (on_chip(nc, c, st, n, [P, w]) for n, w in (("before", P), ("ones", P), ("slot_numbers", SLOTS)))
        place = on_chip(nc, c, st, "place", [P, TT, N_EXP])
        gated = on_chip(nc, c, st, "gated_selection", [P, TT, N_EXP * SLOTS])
        most = on_chip(nc, c, st, "most", [P, 1])
        block, m = st.enter_context(phase(nc, "arrived", "places_ready", "gated_ready", "turned", "vstep"))

        @block.sync
        def _(sp):
            for dst, src in ((before, a["before"]), (ones, a["ones"]), (slots, a["slot_numbers"])):
                sp.dma_start(dst[:], src).then_inc(m["arrived"], 16)

        @block.tensor
        def _(pe):
            pe.wait_ge(m["arrived"], 48)
            nc.tensor.matmul(c.ps[:, 0, 0:N_EXP], before[:], c.assigned[:, 0, :], start=True, stop=True)
            nc.tensor.matmul(c.ps[:, 1, 0:N_EXP], ones[:], c.assigned[:, 0, :], start=True, stop=False)
            nc.tensor.matmul(c.ps[:, 1, 0:N_EXP], before[:], c.assigned[:, 1, :], start=False, stop=True)
            nc.tensor.matmul(c.ps[:, 2, 0:N_EXP], ones[:], c.assigned[:, 0, :], start=True, stop=False)
            nc.tensor.matmul(c.ps[:, 2, 0:N_EXP], ones[:], c.assigned[:, 1, :], start=False, stop=True).then_inc(m["places_ready"], 1)
            for t in range(TT):
                pe.wait_ge(m["gated_ready"], t + 1)
            for p in range(PAIRS):
                for t in range(TT):
                    at = p * SEQ + t * P
                    last = nc.tensor.transpose(c.psflat[:, at:at + P], gated[:, t, p * PAIR:(p + 1) * PAIR], c.ident[:])
            last.then_inc(m["turned"], 1)

        @block.scalar
        def _(act):
            act.wait_ge(m["turned"], 1)
            nc.scalar.activation(c.back[:, PAIRS // 2:, :], c.psflat[:, 2048:4096].rearrange("p (a s) -> p a s", s=SEQ), ACT.Copy)

        @block.vector
        def _(dve):
            do = Chain(dve, m["vstep"])
            tt = nc.vector.tensor_tensor
            dve.wait_ge(m["arrived"], 48)
            dve.wait_ge(m["places_ready"], 1)
            do(nc.vector.tensor_copy(place[:], c.ps[:, 0:TT, 0:N_EXP]))
            do(nc.vector.tensor_reduce(most[:], c.ps[:, 2, 0:N_EXP], AX.X, ALU.max))
            do(nc.vector.tensor_copy(c.most[:], most[:]))
            do(nc.vector.tensor_scalar(c.rest[:], place[:], float(SLOTS), None, ALU.is_ge))
            do(tt(c.rest[:], c.rest[:], c.gates[:], ALU.mult))
            for t in range(TT):
                shape = [P, N_EXP, SLOTS]
                sel = c.sel[:, t, :].rearrange("p (e s) -> p e s", s=SLOTS)
                do(tt(sel, slots[:].unsqueeze(1).to_broadcast(shape), place[:, t, :].unsqueeze(2).to_broadcast(shape), ALU.is_equal))
                do(tt(sel, sel, c.assigned[:, t, :].unsqueeze(2).to_broadcast(shape), ALU.mult))
                do(tt(gated[:, t, :].rearrange("p (e s) -> p e s", s=SLOTS), sel, c.gates[:, t, :].unsqueeze(2).to_broadcast(shape), ALU.mult), m["gated_ready"])
            dve.wait_ge(m["turned"], 1)
            nc.vector.tensor_copy(c.back[:, 0:PAIRS // 2, :], c.psflat[:, 0:2048].rearrange("p (a s) -> p a s", s=SEQ))


def sparse_experts_phase(nc, c, stream, gain):
    with ExitStack() as st:
        xg = on_chip(nc, c, st, "gathered", [P, 2, KT, PAIR])
        hid = on_chip(nc, c, st, "hidden", [P, 2, F_STEP])
        hidT = on_chip(nc, c, st, "hidden_turned", [P, 4, PAIR])
        gated = on_chip(nc, c, st, "silu_gate", [P, 2, F_STEP])
        y = on_chip(nc, c, st, "outputs", [P, D])
        back = on_chip(nc, c, st, "back_now", [P, SEQ])
        block, m = st.enter_context(phase(nc, "zeroed", "gathered", "xg_ready", "gu_ready", "silu_done", "hid_done", "down_used", "y_low", "y_high",
                                          "back_ready", "scattered", "turned", "turned_copied_0", "turned_copied_1", keep=c.loaded + c.down_loaded))

        @block.sync
        def _(sp):
            with sp.Fori(1, PAIRS) as p:
                for half in range(2):
                    sp.wait_ge(m["gu_ready"], p * 2 + (half - 1))
                    for s in (half, half + 2):
                        sp.dma_start(c.ring[:, s, 0:DOWN], stream[p * 4 + s][:, 0:DOWN]).then_inc(c.loaded[s], 16)
                for half in range(2):
                    sp.wait_ge(m["down_used"], p * 2 + (half - 1))
                    for s in (half, half + 2):
                        sp.dma_start(c.ring[:, s, DOWN:], stream[p * 4 + s][:, DOWN:]).then_inc(c.down_loaded[s], 16)

        @block.tensor
        def _(pe):
            def gather(p):
                for k in range(KT):
                    for t in range(TT):
                        at = 1024 + k * PAIR
                        last = nc.tensor.matmul(c.psflat[:, at:at + PAIR], c.xn[:, t, k * P:(k + 1) * P],
                                                c.sel[:, t, bass.ds(p * PAIR, PAIR)], start=(t == 0), stop=(t == 1))
                last.then_inc(m["gathered"], 1)

            def gate_up(p, parity, half):
                for s in (half, half + 2):
                    pe.wait_ge(c.loaded[s], p * 16 + 16)
                for k in range(KT):
                    for e in range(2):
                        w = c.ring[:, half + 2 * e, 0:DOWN].rearrange("p (a k n) -> p a k n", a=2, k=KT)[:, :, k, :]
                        out = c.ps[e * SLOTS:(e + 1) * SLOTS, half, :].rearrange("p (a n) -> p a n", a=2)
                        last = nc.tensor.matmul(out, xg[:, parity, k, e * SLOTS:(e + 1) * SLOTS], w, start=(k == 0), stop=(k == KT - 1))
                last.then_inc(m["gu_ready"], 1)

            def turn_hidden(p, half):
                pe.wait_ge(m["hid_done"], p * 2 + (half + 1))
                for f in range(2):
                    last = nc.tensor.transpose(c.ps[:, half, f * P:(f + 1) * P], hid[:, half, f * P:(f + 1) * P], c.ident[:])
                last.then_inc(m["turned"], 1)

            def scatter(p, final=False):
                pe.wait_ge(m["back_ready"], p + 1)
                for t in range(TT):
                    for n in range(2):
                        last = nc.tensor.matmul(c.ps[:, 4 + 2 * t + n, :], back[:, t * P:(t + 1) * P], y[:, n * 512:(n + 1) * 512],
                                                start=False, stop=final)
                last.then_inc(m["scattered"], 1)

            def outputs_copied(p):
                pe.wait_ge(m["y_low"], p + 1)
                pe.wait_ge(m["y_high"], p + 1)

            def down(p, half):
                pe.wait_ge(m[f"turned_copied_{half}"], p + 1)
                for s in (half, half + 2):
                    pe.wait_ge(c.down_loaded[s], p * 16 + 16)
                for f in range(2):
                    for n in range(2):
                        for e in range(2):
                            w = DOWN + f * D + n * 512
                            last = nc.tensor.matmul(c.ps[e * SLOTS:(e + 1) * SLOTS, 2 + n, :], hidT[:, half * 2 + f, e * SLOTS:(e + 1) * SLOTS],
                                                    c.ring[:, half + 2 * e, w:w + 512], start=(half == 0 and f == 0), stop=(half == 1 and f == 1))
                last.then_inc(m["down_used"], 1)

            def turn(p, parity, first=False, last=False):
                gate_up(p, parity, 0)
                if not last:
                    if not first:
                        outputs_copied(p - 1)
                    gather(p + 1)
                gate_up(p, parity, 1)
                turn_hidden(p, 0)
                if not first:
                    if last:
                        outputs_copied(p - 1)
                    scatter(p - 1)
                turn_hidden(p, 1)
                if not last:
                    pe.wait_ge(m["xg_ready"], p + 2)
                down(p, 0)
                down(p, 1)

            pe.wait_ge(m["zeroed"], 1)
            for b in range(4):
                nc.tensor.matmul(c.ps[:, 4 + b, :], c.ident[:], y[:, 0:512], start=True, stop=False)
            gather(0)
            pe.wait_ge(m["xg_ready"], 1)
            turn(0, 0, first=True)
            with pe.Fori(0, (PAIRS - 2) // 2) as h:
                for u in (1, 2):
                    turn(h * 2 + u, u % 2)
            turn(PAIRS - 1, 1, last=True)
            outputs_copied(PAIRS - 1)
            scatter(PAIRS - 1, final=True)

        @block.scalar
        def _(act):
            def body(p, first):
                for half in range(2):
                    act.wait_ge(m["gu_ready"], p * 2 + (half + 1))
                    nc.scalar.activation(gated[:, half, :], c.ps[:, half, 0:F_STEP], ACT.Silu).then_inc(m["silu_done"], 1)
                act.wait_ge(m["turned"], p * 2 + 1)
                nc.scalar.activation(hidT[:, 0:2, :], c.ps[:, 0, 0:2 * P].rearrange("p (f s) -> p f s", f=2), ACT.Copy).then_inc(m["turned_copied_0"], 1)
                if not first:
                    act.wait_ge(m["scattered"], p)
                nc.scalar.activation(back[:], c.back[:, bass.ds(p, 1), :].rearrange("p a s -> p (a s)"), ACT.Copy).then_inc(m["back_ready"], 1)
                act.wait_ge(m["down_used"], p * 2 + 2)
                nc.scalar.activation(y[:, 512:], c.ps[:, 3, :], ACT.Copy).then_inc(m["y_high"], 1)

            body(0, True)
            with act.Fori(1, PAIRS) as p:
                body(p, False)

        @block.vector
        def _(dve):
            def take_gathered(p, parity):
                dve.wait_ge(m["gathered"], p + 1)
                nc.vector.tensor_tensor(xg[:, parity], c.psflat[:, 1024:1024 + KT * PAIR].rearrange("p (k s) -> p k s", k=KT),
                                        gain.unsqueeze(2).to_broadcast([P, KT, PAIR]), ALU.mult).then_inc(m["xg_ready"], 1)

            def hidden_values(p, half):
                dve.wait_ge(m["silu_done"], p * 2 + (half + 1))
                nc.vector.tensor_tensor(hid[:, half, :], gated[:, half, :], c.ps[:, half, F_STEP:2 * F_STEP], ALU.mult).then_inc(m["hid_done"], 1)

            def turn(p, parity, last=False):
                hidden_values(p, 0)
                if not last:
                    take_gathered(p + 1, 1 - parity)
                hidden_values(p, 1)
                dve.wait_ge(m["turned"], p * 2 + 2)
                nc.vector.tensor_copy(hidT[:, 2:4, :], c.ps[:, 1, 0:2 * P].rearrange("p (f s) -> p f s", f=2)).then_inc(m["turned_copied_1"], 1)
                dve.wait_ge(m["down_used"], p * 2 + 2)
                nc.vector.tensor_copy(y[:, 0:512], c.ps[:, 2, :]).then_inc(m["y_low"], 1)

            nc.vector.memset(y[:], 0.0).then_inc(m["zeroed"], 1)
            take_gathered(0, 0)
            turn(0, 0)
            with dve.Fori(0, (PAIRS - 2) // 2) as h:
                for u in (1, 2):
                    turn(h * 2 + u, u % 2)
            turn(PAIRS - 1, 1, last=True)
            dve.wait_ge(m["scattered"], PAIRS)
            for t in range(TT):
                for n in range(2):
                    at = slice(n * 512, (n + 1) * 512)
                    nc.vector.tensor_tensor(c.x[:, t, at], c.ps[:, 4 + 2 * t + n, :], c.x[:, t, at], ALU.add)


def routing_phase(nc, c, a):
    BIG = 64.0
    with ExitStack() as st:
        w = on_chip(nc, c, st, "router", [P, KT, N_GRP + N_EXP])
        bias = on_chip(nc, c, st, "router_bias", [P, N_GRP + N_EXP])
        order = on_chip(nc, c, st, "ordinals", [P, N_PER])
        lg = on_chip(nc, c, st, "logits", [P, TT, N_GRP + N_EXP])
        g4 = on_chip(nc, c, st, "group_work", [P, 3, TT, N_GRP])
        e8 = on_chip(nc, c, st, "expert_work", [P, 6, TT, N_PER])
        wide = on_chip(nc, c, st, "wide_work", [P, TT, N_GRP, N_PER])
        one = on_chip(nc, c, st, "token_work", [P, 8, TT])
        block, m = st.enter_context(phase(nc, "arrived", "logits_ready", "shifted", "exp_done", "vstep"))

        @block.sync
        def _(sp):
            sp.dma_start(w[:], a["router"]).then_inc(m["arrived"], 16)
            sp.dma_start(bias[:], a["router_bias"]).then_inc(m["arrived"], 16)
            sp.dma_start(order[:], a["ordinals"]).then_inc(m["arrived"], 16)

        @block.tensor
        def _(pe):
            pe.wait_ge(m["arrived"], 48)
            for t in range(TT):
                for k in range(KT):
                    last = nc.tensor.matmul(c.ps[:, t, 0:N_GRP + N_EXP], c.hT[:, k, t * P:(t + 1) * P], w[:, k, :], start=(k == 0), stop=(k == KT - 1))
            last.then_inc(m["logits_ready"], 1)

        @block.scalar
        def _(act):
            act.wait_ge(m["shifted"], 1)
            nc.scalar.activation(g4[:, 1], g4[:, 1], ACT.Exp).then_inc(m["exp_done"], 1)
            act.wait_ge(m["shifted"], 2)
            nc.scalar.activation(e8[:, 1], e8[:, 1], ACT.Exp).then_inc(m["exp_done"], 1)

        @block.vector
        def _(dve):
            do = Chain(dve, m["vstep"])
            tt, V = nc.vector.tensor_tensor, nc.vector

            def spread(x, n):
                return x.unsqueeze(2).to_broadcast([P, TT, n])

            def first_top(out, x, top, n, work, least):
                do(V.tensor_reduce(top, x, AX.X, ALU.max))
                do(tt(work, x, spread(top, n), ALU.is_equal))
                do(V.scalar_tensor_tensor(work, work, -BIG, order[:, 0:n].unsqueeze(1).to_broadcast([P, TT, n]), ALU.mult, ALU.add))
                do(V.tensor_reduce(least, work, AX.X, ALU.min))
                do(tt(out, work, spread(least, n), ALU.is_equal))

            dve.wait_ge(m["logits_ready"], 1)
            do(tt(lg[:], c.ps[:, 0:TT, 0:N_GRP + N_EXP], bias[:].unsqueeze(1).to_broadcast([P, TT, N_GRP + N_EXP]), ALU.add))
            grp = lg[:, :, 0:N_GRP]
            first_top(g4[:, 0], grp, one[:, 0], N_GRP, g4[:, 2], one[:, 1])
            do(tt(g4[:, 1], grp, spread(one[:, 0], N_GRP), ALU.subtract), m["shifted"])
            ex = lg[:, :, N_GRP:].rearrange("p t (g e) -> p t g e", g=N_GRP)
            do(tt(wide[:], ex, g4[:, 0].unsqueeze(3).to_broadcast([P, TT, N_GRP, N_PER]), ALU.mult))
            do(V.tensor_reduce(e8[:, 0], wide[:].rearrange("p t g e -> p t e g"), AX.X, ALU.add))
            do(V.tensor_reduce(one[:, 2], e8[:, 0], AX.X, ALU.max))
            do(tt(e8[:, 1], e8[:, 0], spread(one[:, 2], N_PER), ALU.subtract), m["shifted"])
            dve.wait_ge(m["exp_done"], 1)
            do(V.tensor_reduce(one[:, 3], g4[:, 1], AX.X, ALU.add))
            do(V.reciprocal(one[:, 3], one[:, 3]))
            dve.wait_ge(m["exp_done"], 2)
            do(V.tensor_reduce(one[:, 4], e8[:, 1], AX.X, ALU.add))
            do(V.reciprocal(one[:, 4], one[:, 4]))
            do(tt(e8[:, 1], e8[:, 1], spread(one[:, 4], N_PER), ALU.mult))
            first_top(e8[:, 2], e8[:, 1], one[:, 5], N_PER, e8[:, 5], one[:, 1])
            do(V.scalar_tensor_tensor(e8[:, 4], e8[:, 2], -BIG, e8[:, 1], ALU.mult, ALU.add))
            first_top(e8[:, 3], e8[:, 4], one[:, 6], N_PER, e8[:, 5], one[:, 1])
            do(tt(one[:, 7], one[:, 5], one[:, 6], ALU.add))
            do(V.reciprocal(one[:, 7], one[:, 7]))
            do(tt(one[:, 7], one[:, 7], one[:, 3], ALU.mult))
            do(tt(e8[:, 2], e8[:, 2], e8[:, 3], ALU.add))
            for t in range(TT):
                do(tt(c.assigned[:, t, :].rearrange("p (g e) -> p g e", g=N_GRP), g4[:, 0, t].unsqueeze(2).to_broadcast([P, N_GRP, N_PER]),
                      e8[:, 2, t].unsqueeze(1).to_broadcast([P, N_GRP, N_PER]), ALU.mult))
            do(tt(e8[:, 2], e8[:, 2], e8[:, 1], ALU.mult))
            do(tt(e8[:, 2], e8[:, 2], spread(one[:, 7], N_PER), ALU.mult))
            for t in range(TT):
                do(tt(c.gates[:, t, :].rearrange("p (g e) -> p g e", g=N_GRP), g4[:, 0, t].unsqueeze(2).to_broadcast([P, N_GRP, N_PER]),
                      e8[:, 2, t].unsqueeze(1).to_broadcast([P, N_GRP, N_PER]), ALU.mult))


@contextmanager
def overflowing(eng, c):
    most = eng.value_load(c.most[0:1, 0:1], min_val=0, max_val=SEQ)
    with eng.If(most > SLOTS):
        yield


def experts_phase(nc, c, stream, gates):
    N = EXP_STEPS
    with ExitStack() as st:
        hid = on_chip(nc, c, st, "hidden", [P, NSLOT, 2, SEQ])
        gated = on_chip(nc, c, st, "silu_gate", [P, 2, 2, SEQ])
        block, m = st.enter_context(phase(nc, "up_ready", "silu_done", "hid_done", "down_used", "summed", keep=c.loaded))

        @block.sync
        def _(sp):
            def body(j, s, q):
                if not isinstance(j, int) or j >= NSLOT:
                    sp.wait_ge(m["down_used"], j - (NSLOT - 1))
                    sp.dma_start(c.ring[:, s, :], stream[j]).then_inc(c.loaded[s], 16)

            with overflowing(sp, c):
                prefetch(sp, c, stream)
                steps(sp, N, NSLOT, body)

        @block.tensor
        def _(pe):
            def down(j, s, q):
                pe.wait_ge(m["hid_done"], j * 2 + 2)
                expert = q * 2 + s // 2
                if s % 2 == 0 and not (isinstance(expert, int) and expert == 0):
                    pe.wait_ge(m["summed"], expert)
                for f in range(2):
                    for t in range(TT):
                        for n in range(2):
                            w = DOWN + f * D + n * 512
                            last = nc.tensor.matmul(c.ps[:, 4 + 2 * t + n, :], hid[:, s, f, t * P:(t + 1) * P],
                                                    c.ring[:, s, w:w + 512], start=(s % 2 == 0 and f == 0), stop=(s % 2 == 1 and f == 1))
                last.then_inc(m["down_used"], 1)

            def body(j, s, q):
                gate_up(nc, pe, c, m, j, s, q)
                if not isinstance(j, int) or j > 0:
                    down(j - 1, (s - 1) % NSLOT, q if s else q - 1)

            with overflowing(pe, c):
                steps(pe, N, 2, body)
                down(N - 1, (N - 1) % NSLOT, (N - 1) // NSLOT)

        @block.scalar
        def _(act):
            with overflowing(act, c):
                steps(act, N, 2, lambda j, s, q: silu_gate(nc, act, c, m, gated, j, s))

        @block.vector
        def _(dve):
            def add(j, s, q):
                dve.wait_ge(m["down_used"], j + 1)
                expert = q * 2 + s // 2
                for t in range(TT):
                    for n in range(2):
                        at = slice(n * 512, (n + 1) * 512)
                        g = gates[:, t, bass.ds(expert, 1)]
                        last = nc.vector.scalar_tensor_tensor(c.x[:, t, at], c.ps[:, 4 + 2 * t + n, :], g, c.x[:, t, at], ALU.mult, ALU.add)
                last.then_inc(m["summed"], 1)

            def body(j, s, q):
                hidden(nc, dve, c, m, hid, gated, j, s)
                if s % 2 == 0 and not (isinstance(j, int) and j == 0):
                    if not isinstance(j, int) or j >= 4:
                        dve.wait_ge(m["summed"], q * 2 + (s // 2 - 1))
                    add(j - 1, (s - 1) % NSLOT, q if s else q - 1)

            with overflowing(dve, c):
                steps(dve, N, NSLOT, body)
                dve.wait_ge(m["summed"], N_EXP - 1)
                add(N - 1, (N - 1) % NSLOT, (N - 1) // NSLOT)


def second_block(nc, c, a):
    with ExitStack() as st:
        def sb(stack, name, shape):
            return on_chip(nc, c, stack, name, shape)
        c.par2, c.head_ones, c.masks, c.ident2 = (sb(st, "params2", [P, N_PAR2]), sb(st, "head_ones", [P, P]), sb(st, "masks", [P, 5, P]),
                                                  sb(st, "half_identity", [P, HEAD]))
        c.exchange = sb(st, "exchange", [P, P])
        c.gates = sb(st, "expert_gates", [P, TT, N_EXP])
        c.memT = sb(st, "room", [P, KT, SEQ])
        load_phase(nc, c, (c.par2[:], a["par2"]), (c.head_ones[:], a["head_ones"]), (c.masks[:], a["masks"]), (c.ident2[:], a["ident2"]), (c.exchange[:], a["exchange"]))
        scale_rows_phase(nc, c, a["final_gain"])
        chunks = [a["rkv"][n] for n in range(3)] + [a["lora_in"]] + [a["gates2"][n] for n in range(4)] + [a["qkv"][n] for n in range(6)]
        norm_phase(nc, c, c.x, c.par2[:, PAR2["norm1"]], c.hT, a["rkv"], MIX_RING)
        with ExitStack() as mid:
            c.gT2, c.rw, c.oT2 = sb(mid, "branch_gates", [P, 16, SEQ]), sb(mid, "rwkv_in", [P, LATE, SEQ + 1]), sb(mid, "att_out", [P, 2, SEQ])
            with ExitStack() as inner:
                c.qkv, c.qT2, c.kT2 = sb(inner, "qkv", [P, TT, 2304]), sb(inner, "qT", [P, 6, SEQ]), sb(inner, "kT", [P, 6, SEQ])
                projection2_phase(nc, c, chunks)
                flat = c.ring[:, :, :].rearrange("p s n -> p (s n)")
                c.bias0 = flat[:, 0:1536].rearrange("p (h l) -> p h l", h=4)
                c.bias1 = flat[:, 1536:1536 + 3072].rearrange("p (h l) -> p h l", h=4)
                c.bias_all, c.bias_reversed = flat[:, 0:4608], flat[:, 4608:9216]
                c.bias_rows = nc.dram_tensor("bias_rows", (12, 512), F32).ap()
                qk_norm_phase(nc, c, a)
                attention_phase(nc, c, dilated_units(c), "dilated", *[t[:, :, :].rearrange("p k s -> p (k s)") for t in (c.hT, c.memT)])
            r = Tensors()
            r.at = 0
            flat = c.ring[:, :, :].rearrange("p s n -> p (s n)")

            def carve(*shape):
                n = int(np.prod(shape))
                assert r.at + n <= NSLOT * SLOT
                v = flat[:, r.at:r.at + n]
                r.at += n
                names = "abcd"[:len(shape)]
                spec = f"p ({' '.join(names)}) -> p {' '.join(names)}"
                return v.rearrange(spec, **dict(zip(names[1:], shape[1:])))

            r.pm, r.lora, r.gup = carve(LATE, SEQ), carve(1, RW)[:, 0], carve(2, RW)
            r.kk, r.k2, r.rate, r.tmp = (carve(RT, SEQ) for _ in range(4))
            r.cum = carve(RT * 4, CHUNK + 1)
            r.decay, r.bonus, r.gate, r.out = (sb(mid, n, [P, RT, SEQ]) for n in ("decay", "bonus", "rwkv_gate", "rwkv_out"))
            with ExitStack() as inner:
                r.kT, r.rT = (sb(inner, n, [P, RT, SEQ]) for n in ("kT", "rT"))
                r.nat = sb(inner, "natural", [P, TT, 3, RW])
                r.aT, r.bT = c.hT[:, 0:RT, :], c.hT[:, RT:KT, :]
                r.Z = c.memT[:, :, :].rearrange("p k s -> p (k s)").rearrange("p (t h e) -> p t h e", t=TT, h=RHEADS)
                rwkv_prepare_phase(nc, c, r, a)
                r.at = 0
                r.mats = {n: carve(4, 4, P) for n in ("p1", "p1t", "p2", "p2t", "lo", "mt", "qb", "qk", "d")}
                r.step, r.fresh, r.state = carve(4, 4, HEAD), carve(4, 4, HEAD), carve(4, HEAD)
                wkv_phase(nc, c, r)
            r.centred, r.root, r.scratch = (sb(mid, n, [P, RT, SEQ]) for n in ("centred", "root", "newton"))
            rwkv_output_phase(nc, c, r, a["merge2"])
            merge_phase(nc, c, [c.oT2, r.out], c.gT2, "second")
        c.assigned, c.rest = sb(st, "assigned", [P, TT, N_EXP]), sb(st, "rest_gates", [P, TT, N_EXP])
        c.most = st.enter_context(nc.sbuf_tensor("most_tokens", [P, 1], mybir.dt.int32))
        c.down_loaded = [st.enter_context(nc.semaphore(f"down_loaded_{i}")) for i in range(NSLOT)]
        gain = c.par2[:, PAR2["norm2"]]
        with ExitStack() as inner:
            c.xn = c.memT[:, :, :].rearrange("p k s -> p (k s)").rearrange("p (t d) -> p t d", t=TT)
            c.sel, c.back = sb(inner, "selection", [P, TT, N_EXP * SLOTS]), sb(inner, "way_back", [P, PAIRS, SEQ])
            norm_phase(nc, c, c.x, gain, c.hT, a["experts"], scaled=c.xn, load=prefetch_experts)
            routing_phase(nc, c, a)
            dispatch_phase(nc, c, a)
            sparse_experts_phase(nc, c, a["experts"], gain)
        experts_phase(nc, c, a["experts"], c.rest)


ORDER = [0, 2, 4, 6, 1, 3, 5, 7]
SLOPES = [2.0 ** (-8.0 * (h + 1) / NQ) for h in ORDER]


def load_phase(nc, c, *pairs):
    block_sems = ("arrived",)
    with phase(nc, *block_sems) as (block, m):
        @block.sync
        def _(sp):
            for dst, src in pairs:
                sp.dma_start(dst, src).then_inc(m["arrived"], 16)
            sp.wait_ge(m["arrived"], 16 * len(pairs))


def layer(nc, c, a, l):
    par = c.par
    load_phase(nc, c, (par[:], a["par"][l]))
    norm_phase(nc, c, c.x, par[:, PAR["ffn1"]], c.hT, a["ffn1"][l])
    ffn_phase(nc, c, a["ffn1"][l])
    with ExitStack() as st:
        c.memT = on_chip(nc, c, st, "memory_normed", [P, KT, SEQ])
        with ExitStack() as inner:
            memx = on_chip(nc, c, inner, "memory", [P, TT, D])
            load_phase(nc, c, (memx[:], a["mem"].rearrange("(t p) d -> p t d", p=P)))
            norm_phase(nc, c, memx, par[:, PAR["mem"]], c.memT)
        norm_phase(nc, c, c.x, par[:, PAR["mix"]], c.hT, a["w_in"][l], MIX_RING)
        def sb(name, shape):
            return on_chip(nc, c, st, name, shape)
        c.gT, c.yg, c.xr = sb("gates", [P, N_GATES * KT, SEQ]), sb("gelu_y", [P, KT, SEQ]), sb("conv_in", [P, KT, SEQ + CONV - 1])
        c.oT, c.omT = sb("window_out", [P, 4, SEQ]), sb("memory_out", [P, 4, SEQ])
        c.wa, c.wx = sb("gate_a_blocks", [P, KT, P]), sb("gate_x_blocks", [P, KT, P])
        c.gate_bias = par[:, PAR["gate_bias"]]
        with phase(nc, "zeroed", "blocks_arrived") as (block, m):
            @block.sync
            def _(sp):
                sp.wait_ge(m["zeroed"], 2)
                for w, src in ((c.wa, a["wa"][l]), (c.wx, a["wx"][l])):
                    for half in (slice(0, HEAD), slice(HEAD, P)):
                        sp.dma_start(w[half, :, half], src[half]).then_inc(m["blocks_arrived"], 16)
                sp.wait_ge(m["blocks_arrived"], 64)

            @block.vector
            def _(dve):
                nc.vector.memset(c.wa[:], 0.0).then_inc(m["zeroed"], 1)
                nc.vector.memset(c.wx[:], 0.0).then_inc(m["zeroed"], 1)
                nc.vector.memset(c.xr[:, :, 0:CONV - 1], 0.0)
        with ExitStack() as inner:
            def sb2(name, shape):
                return on_chip(nc, c, inner, name, shape)
            c.qT, c.cqT, c.kT, c.v = sb2("q", [P, 4, SEQ]), sb2("mem_q", [P, 4, SEQ]), sb2("k", [P, NKV, SEQ]), sb2("v", [P, TT, P])
            c.memK, c.memV = sb2("mem_k", [P, MEM_HEADS, SEQ]), sb2("mem_v", [P, TT, 512])
            mix_projection_phase(nc, c, par, a["w_in"][l], a["w_kv"][l], a["w_mem"][l])
            flat = [t[:, :, :].rearrange("p k s -> p (k s)") for t in (c.hT, c.memT)]
            attention_phase(nc, c, window_units(c), "window", *flat)
            attention_phase(nc, c, memory_units(c), "memory", *flat)
        lru_phase(nc, c, par, a["merge"][l])
        merge_phase(nc, c, [c.oT, c.omT, c.yg], c.gT, "mix")
    norm_phase(nc, c, c.x, par[:, PAR["ffn2"]], c.hT, a["ffn2"][l])
    ffn_phase(nc, c, a["ffn2"][l])


def program(nc, a, out, stop=None):
    c = Tensors()
    c.ids = count()
    with ExitStack() as st:
        def sb(name, shape):
            return on_chip(nc, c, st, name, shape)
        c.ps = st.enter_context(nc.psum_tensor("psum", [P, 8, 512], F32))
        c.psflat = c.ps[:, :, :].rearrange("p b n -> p (b n)")
        c.ring = sb("weight_ring", [P, NSLOT, SLOT])
        c.loaded = [st.enter_context(nc.semaphore(f"weights_loaded_{i}")) for i in range(NSLOT)]
        c.x, c.hT = sb("residual", [P, TT, D]), sb("normed", [P, KT, SEQ])
        c.ident = sb("identity", [P, P])
        with ExitStack() as first:
            def sb1(name, shape):
                return on_chip(nc, c, first, name, shape)
            c.par, c.distance = sb1("params", [P, N_PAR]), sb1("distances", [P, 3 * P])
            with phase(nc, "arrived") as (block, m):
                @block.sync
                def _(sp):
                    pairs = ((c.x[:], a["x"].rearrange("(t p) d -> p t d", p=P)), (c.ident[:], a["ident"]),
                             (c.distance[:], a["distance"]))
                    for dst, src in pairs:
                        sp.dma_start(dst, src).then_inc(m["arrived"], 16)
                    sp.wait_ge(m["arrived"], 16 * len(pairs))
            with nc.Fori(0, DEPTH) as l:
                layer(nc, c, a, l)
        if stop == 1:
            store_phase(nc, c, out)
            return
        second_block(nc, c, a)
        store_phase(nc, c, out)


def store_phase(nc, c, out):
    with phase(nc, "stored") as (block, m):
        @block.sync
        def _(sp):
            sp.dma_start(out.rearrange("(t p) d -> p t d", p=P), c.x[:]).then_inc(m["stored"], 16)
            sp.wait_ge(m["stored"], 16)


def layout(i):
    f = np.float32
    def rows(w, n):
        L, K, N = w.shape
        return w.reshape(L, K // P, P, N // n, n).transpose(0, 3, 2, 1, 4).reshape(L, N // n, P, K // P * n)

    def down(w, n=2):
        L, K, N = w.shape
        return w.reshape(L, K // (n * P), n, P, N).transpose(0, 1, 3, 2, 4).reshape(L, K // (n * P), P, n * N)

    def cols(v):
        return v.reshape(v.shape[0], -1, P).transpose(0, 2, 1)

    a = {}
    a["x"], a["mem"] = i["x"][0], i["mem"][0]
    a["ident"] = np.eye(P, dtype=f)
    q, k = np.arange(SEQ)[:, None], np.arange(SEQ)[None, :]
    seen = (k // CHUNK <= q // CHUNK) & (k // CHUNK >= q // CHUNK - 2)
    dist = np.where(seen, -np.abs(q - k), NEG).astype(f)
    a["distance"] = np.concatenate([dist[:P, :P], dist[P:, :]], 1)
    for n in (1, 2):
        a[f"ffn{n}"] = np.concatenate([rows(i[f"ffn{n}_w_gate"], F_STEP), rows(i[f"ffn{n}_w_up"], F_STEP), down(i[f"ffn{n}_w_down"])], 3)
    w = i["w_in"]
    o = np.cumsum([0, 512, 128, 128, 1024, 1024, 512, 3072])
    part = [w[:, :, o[n]:o[n + 1]] for n in range(7)]
    def order(g):
        return [g[..., n * D:(n + 1) * D] for n in (0, 2, 1)]

    a["w_in"] = rows(np.concatenate([part[0], part[5], part[3], part[4], *order(part[6])], 2), 512)
    a["w_kv"] = rows(np.concatenate([part[1], part[2]], 2), 256)[:, 0]
    a["w_mem"] = rows(i["w_mem_kv"], 512)
    a["merge"] = np.concatenate([rows(i["w_attn_out"], F_STEP), rows(i["w_mem_out"], F_STEP), rows(i["w_lru_out"], F_STEP),
                                 down(i["w_out"])], 3)
    L = DEPTH
    gb = np.concatenate(order(i["gate_bias"]), 1)
    small = [cols(i["ffn1_norm"]), cols(i["mix_norm"]), cols(i["mem_norm"]), cols(i["ffn2_norm"]), cols(gb),
             i["conv_w"].reshape(L, CONV, KT, P).transpose(0, 3, 2, 1).reshape(L, P, CONV * KT),
             cols(i["conv_b"]), cols(i["lru_ba"]), cols(i["lru_bx"]), cols(i["lru_lambda"]),
             np.repeat(i["attn_sinks"][:, None, ORDER], P, 1)]
    a["par"] = np.concatenate(small, 2)
    for n in ("wa", "wx"):
        a[n] = i[f"lru_{n}"].reshape(L, KT, 2, HEAD, HEAD).transpose(0, 2, 3, 1, 4).reshape(L, P, KT, HEAD)
    w = i["w_in_2"][0]
    n1, n2 = 2304, 2304 + 3 * RW
    qkv, rkv, lora, gates = w[:, :n1], w[:, n1:n2], w[:, n2:n2 + 288], w[:, n2 + 288:]
    a["qkv"], a["rkv"], a["gates2"] = rows(qkv[None], NAT)[0], rows(rkv[None], 512)[0], rows(gates[None], 512)[0]
    a["lora_in"] = rows(lora[None], 288)[0, 0]
    mu = np.concatenate([i["rwkv_shift_mu_2"], np.zeros((1, LATE * P - 1824), f)], 1)

    def heads_gain(g):
        return np.concatenate([g[0, n // 2][[*range(HEAD), *range(HEAD)], None] for n in range(6)], 1)

    a["par2"] = np.concatenate([cols(i["norm1_gain_2"])[0], cols(i["norm2_gain_2"])[0], heads_gain(i["q_norm_gain_2"]), heads_gain(i["k_norm_gain_2"]),
                                cols(mu)[0]] + [cols(i[f"rwkv_{n}_2"].reshape(1, RW))[0] for n in ("w0", "a0", "k_k", "k_a", "r_k", "ln_w", "ln_b")], 1)
    a["final_gain"] = np.repeat(i["final_norm"][None], P, 0)
    a["lora"] = np.concatenate([i["rwkv_w_up_2"][0], i["rwkv_a_up_2"][0]], 0)
    gup = np.concatenate([i["rwkv_g_up_2"][0], np.zeros((2 * P - 160, RW), f)], 0)
    a["gup"] = gup.reshape(2, P, RW).transpose(1, 0, 2)
    same = (np.arange(P)[:, None] // HEAD == np.arange(P)[None, :] // HEAD)
    a["head_ones"] = same.astype(f)
    a["before"], a["ones"] = (np.arange(P)[:, None] < np.arange(P)[None, :]).astype(f), np.ones((P, P), f)
    a["slot_numbers"] = np.repeat(np.arange(SLOTS, dtype=f)[None], P, 0)
    a["exchange"] = np.eye(P, dtype=f)[::-1]
    a["ident2"] = np.tile(np.eye(HEAD, dtype=f), (2, 1))
    s, t = np.arange(P)[:, None], np.arange(P)[None, :]
    same16 = s // 16 == t // 16
    a["masks"] = np.stack([same16 & (s < t), same & ~same16 & (s > t), same16 & (s > t), same & (s < t), same & (s <= t)], 1).astype(f)
    d = 255 - np.arange(512)
    df = np.maximum(d, 1).astype(f)
    large = 16 + (np.log(df / f(16)) / f(np.log(2048 / 16)) * f(16)).astype(np.int32)
    bucket = np.where(d < 16, d, np.minimum(large, N_BUCKETS - 1))
    hot = np.zeros((N_BUCKETS + 1, GROUPS, 512), f)
    for g, dil in enumerate(DIL):
        seen = (d >= 0) & (d % dil == 0) & (d <= P * dil)
        hot[:N_BUCKETS, g] = seen & (bucket[None] == np.arange(N_BUCKETS)[:, None])
        hot[N_BUCKETS, g] = np.where(seen, 0, NEG)
    a["onehot"], a["bias_table"] = hot, i["rel_bias_table_2"]
    a["merge2"] = np.concatenate([rows(i["w_att_out_2"], F_STEP), rows(i["w_rwkv_out_2"], F_STEP), down(i["w_out_2"])], 3)[0]
    a["router"] = np.concatenate([i["w_group_router_2"][0], i["w_expert_router_2"][0]], 1).reshape(KT, P, -1).transpose(1, 0, 2)
    a["router_bias"] = np.repeat(np.concatenate([i["b_group_router_2"], i["b_expert_router_2"]], 1), P, 0)
    a["ordinals"] = np.repeat(np.arange(N_PER, dtype=f)[None], P, 0)
    a["experts"] = np.concatenate([rows(i["w_expert_gate_2"][0], F_STEP), rows(i["w_expert_up_2"][0], F_STEP), down(i["w_expert_down_2"][0])],
                                  3).reshape(EXP_STEPS, P, SLOT)
    return {n: np.ascontiguousarray(v) for n, v in a.items()}


def kernel(**inputs):
    import concourse.bacc as _bacc
    from concourse.bass_utils import run_bass_kernel_spmd as _run

    nc = _bacc.Bacc("TRN2", target_bir_lowering=False, num_devices=1)
    arrays, args = {}, {}
    for name, a in layout({n: np.asarray(v) for n, v in inputs.items()}).items():
        arrays[f"in_{name}_dram"] = a
        args[name] = nc.dram_tensor(f"in_{name}_dram", a.shape, mybir.dt.from_np(a.dtype), kind="ExternalInput").ap()
    out = nc.dram_tensor("out_0_dram", (SEQ, D), F32, kind="ExternalOutput").ap()
    program(nc, args, out)
    r = _run(nc, [arrays], core_ids=[0])
    return r.results[0]["out_0_dram"].reshape(1, SEQ, D)
```
